# Optimizing a Trainium2 kernel written in Bass

```python
import jax, jax.numpy as jnp
from jax import lax
import numpy as np

D_MODEL = 1024
BATCH = 1
SEQ = 512
DEPTH = 2
DEC_BATCH = 8
DEC_SEQ = 8
PAST_LEN = 4096
PAGE_SIZE = 128

D_PLE = 256
D_FF = 2816
D_HALF = D_MODEL // 2
H_A = 4
DK_A = D_HALF // H_A
DV_A = D_HALF // H_A
H_B = 4
DK_B = D_HALF // 2 // H_B
DV_B = D_HALF // H_B
GLA_RANK = 16
GLA_GATE_NORM = 16.0
H_C = 4
DK_C = D_MODEL // H_C
DV_C = 2 * D_MODEL // H_C
ROPE_THETA = 10000.0
CHUNK = 64
EPS = 1e-6
N_AB_LAYERS = (DEPTH + 1) // 2
N_RET_LAYERS = DEPTH // 2
AB_SIZES = (H_A * DK_A, H_A * DK_A, H_A * DV_A, H_A * DV_A,
            H_B * DK_B, H_B * DK_B, H_B * DV_B, GLA_RANK, H_B * DV_B)
RET_SIZES = (H_C * DK_C, H_C * DK_C, H_C * DV_C, H_C * DV_C)

kernel_name = "hgrn2_gla_retnet_macaron_step"

F32 = jnp.float32

def split_cols(x, sizes):
    return jnp.split(x, [int(v) for v in np.cumsum(sizes)[:-1]], axis=-1)

def rmsnorm(x, g):
    xf = x.astype(F32)
    y = xf * lax.rsqrt(jnp.mean(xf * xf, axis=-1, keepdims=True) + EPS)
    return (y * g.astype(F32)).astype(x.dtype)

def headnorm(x, g):
    xf = x.astype(F32)
    mu = jnp.mean(xf, axis=-1, keepdims=True)
    xc = xf - mu
    y = xc * lax.rsqrt(jnp.mean(xc * xc, axis=-1, keepdims=True) + EPS)
    return (y * g.astype(F32)).astype(x.dtype)

def swiglu(x, w_in, w_out):
    a, b = jnp.split(x @ w_in, 2, axis=-1)
    return (jax.nn.silu(a) * b) @ w_out

def heads(x, h):
    b, l, _ = x.shape
    return x.reshape(b, l, h, -1).transpose(0, 2, 1, 3)

def merge(x):
    b, h, l, d = x.shape
    return x.transpose(0, 2, 1, 3).reshape(b, l, h * d)

def rope(x, pos):
    half = x.shape[-1] // 2
    inv = ROPE_THETA ** (-jnp.arange(half, dtype=F32) / half)
    ang = pos.astype(F32)[:, None] * inv[None, :]
    cos, sin = jnp.cos(ang), jnp.sin(ang)
    x1 = x[..., :half].astype(F32)
    x2 = x[..., half:].astype(F32)
    return jnp.concatenate([x1 * cos - x2 * sin, x2 * cos + x1 * sin], axis=-1).astype(x.dtype)

def chunk_gated_linear_attention(q, k, v, log_g, s0):
    bsz, h, L, _ = q.shape
    dv = v.shape[-1]
    c = min(CHUNK, L)
    n = -(-L // c)
    pad = n * c - L
    scalar = log_g.shape[-1] == 1

    def prep(t):
        t = jnp.pad(t.astype(F32), ((0, 0), (0, 0), (0, pad), (0, 0)))
        return t.reshape(bsz, h, n, c, t.shape[-1]).transpose(2, 0, 1, 3, 4)

    qs, ks, vs, gs = prep(q), prep(k), prep(v), prep(log_g)
    causal = jnp.tril(jnp.ones((c, c), dtype=bool))

    def step(S, inp):
        qc, kc, vc, gc = inp
        b = jnp.cumsum(gc, axis=-2)
        rel = jnp.exp(jnp.where(causal[:, :, None],
                                b[..., :, None, :] - b[..., None, :, :], -jnp.inf))
        if scalar:
            att = jnp.einsum('bhtk,bhsk->bhts', qc, kc) * rel[..., 0]
        else:
            att = jnp.einsum('bhtk,bhtsk,bhsk->bhts', qc, rel, kc)
        o = (jnp.einsum('bhts,bhsv->bhtv', att, vc)
             + jnp.einsum('bhtk,bhkv->bhtv', qc * jnp.exp(b), S))
        b_last = b[..., -1:, :]
        S = (jnp.exp(b_last)[..., 0, :, None] * S
             + jnp.einsum('bhsk,bhsv->bhkv', kc * jnp.exp(b_last - b), vc))
        return S, o

    S, o = lax.scan(step, s0.astype(F32), (qs, ks, vs, gs))
    o = o.transpose(1, 2, 0, 3, 4).reshape(bsz, h, n * c, dv)[:, :, :L]
    return o.astype(q.dtype), S.astype(s0.dtype)

def mixer_hgrn2_gla(x, s_hgrn, s_gla, lb, w_in, w_gk2, b_gk, gn_a, gn_b, w_out):
    qa, fa, ia, ga, qb, kb, vb, lrb, gb = split_cols(x @ w_in, AB_SIZES)
    fz = fa.astype(F32)
    log_f = jnp.log(lb + (1.0 - lb) * jax.nn.sigmoid(fz))
    ka = (1.0 - lb) * jax.nn.sigmoid(-fz)
    oa, s_hgrn = chunk_gated_linear_attention(heads(jax.nn.silu(qa), H_A), heads(ka, H_A),
                                              heads(ia, H_A), heads(log_f, H_A), s_hgrn)
    oa = merge(rmsnorm(oa, gn_a)) * jax.nn.silu(ga)
    log_a = jax.nn.log_sigmoid((lrb @ w_gk2 + b_gk).astype(F32)) / GLA_GATE_NORM
    ob, s_gla = chunk_gated_linear_attention(heads(qb * (DK_B ** -0.5), H_B), heads(kb, H_B),
                                             heads(vb, H_B), heads(log_a, H_B), s_gla)
    ob = merge(rmsnorm(ob, gn_b)) * jax.nn.silu(gb)
    return jnp.concatenate([oa, ob], axis=-1) @ w_out, s_hgrn, s_gla

def mixer_retention(x, pos, s_ret, w_in, gn, w_out):
    q, k, v, g = split_cols(x @ w_in, RET_SIZES)
    bsz, L, _ = x.shape
    qh = rope(heads(q, H_C), pos)
    kh = rope(heads(k, H_C), pos) * (DK_C ** -0.5)
    log_gamma = jnp.log1p(-jnp.exp2(-5.0 - jnp.arange(H_C, dtype=F32)))
    log_g = jnp.broadcast_to(log_gamma[None, :, None, None], (bsz, H_C, L, 1))
    o, s_ret = chunk_gated_linear_attention(qh, kh, heads(v, H_C), log_g, s_ret)
    o = merge(headnorm(o, gn)) * jax.nn.silu(g)
    return o @ w_out, s_ret

def decoder_trunk(x, p, pos, s_hgrn, s_gla, s_ret,
                  norm_ffn1, ffn1_w_in, ffn1_w_out, norm_mix,
                  ab_w_in, ab_w_gk2, ab_b_gk, hgrn_lb_logits, ab_gn_hgrn, ab_gn_gla, ab_w_out,
                  ret_w_in, ret_gn, ret_w_out,
                  norm_ffn2, ffn2_w_in, ffn2_w_out, norm_ple, ple_w_gate, ple_w_proj, norm_final):
    lb_all = jnp.cumsum(jax.nn.softmax(hgrn_lb_logits.astype(F32), axis=0), axis=0)
    new_hgrn, new_gla, new_ret = [], [], []
    for i in range(DEPTH):
        j = i // 2
        x = x + 0.5 * swiglu(rmsnorm(x, norm_ffn1[i]), ffn1_w_in[i], ffn1_w_out[i])
        h = rmsnorm(x, norm_mix[i])
        if i % 2 == 0:
            m, sa, sb = mixer_hgrn2_gla(h, s_hgrn[j], s_gla[j], lb_all[j], ab_w_in[j], ab_w_gk2[j],
                                        ab_b_gk[j], ab_gn_hgrn[j], ab_gn_gla[j], ab_w_out[j])
            new_hgrn.append(sa)
            new_gla.append(sb)
        else:
            m, sc = mixer_retention(h, pos, s_ret[j], ret_w_in[j], ret_gn[j], ret_w_out[j])
            new_ret.append(sc)
        x = x + m
        x = x + 0.5 * swiglu(rmsnorm(x, norm_ffn2[i]), ffn2_w_in[i], ffn2_w_out[i])
        gate = jax.nn.sigmoid(rmsnorm(x, norm_ple[i]) @ ple_w_gate[i])
        x = x + gate * (p[i] @ ple_w_proj[i])
    return rmsnorm(x, norm_final), jnp.stack(new_hgrn), jnp.stack(new_gla), jnp.stack(new_ret)

def setup_inputs(seed: int = 0) -> dict:
    key = jax.random.key(seed)
    ks = iter(jax.random.split(key, 40))

    def nrm(shape, scale):
        return jax.random.normal(next(ks), shape, F32) * scale

    def gain(shape):
        return 1.0 + nrm(shape, 0.02)

    d_ab_in = sum(AB_SIZES)
    d_ret_in = sum(RET_SIZES)
    return {
        "x_prompt": nrm((BATCH, SEQ, D_MODEL), 1.0),
        "x_sample": nrm((DEC_BATCH, DEC_SEQ, D_MODEL), 1.0),
        "state_hgrn": nrm((N_AB_LAYERS, DEC_BATCH, H_A, DK_A, DV_A), 0.5),
        "state_gla": nrm((N_AB_LAYERS, DEC_BATCH, H_B, DK_B, DV_B), 0.5),
        "state_ret": nrm((N_RET_LAYERS, DEC_BATCH, H_C, DK_C, DV_C), 0.5),
        "p_prompt": nrm((DEPTH, BATCH, SEQ, D_PLE), 1.0),
        "p_sample": nrm((DEPTH, DEC_BATCH, DEC_SEQ, D_PLE), 1.0),
        "norm_ffn1": gain((DEPTH, D_MODEL)),
        "ffn1_w_in": nrm((DEPTH, D_MODEL, 2 * D_FF), D_MODEL ** -0.5),
        "ffn1_w_out": nrm((DEPTH, D_FF, D_MODEL), D_FF ** -0.5),
        "norm_mix": gain((DEPTH, D_MODEL)),
        "ab_w_in": nrm((N_AB_LAYERS, D_MODEL, d_ab_in), D_MODEL ** -0.5),
        "ab_w_gk2": nrm((N_AB_LAYERS, GLA_RANK, H_B * DK_B), GLA_RANK ** -0.5),
        "ab_b_gk": nrm((N_AB_LAYERS, H_B * DK_B), 0.1),
        "hgrn_lb_logits": nrm((N_AB_LAYERS + 1, H_A * DK_A), 0.5),
        "ab_gn_hgrn": gain((N_AB_LAYERS, DV_A)),
        "ab_gn_gla": gain((N_AB_LAYERS, DV_B)),
        "ab_w_out": nrm((N_AB_LAYERS, H_A * DV_A + H_B * DV_B, D_MODEL), D_MODEL ** -0.5),
        "ret_w_in": nrm((N_RET_LAYERS, D_MODEL, d_ret_in), D_MODEL ** -0.5),
        "ret_gn": gain((N_RET_LAYERS, DV_C)),
        "ret_w_out": nrm((N_RET_LAYERS, H_C * DV_C, D_MODEL), (H_C * DV_C) ** -0.5),
        "norm_ffn2": gain((DEPTH, D_MODEL)),
        "ffn2_w_in": nrm((DEPTH, D_MODEL, 2 * D_FF), D_MODEL ** -0.5),
        "ffn2_w_out": nrm((DEPTH, D_FF, D_MODEL), D_FF ** -0.5),
        "norm_ple": gain((DEPTH, D_MODEL)),
        "ple_w_gate": nrm((DEPTH, D_MODEL, D_MODEL), D_MODEL ** -0.5),
        "ple_w_proj": nrm((DEPTH, D_PLE, D_MODEL), D_PLE ** -0.5),
        "norm_final": gain((D_MODEL,)),
    }

def reference(x_prompt, x_sample, state_hgrn, state_gla, state_ret, p_prompt, p_sample,
              norm_ffn1, ffn1_w_in, ffn1_w_out, norm_mix,
              ab_w_in, ab_w_gk2, ab_b_gk, hgrn_lb_logits, ab_gn_hgrn, ab_gn_gla, ab_w_out,
              ret_w_in, ret_gn, ret_w_out,
              norm_ffn2, ffn2_w_in, ffn2_w_out, norm_ple, ple_w_gate, ple_w_proj, norm_final):
    bp = x_prompt.shape[0]
    zero_hgrn = jnp.zeros((N_AB_LAYERS, bp, H_A, DK_A, DV_A), x_prompt.dtype)
    zero_gla = jnp.zeros((N_AB_LAYERS, bp, H_B, DK_B, DV_B), x_prompt.dtype)
    zero_ret = jnp.zeros((N_RET_LAYERS, bp, H_C, DK_C, DV_C), x_prompt.dtype)
    pos_prompt = jnp.arange(x_prompt.shape[1], dtype=jnp.int32)
    pos_sample = PAST_LEN + jnp.arange(x_sample.shape[1], dtype=jnp.int32)

    y_prompt, hgrn_p, gla_p, ret_p = decoder_trunk(
        x_prompt, p_prompt, pos_prompt, zero_hgrn, zero_gla, zero_ret,
        norm_ffn1, ffn1_w_in, ffn1_w_out, norm_mix,
        ab_w_in, ab_w_gk2, ab_b_gk, hgrn_lb_logits, ab_gn_hgrn, ab_gn_gla, ab_w_out,
        ret_w_in, ret_gn, ret_w_out,
        norm_ffn2, ffn2_w_in, ffn2_w_out, norm_ple, ple_w_gate, ple_w_proj, norm_final)
    y_sample, hgrn_s, gla_s, ret_s = decoder_trunk(
        x_sample, p_sample, pos_sample, state_hgrn, state_gla, state_ret,
        norm_ffn1, ffn1_w_in, ffn1_w_out, norm_mix,
        ab_w_in, ab_w_gk2, ab_b_gk, hgrn_lb_logits, ab_gn_hgrn, ab_gn_gla, ab_w_out,
        ret_w_in, ret_gn, ret_w_out,
        norm_ffn2, ffn2_w_in, ffn2_w_out, norm_ple, ple_w_gate, ple_w_proj, norm_final)
    return (y_prompt, y_sample, hgrn_p, gla_p, ret_p, hgrn_s, gla_s, ret_s)


_drawn_inputs = setup_inputs


def setup_inputs(seed=0):
    import zlib

    import numpy as np

    out = dict(_drawn_inputs(seed))
    spreads = {}
    factors = {'norm_ffn1': 3.616,
     'ab_gn_hgrn': 20.274,
     'ab_gn_gla': 20.114,
     'ret_gn': 61.032,
     'norm_ffn2': 5.853,
     'norm_ple': 64.0,
     'norm_final': 9.657}
    for name, (base, spread) in spreads.items():
        noise = np.random.default_rng([zlib.crc32(name.encode()), seed]).standard_normal(out[name].shape)
        drawn = base * np.exp(spread * noise) if base else spread * noise
        out[name] = __import__('jax').numpy.asarray(drawn.astype(out[name].dtype))
    for name, factor in factors.items():
        out[name] = (out[name] * factor).astype(out[name].dtype)
    return out
```

```python
import numpy as np
import concourse.bass as bass
import concourse.mybir as mybir

F32 = mybir.dt.float32
F32R = mybir.dt.float32r
I32 = mybir.dt.int32
ALU = mybir.AluOpType
ACT = mybir.ActivationFunctionType

P = 128
D = 1024
NB = D // P
TP, TS = 512, 64
T = TP + TS
TH = T // 2
NBAT, LS = 8, 8
DFF = 2816
FF_PARTS = (8, 8, 6)
H = 4
CH = TP // P
NRAW = 4
NLEV = 7
EPS = 1e-6
PAST = 4096
CT = TP + TS + TS + CH + 1 + 1
NORMS = ("norm_ffn1", "norm_mix", "norm_ffn2", "norm_ple")

N_FFN = sum(2 * j + NB for j in FF_PARTS)
N_HGRN, N_GLA, N_RET = 4, 6, 16
N_PIECES = 4 * N_FFN + H * N_HGRN + 1 + 2 * N_GLA + NB + H * N_RET + 2 * (NB + 2)


def early(eng, n):
    return n if isinstance(n, int) else eng.to_reg(n)


class Lin:

    def __init__(self, c, k=0, i=None):
        self.c, self.k, self.i = c, (k if i is not None else 0), i

    def __add__(self, n):
        return Lin(self.c + n, self.k, self.i)

    def div(self, d):
        assert self.k % d == 0
        return Lin(self.c // d, self.k // d, self.i)

    def mod(self, d):
        assert self.k % d == 0
        return self.c % d

    def value(self):
        return self.c if not self.k else self.i * self.k + self.c


FROM_ONE = ("taken0", "taken1", "o_done", "oss", "orms", "ot", "omixl", "kl", "turned_out", "gated", "silu",
            "hid_low", "rkv", "rmix", "rnew", "ratt", "rturned_out")


def count(name, n):
    n = n if isinstance(n, Lin) else Lin(n)
    assert n.c >= 0 and (not n.k or n.c > 0 or name in FROM_ONE), name
    return (n + 1 if name in FROM_ONE else n).value()


def two(ap):
    return ap.rearrange("p (a b) -> p a b", a=2)


def build(nc, d, out):
    at = [16512]

    def sb(name, cols, dt=F32, where=None):
        n = int(np.prod(cols)) * 4
        if where is None:
            where = at[0]
            at[0] = (where + n + 31) // 32 * 32
        return nc.alloc_sbuf_tensor_at(name, [P] + list(cols), dt, offset=where)

    x = sb("x", [NB, T])
    xh = sb("xh", [NB, T], F32R)
    xl = sb("xl", [NB, T], F32R)
    raw = sb("raw", [NRAW, D])
    wh = sb("wh", [2, D], F32R)
    wl = sb("wl", [2, D], F32R)
    rinv = sb("rinv", [T])
    rms = sb("rms", [T])
    sq = sb("sq", [2, T])
    sqsum = sb("sqsum", [T])
    gains = sb("gains", [9, NB])
    ident = sb("ident", [P])
    ones = sb("ones", [P])
    small = sb("small", [64])
    gnormA = small[:, 0:1]
    gnormB = small[:, 1:2]
    gnormR = small[:, 2:6]
    bgk = small[:, 6:8]
    logits = small[:, 8:16]
    batch_of = small[:, 16:24]
    lbmax, lbe, lbs = small[:, 24:28], small[:, 28:36], small[:, 36:40]
    bounds = sb("bounds", [2, H, 1])
    lb, one_lb = bounds[:, 0, :, 0], bounds[:, 1, :, 0]
    eps = small[:, 48:49]
    spare = at[0] + 4 * T * 4
    hid = [sb("hid_high", [8, T], F32R), sb("hid_low", [8, T], F32R)]
    free = at[0]

    fa = sb("ff_a", [2, T])
    fs = sb("ff_silu", [2, T])
    fb = sb("ff_b", [2, T])
    ff = sb("ff_gated", [2, T])
    at[0] = free
    praw = sb("praw", [2, T])
    ph = sb("ph", [2, T], F32R)
    pl = sb("pl", [2, T], F32R)
    pz = sb("pz", [2, T])
    pg = sb("pgate", [NB, T])
    pt = sb("ptmp", [2, T])
    at[0] = free
    z1 = sb("z1", [T])
    s1 = sb("s1", [T])
    s2 = sb("s2", [T])
    gk = sb("gk", [T])
    gU = sb("gU", [T])
    gL = sb("gL", [T])
    gq = sb("gq", [T])
    qu = sb("qu", [2, T])
    kl = sb("kl", [2, T])
    gate = sb("gate", [2, T])
    vf = sb("vf", [T])
    go = sb("go", [T])
    decay = sb("decay", [2, T])
    vt = sb("vt", [2, CH + 1, P])
    att = sb("att", [2, T])
    klt = sb("klt", [CH + 1, P])
    St = sb("St", [CH, P])
    S0 = sb("S0", [NBAT, P])
    Sn = sb("Sn", [NBAT, P])
    vm = sb("vm", [2, NBAT, P])
    masks = sb("masks", [NLEV, P], I32)
    lr = go
    gk2 = sq[0:16, 0, 0:2 * P]
    at[0] = free
    rz = sb("rz", [2, T])
    rtd = sb("rtd", [T])
    rtp = sb("rtp", [T])
    kdm = sb("kdm", [NBAT, 2 * P], where=free)
    rq = sb("rq", [2, T])
    rk = sb("rk", [2, T])
    rv = sb("rv", [2, T])
    rvt = sb("rvt", [CH + 1, 4 * P])
    kd = sb("kd", [CH + 1, 2 * P])
    ratt = sb("ratt", [1280])
    ratts = sb("ratts", [TS])
    qd = sb("qd", [2, TS])
    rS0 = sb("rS0", [4, 2, 4 * P])
    rSt = sb("rSt", [2, 4 * P])
    ctab = sb("ctab", [CT])
    cosT = sb("cosT", [T])
    sinT = sb("sinT", [T])
    ro = sb("ro", [4, T], where=spare)
    rg = sb("rg", [4, T], where=spare + 8 * T * 4)
    Dm = ctab[:, 0:TP]
    Ds = ctab[0:TS, TP:TP + TS]
    qdec = ctab[:, TP + TS:TP + 2 * TS]
    kdec = ctab[:, TP + 2 * TS:TP + 2 * TS + CH]
    kdecs = ctab[0:TS, TP + 2 * TS + CH:TP + 2 * TS + CH + 1]
    gam = ctab[:, TP + 2 * TS + CH + 1:CT]
    rr = rq[:, 0, :]
    RAT = [0, 512, 896, 1152]

    ps = nc.alloc_psum_tensor("ps", [P, 8, 512], F32)

    sems = {}

    def S(name):
        if name not in sems:
            sems[name] = nc.alloc_semaphore(name)
        return sems[name]

    for name in FROM_ONE:
        nc.sync.sem_inc(S(name), 1)
    block_cm = nc.Block()
    block = block_cm.__enter__()

    phases, n, u, g, norm, ffj, ffu = [], 0, 0, 0, 0, 0, 0
    for layer in range(2):
        for kind in ("ffn", "ab" if layer == 0 else "ret", "ffn", "ple"):
            phases.append(dict(kind=kind, layer=layer, n=n, u=u, norm=norm, j=ffj))
            if kind == "ffn":
                n, u, ffj = n + N_FFN, u + N_FFN, ffj + sum(FF_PARTS)
            elif kind == "ab":
                m = H * N_HGRN + 1 + 2 * N_GLA + NB
                n, u = n + m, u + m
            elif kind == "ret":
                n, u = n + H * N_RET, u + H * (12 + NB)
            else:
                n, u = n + NB + 2, u + 2 * NB
            norm += 1
    assert n == N_PIECES

    def per_group(name, ns):
        return {"sig": 4 if ns == 1 else 2, "scores": 8 * ns, "picked": 8 * ns, "qu": 8, "kl": 7, "u_up": 7,
                "l_up": 8, "turned": 2 * ns + 4, "turned_out": 2 * ns + 4, "s_step": 3, "S0_in": 16, "S_out": 32,
                "s_new": 1}.get(name, ns)

    def ready_k(eng, ns, u, i):
        if ns == 1:
            eng.wait_ge(S("k_ready"), count("k_ready", Lin(1, 1, i)))
        else:
            eng.wait_ge(S(f"taken{u.mod(2)}"), count(f"taken{u.mod(2)}", u.div(2) + 1))

    def ready_q(eng, ns, u, i):
        if ns == 1:
            eng.wait_ge(S("q_ready"), count("q_ready", Lin(1, 1, i)))
        else:
            eng.wait_ge(S(f"taken{(u + 1).mod(2)}"), count(f"taken{(u + 1).mod(2)}", (u + 1).div(2) + 1))

    def group_count(name, ns, i, pair, k):
        if ns == 1:
            return Lin(k, per_group(name, 1), i)
        assert name not in ("k_ready", "q_ready")
        return Lin(H * per_group(name, 1) + pair * per_group(name, 2) + k)

    @block.sync
    def _(sp):
        for m in range(NB):
            sp.dma_start(x[:, m, :], d["xT"][m]).then_inc(S("x_in"), 16)
            if m == 0:
                sp.dma_start(gains[:, :, :], d["gains"]).then_inc(S("const_in"), 16)
                sp.dma_start(small[:, 0:24], d["small"][:, 0:24]).then_inc(S("const_in"), 16)
                sp.dma_start(ident[:, :], d["ident"]).then_inc(S("const_in"), 16)
                sp.dma_start(raw[:, 0, :], d["w"][0]).then_inc(S("landed0"), 16)
            if m in (1, 2, 3):
                sp.dma_start(raw[:, m, :], d["w"][m]).then_inc(S(f"landed{m}"), 16)

        def piece(k, i):
            n = Lin(NRAW + k, NRAW, i)
            sp.wait_ge(S("lo_made"), count("lo_made", n + (1 - NRAW)))
            sp.dma_start(raw[:, k % NRAW, :], d["w"][n.value()]).then_inc(S(f"landed{k % NRAW}"), 16)

        rounds = (N_PIECES - NRAW) // NRAW
        with sp.Fori(0, rounds) as i:
            for k in range(NRAW):
                piece(k, i)
        for k in range(rounds * NRAW, N_PIECES - NRAW):
            piece(k, None)
        for m in range(NB):
            sp.wait_ge(S("y_ready"), count("y_ready", m + 1))
            sp.dma_start(out["yT"][m], x[:, m, :]).then_inc(S("y_out"), 16)
        sp.wait_ge(S("y_out"), count("y_out", 16 * NB))

    @block.tensor
    def _(pe):
        def product(bank_pair, w0, rhs, K, first_piece_col=0):
            last = None
            for k in range(K):
                w = slice((w0 + k) * P, (w0 + k + 1) * P)
                for j, (wt, r) in enumerate(((wh, 0), (wh, 1), (wl, 0))):
                    for a in range(2):
                        last = nc.tensor.matmul(
                            ps[:, 2 * bank_pair + a, 0:TH], lhsT=wt[:, first_piece_col, w],
                            rhs=rhs(r, k)[:, a * TH:(a + 1) * TH],
                            start=(k == 0 and j == 0), stop=(k == K - 1 and j == 2))
            return last

        def unit(n, u, rhs, K, w0=0, before=None):
            pe.wait_ge(S("lo_made"), count("lo_made", n + 1))
            s = u.mod(2)
            pe.wait_ge(S(f"taken{s}"), count(f"taken{s}", u.div(2)))
            slot = n.mod(2)
            if before is None:
                product(s, w0, rhs, K, slot).then_inc(S("unit"), 1)
                return
            last = None
            for k in range(K):
                before(k)
                w = slice((w0 + k) * P, (w0 + k + 1) * P)
                for j, (wt, r) in enumerate(((wh, 0), (wh, 1), (wl, 0))):
                    for a in range(2):
                        last = nc.tensor.matmul(
                            ps[:, 2 * s + a, 0:TH], lhsT=wt[:, slot, w],
                            rhs=rhs(r, k)[:, a * TH:(a + 1) * TH],
                            start=(k == 0 and j == 0), stop=(k == K - 1 and j == 2))
            last.then_inc(S("unit"), 1)

        def xin(r, k):
            return (xh, xl)[r][:, k, :]

        def hin(r, k):
            return hid[r][:, k, :]

        def norm_sum(norm):
            pe.wait_ge(S("sqsum"), count("sqsum", 7 * (norm + 1)))
            for a in range(2):
                last = nc.tensor.matmul(ps[:, 4 + a, 0:TH], lhsT=ones[:, :], rhs=sqsum[:, a * TH:(a + 1) * TH],
                                        start=True, stop=True)
            last.then_inc(S("norm_sum"), 1)

        def gated_group(ns, n, u, i, pair):
            G = lambda name, k: group_count(name, ns, i, pair, k)
            rows = [slice(0, P)] if ns == 1 else [slice(0, 64), slice(64, P)]

            def scores(lev):
                if lev == 0:
                    ready_k(pe, ns, u, i)
                    ready_q(pe, ns, u, i)
                    ka, qa = gk[:, :], gq[:, :]
                else:
                    pe.wait_ge(S("qu"), count("qu", G("qu", lev)))
                    ka, qa = gk[:, :], qu[:, lev % 2, :]
                    if lev > 1:
                        pe.wait_ge(S("kl"), count("kl", G("kl", lev - 1)))
                        ka = kl[:, lev % 2, :]
                for s in range(ns):
                    j = lev * ns + s
                    bank = 4 + j % 2
                    if j >= 2:
                        pe.wait_ge(S("picked"), count("picked", G("picked", j - 1)))
                    else:
                        pe.wait_ge(S("orms"), count("orms", G("orms", 0)))
                    for c in range(CH):
                        t = slice(c * P, (c + 1) * P)
                        last = nc.tensor.matmul(ps[:, bank, t], lhsT=ka[rows[s], t], rhs=qa[rows[s], t],
                                                start=True, stop=True)
                    if lev <= 3:
                        t = slice(TP, T)
                        o = 256 * s + 64 * lev
                        if j:
                            pe.wait_ge(S("picked"), count("picked", G("picked", j)))
                        last = nc.tensor.matmul(ps[0:TS, 6, o:o + TS], lhsT=ka[rows[s], t], rhs=qa[rows[s], t],
                                                start=True, stop=True)
                    last.then_inc(S("scores"), 1)

            turn = [0]

            def free_turn():
                reached = early(pe, count("turned_out", G("turned_out", turn[0])))
                pe.wait_ge(S("ones"), 1)
                pe.wait_ge(S("turned_out"), reached)
                turn[0] += 1

            def turn_tiles(src, prompt):
                free_turn()
                if prompt:
                    for c in range(CH):
                        last = nc.tensor.transpose(ps[:, 7, c * P:(c + 1) * P], src[:, c * P:(c + 1) * P], ident[:, :])
                else:
                    last = nc.tensor.transpose(ps[0:TS, 7, 0:P], src[:, TP:T], ident[:, :])
                last.then_inc(S("turned"), 1)

            def turn_v(s, uv):
                pe.wait_ge(S(f"taken{uv.mod(2)}"), count(f"taken{uv.mod(2)}", uv.div(2) + 1))
                turn_tiles(vf, True)
                turn_tiles(vf, False)

            npc = 0

            def proj(k, before=None):
                unit(n + k, u + k, xin, NB, before=before)

            proj(0)
            proj(1)
            proj(2)
            scores(0)
            turn_v(0, u + 2)
            scores(1)
            if ns == 2:
                proj(3)
                turn_v(1, u + 3)
                proj(4)
                proj(5)
            else:
                proj(3)
            for lev in range(2, NLEV + 1):
                scores(lev)
            pe.wait_ge(S("kl"), count("kl", G("kl", 7)))
            turn_tiles(kl[:, 0, :], True)
            turn_tiles(kl[:, 0, :], False)
            free_turn()
            for s in range(ns):
                for c in range(CH):
                    last = nc.tensor.matmul(ps[rows[s], 7, c * P:(c + 1) * P], lhsT=klt[:, c, rows[s]],
                                            rhs=vt[:, s, c, :], start=True, stop=True)
            last.then_inc(S("turned"), 1)
            free_turn()
            pe.wait_ge(S("picked"), count("picked", G("picked", 8 * ns)))
            for s in range(ns):
                pe.wait_ge(S("vm"), count("vm", G("vm", s + 1)))
                for a in range(2):
                    last = nc.tensor.matmul(ps[rows[s], 6 + a, :], lhsT=klt[0:TS, CH, rows[s]],
                                            rhs=vm[0:TS, s, 4 * a:4 * a + 4, :], start=True, stop=True)
            last.then_inc(S("turned"), 1)
            pe.wait_ge(S("qu"), count("qu", G("qu", 8)))
            pe.wait_ge(S("S0_in"), count("S0_in", G("S0_in", 16)))
            for s in range(ns):
                if s:
                    pe.wait_ge(S("orms"), count("orms", G("orms", s)))
                for c in range(CH):
                    t = slice(c * P, (c + 1) * P)
                    last = nc.tensor.matmul(ps[:, 4, t], lhsT=vt[:, s, c, :], rhs=att[:, s, t],
                                            start=True, stop=(c == 0))
                    if c:
                        last = nc.tensor.matmul(ps[:, 4, t], lhsT=St[rows[s], c - 1, :], rhs=qu[rows[s], 0, t],
                                                start=False, stop=True)
                last = nc.tensor.matmul(ps[:, 5, 0:TS], lhsT=vt[0:TS, s, CH, :], rhs=att[0:TS, s, TP:T],
                                        start=True, stop=True, skip_group_check=True)
                if s:
                    last.then_inc(S("own_tokens"), 1)
                    pe.wait_ge(S("own_tokens"), count("own_tokens", pair + 1))
                for b in range(NBAT):
                    t = slice(LS * b, LS * b + LS)
                    last = nc.tensor.matmul(ps[:, 5, t], lhsT=S0[rows[s], b, :],
                                            rhs=qu[rows[s], 0, TP + LS * b:TP + LS * b + LS],
                                            start=False, stop=True, skip_group_check=True)
                last.then_inc(S("o_done"), 1)
                pe.wait_ge(S("osq"), count("osq", G("osq", s + 1)))
                for a in range(2):
                    last = nc.tensor.matmul(ps[:, 4 + a, 0:TH], lhsT=ones[:, :],
                                            rhs=s1[:, a * TH:(a + 1) * TH], start=True, stop=True)
                last.then_inc(S("oss"), 1)

        def retention_head(n, u, i):
            R = lambda k, per: Lin(k, per, i)
            for k in range(4):
                unit(n + k, u + k, xin, NB)
            unit(n + 4, u + 4, xin, NB)

            def turn_v(vb):
                pe.wait_ge(S(f"taken{(u + 4 + vb).mod(2)}"), count(f"taken{(u + 4 + vb).mod(2)}", (u + 4 + vb).div(2) + 1))
                pe.wait_ge(S("rturned_out"), count("rturned_out", R(vb, 6)))
                for c in range(CH):
                    nc.tensor.transpose(ps[:, 7, c * P:(c + 1) * P], rv[:, vb % 2, c * P:(c + 1) * P], ident[:, :])
                nc.tensor.transpose(ps[0:TS, 6, 0:P], rv[:, vb % 2, TP:T], ident[:, :]).then_inc(S("rturned"), 1)

            def turn_k(kk):
                pe.wait_ge(S("rturned_out"), count("rturned_out", R(4 + kk, 6)))
                for c in range(CH):
                    nc.tensor.transpose(ps[:, 7, c * P:(c + 1) * P], rk[:, kk, c * P:(c + 1) * P], ident[:, :])
                nc.tensor.transpose(ps[0:TS, 6, 0:P], rk[:, kk, TP:T], ident[:, :]).then_inc(S("rturned"), 1)

            def scores(j):
                if j >= 2 and j < 4:
                    pe.wait_ge(S("ratt"), count("ratt", R(j - 1, 5)))
                if j == 0:
                    pe.wait_ge(S("rot_k0"), count("rot_k0", R(1, 1)))
                    pe.wait_ge(S("rot_k1"), count("rot_k1", R(1, 1)))
                if j == 4:
                    pe.wait_ge(S("rturned_out"), count("rturned_out", R(6, 6)))
                for kk in range(2):
                    if j < 4:
                        last = nc.tensor.matmul(ps[:, 4 + j % 2, 0:TP - P * j], lhsT=rk[:, kk, P * j:P * j + P],
                                                rhs=rq[:, kk, P * j:TP], start=(kk == 0), stop=(kk == 1))
                    else:
                        last = nc.tensor.matmul(ps[0:TS, 6, 0:TS], lhsT=rk[:, kk, TP:T], rhs=rq[:, kk, TP:T],
                                                start=(kk == 0), stop=(kk == 1))
                last.then_inc(S("rscores"), 1)

            for vb in range(1, 4):
                unit(n + 4 + vb, u + 4 + vb, xin, NB)
                turn_v(vb - 1)
            unit(n + 8, u + 8, xin, NB)
            turn_v(3)
            pe.wait_ge(S("rot_k0"), count("rot_k0", R(1, 1)))
            pe.wait_ge(S("rot_k1"), count("rot_k1", R(1, 1)))
            turn_k(0)
            turn_k(1)
            scores(0)
            for gb in range(1, 4):
                unit(n + 8 + gb, u + 8 + gb, xin, NB)
                scores(gb)
            scores(4)
            pe.wait_ge(S("ratt"), count("ratt", R(5, 5)))
            for vb in range(4):
                if vb >= 2:
                    pe.wait_ge(S("ro_out"), count("ro_out", R(vb - 1, 5)))
                for j in range(CH):
                    last = nc.tensor.matmul(ps[:, 4 + vb % 2, P * j:TP], lhsT=rvt[:, j, vb * P:(vb + 1) * P],
                                            rhs=ratt[:, RAT[j]:RAT[j] + TP - P * j],
                                            start=(j == 0), stop=True, skip_group_check=True)
                last.then_inc(S("ro_done"), 1)
            for kk in range(2):
                pe.wait_ge(S("ro_out"), count("ro_out", R(3 + kk, 5)))
                for j in range(CH):
                    last = nc.tensor.matmul(ps[:, 4 + kk, :], lhsT=kd[:, j, kk * P:(kk + 1) * P], rhs=rvt[:, j, :],
                                            start=(j == 0), stop=(j == CH - 1))
                last.then_inc(S("rstate"), 1)
            for vb in range(4):
                nc.tensor.matmul(ps[:, 6, vb * TS:(vb + 1) * TS], lhsT=rvt[0:TS, CH, vb * P:(vb + 1) * P],
                                 rhs=ratts[0:TS, :], start=(vb == 0), stop=True, skip_group_check=True)
            pe.wait_ge(S("kdm"), count("kdm", R(1, 1)))
            pe.wait_ge(S("qd"), count("qd", R(1, 1)))
            pe.wait_ge(S("rstate_out"), count("rstate_out", R(2, 2)))
            for b in range(NBAT):
                g = R(b, NBAT)
                pe.wait_ge(S(f"rS0_in{b % 4}"), count(f"rS0_in{b % 4}", Lin(16 * (b // 4 + 1), 32, i)))
                for kk in range(2):
                    for vb in range(4):
                        o = vb * TS + LS * b
                        last = nc.tensor.matmul(ps[:, 6, o:o + LS], lhsT=rS0[:, b % 4, kk, vb * P:(vb + 1) * P],
                                                rhs=qd[:, kk, LS * b:LS * b + LS], start=False,
                                                stop=(kk == 1), skip_group_check=True)
                if b == NBAT - 1:
                    last.then_inc(S("ro_done"), 1)
                for kk in range(2):
                    j = 2 * b + kk
                    if j >= 2:
                        pe.wait_ge(S("rnew"), count("rnew", R(j - 1, 16)))
                    last = nc.tensor.matmul(ps[:, 5 + 2 * kk, :], lhsT=kdm[0:TS, b, kk * P:(kk + 1) * P],
                                            rhs=rvt[0:TS, CH, :], start=True, stop=True)
                    last.then_inc(S("rkv"), 1)
            pe.wait_ge(S("rnew"), count("rnew", R(16, 16)))
            pe.wait_ge(S("ro_out"), count("ro_out", R(5, 5)))
            for a in range(2):
                for vb in range(4):
                    last = nc.tensor.matmul(ps[:, 4 + a, 0:TH], lhsT=ones[:, :], rhs=ro[:, vb, a * TH:(a + 1) * TH],
                                            start=(vb == 0), stop=(vb == 3))
            last.then_inc(S("rmean"), 1)
            pe.wait_ge(S("rcent"), count("rcent", R(4, 4)))
            for vb in range(4):
                pe.wait_ge(S("rsq"), count("rsq", R(vb + 1, 4)))
                for a in range(2):
                    last = nc.tensor.matmul(ps[:, 4 + a, 0:TH], lhsT=ones[:, :], rhs=rv[:, vb % 2, a * TH:(a + 1) * TH],
                                            start=(vb == 0), stop=(vb == 3), skip_group_check=True)
                last.then_inc(S("rvar"), 1)
            for m in range(NB):
                def ready(k):
                    if m == 0:
                        pe.wait_ge(S("rmixl"), count("rmixl", R(k + 1, 4)))
                unit(n + 12 + m // 2, u + 12 + m, hin, 4, w0=4 * (m % 2), before=ready if m == 0 else None)

        pe.wait_ge(S("const_in"), count("const_in", 48))
        pe.wait_ge(S("ones"), count("ones", 1))
        for ph_ in phases:
            n, u, norm = Lin(ph_["n"]), Lin(ph_["u"]), ph_["norm"]
            norm_sum(norm)
            x_ready = lambda k: pe.wait_ge(S("xl_made"), count("xl_made", NB * norm + k + 1))
            x_ready(NB - 1)
            if ph_["kind"] == "ffn":
                j0 = ph_["j"]
                for J in FF_PARTS:
                    with pe.Fori(0, J // 2) as i:
                        for k in range(4):
                            unit(Lin(n.c + k, 4, i), Lin(u.c + k, 4, i), xin, NB)
                    n, u = n + 2 * J, u + 2 * J
                    for m in range(NB):
                        unit(n + m, u + m, hin, J,
                             before=(lambda k: pe.wait_ge(S("hid_low"), count("hid_low", j0 + k + 1))) if m == 0 else None)
                    n, u, j0 = n + NB, u + NB, j0 + J
            elif ph_["kind"] == "ab":
                with pe.Fori(0, H) as i:
                    gated_group(1, Lin(n.c, 4, i), Lin(u.c, 4, i), i, None)
                n, u = n + 4 * H, u + 4 * H
                unit(n, u, xin, NB)
                pe.wait_ge(S(f"taken{u.mod(2)}"), count(f"taken{u.mod(2)}", u.div(2) + 1))
                pe.wait_ge(S("gk2_in"), count("gk2_in", 16))
                pe.wait_ge(S("orms"), count("orms", H))
                pe.wait_ge(S("turned_out"), count("turned_out", 6 * H))
                for p in range(2):
                    for a in range(2):
                        last = nc.tensor.matmul(ps[:, 4 + 2 * p + a, 0:TH], lhsT=gk2[:, p * P:(p + 1) * P],
                                                rhs=lr[0:16, a * TH:(a + 1) * TH], start=True, stop=True)
                last.then_inc(S("gkz"), 1)
                pe.wait_ge(S("gkz_out"), count("gkz_out", 2))
                n, u = n + 1, u + 1
                for p in range(2):
                    gated_group(2, n, u, None, p)
                    n, u = n + N_GLA, u + N_GLA
                for m in range(NB):
                    unit(n + m, u + m, hin, NB,
                         before=(lambda k: pe.wait_ge(S("omixl"), count("omixl", k + 1))) if m == 0 else None)
            elif ph_["kind"] == "ret":
                with pe.Fori(0, H) as i:
                    retention_head(Lin(n.c, N_RET, i), Lin(u.c, 12 + NB, i), i)
            else:
                for m in range(NB):
                    unit(n + m, u + m, xin, NB)
                pe.wait_ge(S("p_low"), count("p_low", 2 * (ph_["layer"] + 1)))
                n, u = n + NB, u + NB
                for m in range(NB):
                    unit(n + m // 4, u + m, lambda r, k: (ph, pl)[r][:, k, :], 2, w0=2 * (m % 4))
        norm_sum(8)

    @block.scalar
    def _(act):
        def split(n, used):
            if n.c >= N_PIECES:
                return
            r = n.mod(NRAW)
            act.wait_ge(S(f"landed{r}"), count(f"landed{r}", Lin(16 * (n.c // NRAW + 1), 16 * n.k // NRAW, n.i)))
            act.wait_ge(S("unit"), count("unit", used))
            nc.scalar.activation(wh[:, n.mod(2), :], raw[:, r, :], ACT.Copy).then_inc(S("hi_made"), 1)

        def norm_prep(norm, m, ready):
            ready()
            if m >= 2:
                act.wait_ge(S("sqsum"), count("sqsum", 7 * norm + m - 1))
            elif norm:
                act.wait_ge(S("norm_sum"), count("norm_sum", norm))
            nc.scalar.activation(sq[:, m % 2, :], x[:, m, :], ACT.Square).then_inc(S("sq"), 1)
            if norm < 8:
                nc.scalar.activation(xh[:, m, :], x[:, m, :], ACT.Copy, scale=gains[:, norm, m:m + 1])\
                    .then_inc(S("xh_made"), 1)

        def norm_root(norm):
            act.wait_ge(S("norm_sum"), count("norm_sum", norm + 1))
            if norm:
                act.wait_ge(S("rinv"), count("rinv", norm))
            nc.scalar.activation(two(rms[:, :]), ps[:, 4:6, 0:TH], ACT.Sqrt, bias=eps, scale=1.0 / D)\
                .then_inc(S("rms"), 1)

        def gated_group(ns, n, u, i, pair):
            G = lambda name, k: group_count(name, ns, i, pair, k)
            rounds = [0]

            def turn_out(dst, prompt):
                rounds[0] += 1
                act.wait_ge(S("turned"), count("turned", G("turned", rounds[0])))
                if prompt:
                    src = ps[:, 7, :].rearrange("p (c k) -> p c k", c=CH)
                    nc.scalar.activation(dst[:, 0:CH, :], src, ACT.Copy).then_inc(S("turned_out"), 1)
                else:
                    nc.scalar.activation(dst[0:TS, CH, :], ps[0:TS, 7, 0:P], ACT.Copy).then_inc(S("turned_out"), 1)

            def step(k):
                split(n + (k + 2), u + (k + 1))

            def taken(k):
                act.wait_ge(S(f"taken{(u + k).mod(2)}"), count(f"taken{(u + k).mod(2)}", (u + k).div(2) + 1))

            step(0)
            if ns == 1:
                taken(0)
                nc.scalar.activation(s1[:, :], z1[:, :], ACT.Sigmoid).then_inc(S("sig"), 1)
                nc.scalar.activation(s2[:, :], z1[:, :], ACT.Sigmoid, scale=-1.0).then_inc(S("sig"), 1)
            step(1)
            if ns == 1:
                taken(1)
                act.wait_ge(S("k_ready"), count("k_ready", G("k_ready", 1)))
                nc.scalar.activation(s1[:, :], gate[:, 0, :], ACT.Sigmoid).then_inc(S("sig"), 1)
            step(2)
            turn_out(vt[:, 0], True)
            turn_out(vt[:, 0], False)
            step(3)
            if ns == 2:
                turn_out(vt[:, 1], True)
                turn_out(vt[:, 1], False)
                step(4)
                for s in range(2):
                    if s:
                        step(5)
                    taken(4 + s)
                    if s:
                        act.wait_ge(S("gate"), count("gate", G("gate", 1)))
                    nc.scalar.activation(s1[:, :], gate[:, s, :], ACT.Sigmoid).then_inc(S("sig"), 1)
            else:
                taken(3)
                act.wait_ge(S("q_ready"), count("q_ready", G("q_ready", 1)))
                nc.scalar.activation(s1[:, :], gate[:, 0, :], ACT.Sigmoid).then_inc(S("sig"), 1)
            turn_out(klt, True)
            turn_out(klt, False)
            for s in range(ns):
                act.wait_ge(S("o_done"), count("o_done", G("o_done", s + 1)))
                act.wait_ge(S("ot"), count("ot", G("ot", s)))
                act.wait_ge(S("gate"), count("gate", G("gate", ns)))
                nc.scalar.activation(go[:, 0:TP], ps[:, 4, :], ACT.Copy)
                nc.scalar.activation(go[:, TP:T], ps[:, 5, 0:TS], ACT.Copy).then_inc(S("o_out"), 1)
                act.wait_ge(S("o_out"), count("o_out", G("o_out", s + 1)))
                nc.scalar.activation(s1[:, :], go[:, :], ACT.Square).then_inc(S("osq"), 1)
                act.wait_ge(S("oss"), count("oss", G("oss", s + 1)))
                nc.scalar.activation(two(s2[:, :]), ps[:, 4:6, 0:TH], ACT.Sqrt, bias=eps, scale=1.0 / P)\
                    .then_inc(S("orms"), 1)
                act.wait_ge(S("omix"), count("omix", G("omix", s + 1)))
                dst = hid[0][:, i, :] if ns == 1 else hid[0][:, 4 + 2 * pair + s, :]
                nc.scalar.activation(dst, z1[:, :], ACT.Copy).then_inc(S("omixh"), 1)

        def retention_head(n, u, i):
            R = lambda k, per: Lin(k, per, i)

            def step(k):
                used = u + (k + 1 if k < 12 else 12 + 2 * (k - 11))
                split(n + (k + 2), used)

            def taken(k):
                act.wait_ge(S(f"taken{(u + k).mod(2)}"), count(f"taken{(u + k).mod(2)}", (u + k).div(2) + 1))

            def turn_v(vb):
                act.wait_ge(S("rturned"), count("rturned", R(vb + 1, 6)))
                nc.scalar.activation(rvt[:, 0:CH, vb * P:(vb + 1) * P],
                                     ps[:, 7, :].rearrange("p (c k) -> p c k", c=CH), ACT.Copy)
                nc.scalar.activation(rvt[0:TS, CH, vb * P:(vb + 1) * P], ps[0:TS, 6, 0:P], ACT.Copy)\
                    .then_inc(S("rturned_out"), 1)

            def silu(gb):
                taken(8 + gb)
                nc.scalar.activation(rg[:, gb, :], rv[:, gb % 2, :], ACT.Silu).then_inc(S("rgate"), 1)

            for k in range(4):
                step(k)
            step(4)
            for vb in range(1, 4):
                step(4 + vb)
                turn_v(vb - 1)
            step(8)
            turn_v(3)
            silu(0)
            act.wait_ge(S("ctab_in"), count("ctab_in", R(16, 16)))
            for kk in range(2):
                act.wait_ge(S("rturned"), count("rturned", R(5 + kk, 6)))
                for c in range(CH):
                    nc.scalar.activation(kd[:, c, kk * P:(kk + 1) * P], ps[:, 7, c * P:(c + 1) * P], ACT.Copy,
                                         scale=kdec[:, c:c + 1])
                nc.scalar.activation(kd[0:TS, CH, kk * P:(kk + 1) * P], ps[0:TS, 6, 0:P], ACT.Copy, scale=kdecs)\
                    .then_inc(S("rturned_out"), 1)
            for gb in range(1, 4):
                step(8 + gb)
                silu(gb)
            for vb in range(4):
                act.wait_ge(S("ro_done"), count("ro_done", R(vb + 1, 5)))
                nc.scalar.activation(ro[:, vb, 0:TP], ps[:, 4 + vb % 2, :], ACT.Copy).then_inc(S("ro_out"), 1)
            for kk in range(2):
                act.wait_ge(S("rstate"), count("rstate", R(kk + 1, 2)))
                nc.scalar.activation(rSt[:, kk, :], ps[:, 4 + kk, :], ACT.Copy).then_inc(S("rstate_out"), 1)
            act.wait_ge(S("ro_done"), count("ro_done", R(5, 5)))
            nc.scalar.activation(ro[:, :, TP:T], ps[:, 6, 0:4 * TS].rearrange("p (v t) -> p v t", v=4), ACT.Copy)\
                .then_inc(S("ro_out"), 1)
            for vb in range(4):
                act.wait_ge(S("rcent"), count("rcent", R(vb + 1, 4)))
                if vb >= 2:
                    act.wait_ge(S("rvar"), count("rvar", R(vb - 1, 4)))
                nc.scalar.activation(rv[:, vb % 2, :], ro[:, vb, :], ACT.Square).then_inc(S("rsq"), 1)
            act.wait_ge(S("rvar"), count("rvar", R(4, 4)))
            nc.scalar.activation(two(rr), ps[:, 4:6, 0:TH], ACT.Sqrt, bias=eps, scale=1.0 / 512).then_inc(S("rrms"), 1)
            for vb in range(4):
                act.wait_ge(S("rmix"), count("rmix", R(vb + 1, 4)))
                nc.scalar.activation(hid[0][:, vb, :], ro[:, vb, :], ACT.Copy).then_inc(S("rmixh"), 1)
            for k in range(12, 16):
                step(k)

        act.wait_ge(S("lb_shift"), count("lb_shift", 1))
        nc.scalar.activation(lbe, lbe, ACT.Exp).then_inc(S("lb_exp"), 1)
        act.wait_ge(S("eps"), count("eps", 1))
        split(Lin(0), 0)
        split(Lin(1), 0)
        act.wait_ge(S("const_in"), count("const_in", 48))
        act.wait_ge(S("x_in"), count("x_in", 16 * NB))
        for m in range(NB):
            norm_prep(0, m, lambda: None)
        for ph_ in phases:
            n, u, norm = Lin(ph_["n"]), Lin(ph_["u"]), ph_["norm"]
            norm_root(norm)

            def x_new(k):
                act.wait_ge(S(f"taken{(u + k).mod(2)}"), count(f"taken{(u + k).mod(2)}", (u + k).div(2) + 1))

            if ph_["kind"] == "ffn":
                j0 = ph_["j"]
                for part, J in enumerate(FF_PARTS):
                    with act.Fori(0, J // 2) as i:
                        for k in range(2):
                            nn, uu = Lin(n.c + 2 * k, 4, i), Lin(u.c + 2 * k, 4, i)
                            j = Lin(j0 + k, 2, i)
                            split(nn + 2, uu + 1)
                            act.wait_ge(S(f"taken{uu.mod(2)}"), count(f"taken{uu.mod(2)}", uu.div(2) + 1))
                            act.wait_ge(S("gated"), count("gated", j))
                            nc.scalar.activation(fs[:, k, :], fa[:, k, :], ACT.Silu).then_inc(S("silu"), 1)
                            split(nn + 3, uu + 2)
                            act.wait_ge(S("gated"), count("gated", j + 1))
                            dst = hid[0][:, i * 2 + k, :]
                            nc.scalar.activation(dst, ff[:, k, :], ACT.Copy).then_inc(S("hid_high"), 1)
                    n, u, j0 = n + 2 * J, u + 2 * J, j0 + J
                    for m in range(NB):
                        split(n + (m + 2), u + (m + 1))
                        if part == 2:
                            norm_prep(norm + 1, m, lambda: x_new(m))
                    n, u = n + NB, u + NB
            elif ph_["kind"] == "ab":
                with act.Fori(0, H) as i:
                    gated_group(1, Lin(n.c, 4, i), Lin(u.c, 4, i), i, None)
                n, u = n + 4 * H, u + 4 * H
                split(n + 2, u + 1)
                for p in range(2):
                    act.wait_ge(S("gkz_out"), count("gkz_out", p + 1))
                    if p:
                        act.wait_ge(S("gk_min"), count("gk_min", 1))
                    nc.scalar.activation(s1[:, :], z1[:, :], ACT.Abs).then_inc(S("gk_ln"), 1)
                    act.wait_ge(S("gk_ln"), count("gk_ln", 3 * p + 1))
                    nc.scalar.activation(s2[:, :], s1[:, :], ACT.Exp, scale=-1.0).then_inc(S("gk_ln"), 1)
                    act.wait_ge(S("gk_ln"), count("gk_ln", 3 * p + 2))
                    nc.scalar.activation(s1[:, :], s2[:, :], ACT.Ln, bias=1.0).then_inc(S("gk_ln"), 1)
                    act.wait_ge(S("gk_min"), count("gk_min", p + 1))
                    nc.scalar.activation(decay[:, p, :], z1[:, :], ACT.Exp, scale=1.0 / 16).then_inc(S("decay"), 1)
                n, u = n + 1, u + 1
                for p in range(2):
                    gated_group(2, n, u, None, p)
                    n, u = n + N_GLA, u + N_GLA
                for m in range(NB):
                    split(n + (m + 2), u + (m + 1))
                    norm_prep(norm + 1, m, lambda: x_new(m))
            elif ph_["kind"] == "ret":
                with act.Fori(0, H) as i:
                    retention_head(Lin(n.c, N_RET, i), Lin(u.c, 12 + NB, i), i)
                u = u + H * (12 + NB)
                for m in range(NB):
                    norm_prep(norm + 1, m, lambda: act.wait_ge(S(f"taken{(u + (-NB + m)).mod(2)}"), count(f"taken{(u + (-NB + m)).mod(2)}", (u + (-NB + m)).div(2) + 1)))
            else:
                lay = ph_["layer"]
                act.wait_ge(S("praw_in"), count("praw_in", 16 * (lay + 1)))
                for k in range(2):
                    nc.scalar.activation(ph[:, k, :], praw[:, k, :], ACT.Copy).then_inc(S("p_high"), 1)
                for m in range(NB):
                    split(n + (m + 2), u + (m + 1))
                    act.wait_ge(S(f"taken{(u + m).mod(2)}"), count(f"taken{(u + m).mod(2)}", (u + m).div(2) + 1))
                    nc.scalar.activation(pg[:, m, :], pz[:, m % 2, :], ACT.Sigmoid).then_inc(S("pgate"), 1)
                n, u = n + NB, u + NB
                for m in range(NB):
                    if m % 4 == 3:
                        split(n + (m // 4 + 2), u + (m + 1))
                    norm_prep(norm + 1, m, lambda: act.wait_ge(S("p_added"), count("p_added", NB * lay + m + 1)))
        norm_root(8)

    @block.vector
    def _(dve):
        def split(n):
            if n.c >= N_PIECES:
                return
            dve.wait_ge(S("hi_made"), count("hi_made", n + 1))
            nc.vector.tensor_tensor(wl[:, n.mod(2), :], raw[:, n.mod(NRAW), :], wh[:, n.mod(2), :], ALU.subtract)\
                .then_inc(S("lo_made"), 1)

        def pair_of(u):
            s = u.mod(2)
            return ps[:, 2 * s:2 * s + 2, 0:TH]

        def scaled(dst, u):
            dve.wait_ge(S("unit"), count("unit", u + 1))
            nc.vector.tensor_tensor(two(dst), pair_of(u), two(rinv[:, :]), ALU.mult).then_inc(S(f"taken{u.mod(2)}"), 1)

        def add_to_x(m, u, scale):
            dve.wait_ge(S("unit"), count("unit", u + 1))
            nc.vector.scalar_tensor_tensor(out=two(x[:, m, :]), in0=pair_of(u), scalar=scale, in1=two(x[:, m, :]),
                                           op0=ALU.mult, op1=ALU.add).then_inc(S(f"taken{u.mod(2)}"), 1)

        def norm_low(norm, m):
            if norm == 8:
                return
            dve.wait_ge(S("xh_made"), count("xh_made", NB * norm + m + 1))
            nc.vector.scalar_tensor_tensor(out=xl[:, m, :], in0=x[:, m, :], scalar=gains[:, norm, m:m + 1],
                                           in1=xh[:, m, :], op0=ALU.mult, op1=ALU.subtract).then_inc(S("xl_made"), 1)

        def norm_inverse(norm):
            dve.wait_ge(S("rms"), count("rms", norm + 1))
            nc.vector.reciprocal(rinv[:, :], rms[:, :]).then_inc(S("rinv"), 1)
            dve.wait_ge(S("rinv"), count("rinv", norm + 1))

        def gated_group(ns, n, u, i, pair):
            G = lambda name, k: group_count(name, ns, i, pair, k)
            U = gU[:, :] if ns == 1 else decay[:, pair, :]

            def picked(lev):
                for s in range(ns):
                    j = lev * ns + s
                    reached = early(dve, count("scores", G("scores", j + 1)))
                    dve.wait_ge(S("masks_in"), 16)
                    dve.wait_ge(S("scores"), reached)
                    src = ps[:, 4 + j % 2, :].rearrange("p (c t) -> p c t", c=CH)
                    dst = att[:, s, 0:TP].rearrange("p (c t) -> p c t", c=CH)
                    if lev <= 3:
                        smp = ps[0:TS, 6, 256 * s + 64 * lev:256 * s + 64 * lev + TS]
                    if lev == 0:
                        dve.wait_ge(S("o_done"), count("o_done", G("o_done", 0)))
                        m = ident[:, :].unsqueeze(1).broadcast_to([P, CH, P])
                        nc.vector.tensor_tensor(dst, src, m, ALU.mult)
                        nc.vector.tensor_tensor(att[0:TS, s, TP:T], smp, ident[0:TS, 0:TS], ALU.mult)\
                            .then_inc(S("picked"), 1)
                        continue
                    dve.wait_ge(S("picked"), count("picked", G("picked", j)))
                    m = masks[:, lev - 1, :].unsqueeze(1).broadcast_to([P, CH, P])
                    last = nc.vector.copy_predicated(dst, m, src)
                    if lev <= 3:
                        last = nc.vector.copy_predicated(att[0:TS, s, TP:T], masks[0:TS, lev - 1, 0:TS], smp)
                    last.then_inc(S("picked"), 1)

            def level(lev):
                h = 1 << (lev - 1)
                R = T if h <= 4 else TP
                if lev > 2:
                    dve.wait_ge(S("scores"), count("scores", G("scores", (lev - 1) * ns)))
                else:
                    dve.wait_ge(S("oss"), count("oss", G("oss", 0)))
                ready_q(dve, ns, u, i)
                if lev > 1:
                    dve.wait_ge(S("u_up"), count("u_up", G("u_up", lev - 1)))
                nc.vector.tensor_tensor(qu[:, lev % 2, 0:R], gq[:, 0:R], U[:, 0:R], ALU.mult).then_inc(S("qu"), 1)
                dve.wait_ge(S("l_up"), count("l_up", G("l_up", lev + 1)))
                dve.wait_ge(S("qu"), count("qu", G("qu", lev)))
                v = U[:, 0:R].rearrange("p (b a h) -> p b a h", a=2, h=h)
                nc.vector.tensor_tensor(v[:, :, 1, :], v[:, :, 1, :],
                                        v[:, :, 0, h - 1:h].broadcast_to([P, R // (2 * h), h]), ALU.mult)\
                    .then_inc(S("u_up"), 1)

            def taken(k):
                dve.wait_ge(S(f"taken{(u + k).mod(2)}"), count(f"taken{(u + k).mod(2)}", (u + k).div(2) + 1))

            split(n + 2)
            if ns == 1:
                dve.wait_ge(S("omixl"), count("omixl", G("omixl", 0)))
                dve.wait_ge(S("kl"), count("kl", G("kl", 0)))
                scaled(z1[:, :], u)
                dve.wait_ge(S("sig"), count("sig", G("sig", 2)))
                nc.vector.tensor_scalar(gU[:, :], s1[:, :], one_lb_at(i), lb_at(i), ALU.mult, ALU.add)
                nc.vector.tensor_scalar(gk[:, :], s2[:, :], one_lb_at(i), None, ALU.mult).then_inc(S("k_ready"), 1)
            else:
                dve.wait_ge(S("unit"), count("unit", u + 1))
                dve.wait_ge(S("kl"), count("kl", G("kl", 0)))
                nc.vector.tensor_tensor(two(gk[:, :]), pair_of(u), two(rinv[:, :]), ALU.mult)\
                    .then_inc(S(f"taken{u.mod(2)}"), 1)
            split(n + 3)
            if ns == 1:
                scaled(gate[:, 0, :], u + 1)
                dve.wait_ge(S("sig"), count("sig", G("sig", 3)))
                nc.vector.tensor_tensor(gq[:, :], gate[:, 0, :], s1[:, :], ALU.mult).then_inc(S("q_ready"), 1)
            else:
                dve.wait_ge(S("unit"), count("unit", u + 2))
                nc.vector.scalar_tensor_tensor(out=two(gq[:, :]), in0=pair_of(u + 1), scalar=0.125,
                                               in1=two(rinv[:, :]), op0=ALU.mult, op1=ALU.mult)\
                    .then_inc(S(f"taken{(u + 1).mod(2)}"), 1)
                dve.wait_ge(S("decay"), count("decay", 2))
            level(1)
            level(2)
            split(n + 4)
            scaled(vf[:, :], u + 2)
            picked(0)
            picked(1)
            level(3)
            split(n + 5)
            if ns == 1:
                scaled(gate[:, 0, :], u + 3)
                dve.wait_ge(S("sig"), count("sig", G("sig", 4)))
                nc.vector.tensor_tensor(gate[:, 0, :], gate[:, 0, :], s1[:, :], ALU.mult).then_inc(S("gate"), 1)
            else:
                dve.wait_ge(S("turned"), count("turned", G("turned", 2)))
                scaled(vf[:, :], u + 3)
                for s in range(2):
                    split(n + (6 + s))
                    scaled(gate[:, s, :], u + (4 + s))
                    dve.wait_ge(S("sig"), count("sig", G("sig", s + 1)))
                    nc.vector.tensor_tensor(gate[:, s, :], gate[:, s, :], s1[:, :], ALU.mult).then_inc(S("gate"), 1)
            for lev in range(2, NLEV + 1):
                picked(lev)
                if lev + 2 <= NLEV:
                    level(lev + 2)
                if lev == NLEV - 1:
                    dve.wait_ge(S("scores"), count("scores", G("scores", 7 * ns)))
                    dve.wait_ge(S("u_up"), count("u_up", G("u_up", 7)))
                    nc.vector.tensor_tensor(qu[:, 0, :], gq[:, :], U, ALU.mult).then_inc(S("qu"), 1)
            k = 2 * ns + 3
            dve.wait_ge(S("turned"), count("turned", G("turned", k)))
            for c in range(CH):
                src = ps[:, 7, c * P:(c + 1) * P]
                if c == 0:
                    nc.vector.tensor_copy(St[:, 0, :], src).then_inc(S("s_step"), 1)
                    continue
                dve.wait_ge(S("s_step"), count("s_step", G("s_step", c)))
                last = nc.vector.scalar_tensor_tensor(out=St[:, c, :], in0=St[:, c - 1, :],
                                                      scalar=U[:, c * P + P - 1:c * P + P], in1=src,
                                                      op0=ALU.mult, op1=ALU.add)
                last.then_inc(S("turned_out" if c == CH - 1 else "s_step"), 1)
            dve.wait_ge(S("S0_in"), count("S0_in", G("S0_in", 16)))
            Tb = U[:, TP:T].rearrange("p (b t) -> p b t", t=LS)[:, :, LS - 1:LS].broadcast_to([P, NBAT, P])
            nc.vector.tensor_tensor(Sn[:, :, :], S0[:, :, :], Tb, ALU.mult).then_inc(S("s_new"), 1)
            dve.wait_ge(S("s_new"), count("s_new", G("s_new", 1)))
            dve.wait_ge(S("turned"), count("turned", G("turned", k + 1)))
            nc.vector.tensor_tensor(Sn[:, :, :].rearrange("p (a b) k -> p a (b k)", a=2),
                                    Sn[:, :, :].rearrange("p (a b) k -> p a (b k)", a=2), ps[:, 6:8, :], ALU.add)\
                .then_inc(S("turned_out"), 1)
            for s in range(ns):
                dve.wait_ge(S("orms"), count("orms", G("orms", s + 1)))
                nc.vector.reciprocal(s2[:, :], s2[:, :]).then_inc(S("orr"), 1)
                dve.wait_ge(S("orr"), count("orr", G("orr", s + 1)))
                dve.wait_ge(S("omixl"), count("omixl", G("omixl", s)))
                nc.vector.scalar_tensor_tensor(out=z1[:, :], in0=go[:, :], scalar=gnormA if ns == 1 else gnormB,
                                               in1=s2[:, :], op0=ALU.mult, op1=ALU.mult).then_inc(S("ot"), 1)
                dve.wait_ge(S("ot"), count("ot", G("ot", s + 1)))
                nc.vector.tensor_tensor(z1[:, :], z1[:, :], gate[:, s, :], ALU.mult).then_inc(S("omix"), 1)

        def one_lb_at(i):
            return bounds[:, 1, i, :]

        def lb_at(i):
            return bounds[:, 0, i, :]

        def retention_head(n, u, i):
            R = lambda k, per: Lin(k, per, i)

            def rotate(dst, second, first, k):
                dve.wait_ge(S(f"taken{(u + k).mod(2)}"), count(f"taken{(u + k).mod(2)}", (u + k).div(2) + 1))
                nc.vector.tensor_tensor(dst[:, 0, :], rz[:, 0, :], cosT[:, :], ALU.mult)
                nc.vector.tensor_tensor(rtd[:, :], rz[:, 1, :], sinT[:, :], ALU.mult).then_inc(S("rot_a"), 1)
                dve.wait_ge(S("rot_a"), count("rot_a", R(first, 2)))
                nc.vector.tensor_tensor(dst[:, 0, :], dst[:, 0, :], rtd[:, :], ALU.subtract).then_inc(S(second), 1)

            split(n + 2)
            dve.wait_ge(S("rkv"), count("rkv", R(0, 16)))
            scaled(rz[:, 0, :], u)
            split(n + 3)
            scaled(rz[:, 1, :], u + 1)
            dve.wait_ge(S("rmix"), count("rmix", R(0, 4)))
            rotate(rq, "rot_q0", 1, 1)
            split(n + 4)
            dve.wait_ge(S("rot_q0"), count("rot_q0", R(1, 1)))
            dve.wait_ge(S("rot_q1"), count("rot_q1", R(1, 1)))
            scaled(rz[:, 0, :], u + 2)
            split(n + 5)
            scaled(rz[:, 1, :], u + 3)
            rotate(rk, "rot_k0", 2, 3)
            for vb in range(4):
                split(n + (6 + vb))
                if vb >= 2:
                    dve.wait_ge(S("rturned"), count("rturned", R(vb - 1, 6)))
                scaled(rv[:, vb % 2, :], u + (4 + vb))

            def picked(j):
                dve.wait_ge(S("rscores"), count("rscores", R(j + 1, 5)))
                if j == 0:
                    dve.wait_ge(S("ctab_in"), count("ctab_in", R(16, 16)))
                if j < 4:
                    nc.vector.tensor_tensor(ratt[:, RAT[j]:RAT[j] + TP - P * j], ps[:, 4 + j % 2, 0:TP - P * j],
                                            Dm[:, 0:TP - P * j], ALU.mult).then_inc(S("ratt"), 1)
                else:
                    nc.vector.tensor_tensor(ratts[0:TS, :], ps[0:TS, 6, 0:TS], Ds, ALU.mult).then_inc(S("ratt"), 1)

            for gb in range(4):
                split(n + (10 + gb))
                if gb >= 2:
                    dve.wait_ge(S("rgate"), count("rgate", R(gb - 1, 4)))
                else:
                    dve.wait_ge(S("rturned"), count("rturned", R(gb + 3, 6)))
                scaled(rv[:, gb % 2, :], u + (8 + gb))
                picked(gb)
            picked(4)
            for b in range(NBAT):
                for kk in range(2):
                    dve.wait_ge(S("rkv"), count("rkv", R(2 * b + kk + 1, 16)))
                    nc.vector.scalar_tensor_tensor(out=rS0[:, b % 4, kk, :], in0=rS0[:, b % 4, kk, :], scalar=gam,
                                                   in1=ps[:, 5 + 2 * kk, :], op0=ALU.mult, op1=ALU.add)\
                        .then_inc(S("rnew"), 1)
            dve.wait_ge(S("rmean"), count("rmean", R(1, 1)))
            for vb in range(4):
                nc.vector.scalar_tensor_tensor(out=two(ro[:, vb, :]), in0=ps[:, 4:6, 0:TH], scalar=-1.0 / 512,
                                               in1=two(ro[:, vb, :]), op0=ALU.mult, op1=ALU.add).then_inc(S("rcent"), 1)
            dve.wait_ge(S("rrms"), count("rrms", R(1, 1)))
            nc.vector.reciprocal(rr, rr).then_inc(S("rrr"), 1)
            dve.wait_ge(S("rrr"), count("rrr", R(1, 1)))
            dve.wait_ge(S("rgate"), count("rgate", R(4, 4)))
            for vb in range(4):
                nc.vector.scalar_tensor_tensor(out=ro[:, vb, :], in0=ro[:, vb, :], scalar=gnormR[:, vb:vb + 1],
                                               in1=rr, op0=ALU.mult, op1=ALU.mult).then_inc(S("rnorm"), 1)
            for vb in range(4):
                dve.wait_ge(S("rnorm"), count("rnorm", R(vb + 1, 4)))
                nc.vector.tensor_tensor(ro[:, vb, :], ro[:, vb, :], rg[:, vb, :], ALU.mult).then_inc(S("rmix"), 1)
            for m in range(NB):
                if m % 2 == 1:
                    split(n + (14 + m // 2))
                add_to_x(m, u + (12 + m), 1.0)

        dve.wait_ge(S("const_in"), count("const_in", 48))
        nc.vector.memset(eps, EPS).then_inc(S("eps"), 1)
        nc.vector.tensor_tensor(lbmax, logits[:, 0:4], logits[:, 4:8], ALU.max).then_inc(S("lb"), 1)
        dve.wait_ge(S("lb"), count("lb", 1))
        nc.vector.tensor_tensor(lbe[:, 0:4], logits[:, 0:4], lbmax, ALU.subtract)
        nc.vector.tensor_tensor(lbe[:, 4:8], logits[:, 4:8], lbmax, ALU.subtract).then_inc(S("lb_shift"), 1)
        dve.wait_ge(S("lb_exp"), count("lb_exp", 1))
        nc.vector.tensor_tensor(lbs, lbe[:, 0:4], lbe[:, 4:8], ALU.add).then_inc(S("lb"), 1)
        dve.wait_ge(S("lb"), count("lb", 2))
        nc.vector.reciprocal(lbs, lbs).then_inc(S("lb"), 1)
        dve.wait_ge(S("lb"), count("lb", 3))
        nc.vector.tensor_tensor(lb, lbe[:, 0:4], lbs, ALU.mult).then_inc(S("lb"), 1)
        dve.wait_ge(S("lb"), count("lb", 4))
        nc.vector.tensor_scalar(one_lb, lb, -1.0, 1.0, ALU.mult, ALU.add).then_inc(S("lb"), 1)
        dve.wait_ge(S("lb"), count("lb", 5))
        split(Lin(0))
        split(Lin(1))
        dve.wait_ge(S("x_in"), count("x_in", 16 * NB))
        for m in range(NB):
            norm_low(0, m)
        for ph_ in phases:
            n, u, norm = Lin(ph_["n"]), Lin(ph_["u"]), ph_["norm"]
            norm_inverse(norm)
            if ph_["kind"] == "ffn":
                j0 = ph_["j"]
                for part, J in enumerate(FF_PARTS):
                    with dve.Fori(0, J // 2) as i:
                        for k in range(2):
                            nn, uu = Lin(n.c + 2 * k, 4, i), Lin(u.c + 2 * k, 4, i)
                            j = Lin(j0 + k, 2, i)
                            split(nn + 2)
                            dve.wait_ge(S("silu"), count("silu", j))
                            scaled(fa[:, k, :], uu)
                            split(nn + 3)
                            scaled(fb[:, k, :], uu + 1)
                            dve.wait_ge(S("silu"), count("silu", j + 1))
                            dve.wait_ge(S(f"taken{(uu + 1).mod(2)}"), count(f"taken{(uu + 1).mod(2)}", (uu + 1).div(2) + 1))
                            dve.wait_ge(S("hid_low"), count("hid_low", j))
                            nc.vector.tensor_tensor(ff[:, k, :], fs[:, k, :], fb[:, k, :], ALU.mult)\
                                .then_inc(S("gated"), 1)
                    n, u, j0 = n + 2 * J, u + 2 * J, j0 + J
                    for m in range(NB):
                        split(n + (m + 2))
                        add_to_x(m, u + m, 0.5)
                        if part == 2 and m:
                            norm_low(norm + 1, m - 1)
                    n, u = n + NB, u + NB
                norm_low(norm + 1, NB - 1)
            elif ph_["kind"] == "ab":
                dve.wait_ge(S("masks_in"), count("masks_in", 16))
                with dve.Fori(0, H) as i:
                    gated_group(1, Lin(n.c, 4, i), Lin(u.c, 4, i), i, None)
                n, u = n + 4 * H, u + 4 * H
                split(n + 2)
                dve.wait_ge(S("unit"), count("unit", u + 1))
                dve.wait_ge(S("omixl"), count("omixl", H))
                nc.vector.tensor_tensor(two(lr[0:16, :]), ps[0:16, 2 * u.mod(2):2 * u.mod(2) + 2, 0:TH],
                                        two(rinv[0:16, :]), ALU.mult).then_inc(S(f"taken{u.mod(2)}"), 1)
                dve.wait_ge(S("gkz"), count("gkz", 1))
                for p in range(2):
                    if p:
                        dve.wait_ge(S("decay"), count("decay", 1))
                    nc.vector.tensor_scalar(two(z1[:, :]), ps[:, 4 + 2 * p:6 + 2 * p, 0:TH], bgk[:, p:p + 1], None,
                                            ALU.add).then_inc(S("gkz_out"), 1)
                    dve.wait_ge(S("gk_ln"), count("gk_ln", 3 * p + 3))
                    nc.vector.scalar_tensor_tensor(out=z1[:, :], in0=z1[:, :], scalar=0.0, in1=s1[:, :],
                                                   op0=ALU.min, op1=ALU.subtract).then_inc(S("gk_min"), 1)
                n, u = n + 1, u + 1
                for p in range(2):
                    gated_group(2, n, u, None, p)
                    n, u = n + N_GLA, u + N_GLA
                for m in range(NB):
                    split(n + (m + 2))
                    add_to_x(m, u + m, 1.0)
                    if m:
                        norm_low(norm + 1, m - 1)
                norm_low(norm + 1, NB - 1)
            elif ph_["kind"] == "ret":
                dve.wait_ge(S("rope_in"), count("rope_in", 32))
                with dve.Fori(0, H) as i:
                    retention_head(Lin(n.c, N_RET, i), Lin(u.c, 12 + NB, i), i)
                for m in range(NB):
                    norm_low(norm + 1, m)
            else:
                lay = ph_["layer"]
                for k in range(2):
                    dve.wait_ge(S("p_high"), count("p_high", 2 * lay + k + 1))
                    nc.vector.tensor_tensor(pl[:, k, :], praw[:, k, :], ph[:, k, :], ALU.subtract)\
                        .then_inc(S("p_low"), 1)
                for m in range(NB):
                    split(n + (m + 2))
                    if m >= 2:
                        dve.wait_ge(S("pgate"), count("pgate", NB * lay + m - 1))
                    scaled(pz[:, m % 2, :], u + m)
                n, u = n + NB, u + NB
                dve.wait_ge(S("pgate"), count("pgate", NB * (lay + 1)))
                for m in range(NB):
                    if m % 4 == 3:
                        split(n + (m // 4 + 2))
                    dve.wait_ge(S("unit"), count("unit", u + (m + 1)))
                    if m >= 2:
                        dve.wait_ge(S("p_added"), count("p_added", NB * lay + m - 1))
                    nc.vector.tensor_tensor(two(pt[:, m % 2, :]), pair_of(u + m), two(pg[:, m, :]), ALU.mult)\
                        .then_inc(S(f"taken{(u + m).mod(2)}"), 1)
                    dve.wait_ge(S(f"taken{(u + m).mod(2)}"), count(f"taken{(u + m).mod(2)}", (u + m).div(2) + 1))
                    nc.vector.tensor_tensor(x[:, m, :], x[:, m, :], pt[:, m % 2, :], ALU.add).then_inc(S("p_added"), 1)
                    if m:
                        norm_low(norm + 1, m - 1)
                norm_low(norm + 1, NB - 1)
        norm_inverse(8)
        for m in range(NB):
            dve.wait_ge(S("sq"), count("sq", NB * 8 + m + 1))
            nc.vector.scalar_tensor_tensor(out=x[:, m, :], in0=x[:, m, :], scalar=gains[:, 8, m:m + 1],
                                           in1=rinv[:, :], op0=ALU.mult, op1=ALU.mult).then_inc(S("y_ready"), 1)

    @block.gpsimd
    def _(pool):
        def norm_total(norm):
            for m in range(1, NB):
                pool.wait_ge(S("sq"), count("sq", NB * norm + m + 1))
                if m == 1:
                    if norm:
                        pool.wait_ge(S("norm_sum"), count("norm_sum", norm))
                    nc.gpsimd.tensor_tensor(sqsum[:, :], sq[:, 0, :], sq[:, 1, :], ALU.add).then_inc(S("sqsum"), 1)
                else:
                    pool.wait_ge(S("sqsum"), count("sqsum", 7 * norm + m - 1))
                    nc.gpsimd.tensor_tensor(sqsum[:, :], sqsum[:, :], sq[:, m % 2, :], ALU.add)\
                        .then_inc(S("sqsum"), 1)

        def gated_group(ns, u, i, pair):
            G = lambda name, k: group_count(name, ns, i, pair, k)
            U = gU[:, :] if ns == 1 else decay[:, pair, :]
            reached = early(pool, count("turned_out", G("turned_out", 0)))
            pool.wait_ge(S("ones"), 1)
            pool.wait_ge(S("turned_out"), reached)
            pool.wait_ge(S("o_done"), count("o_done", G("o_done", 0)))
            if ns == 1:
                pool.dma_start(S0[:, :, :], d["s_hgrn"][i]).then_inc(S("S0_in"), 16)
            else:
                pool.dma_start(S0[:, :, :], d["s_gla"][pair]).then_inc(S("S0_in"), 16)
            reached = early(pool, count("kl", G("kl", 0)))
            pool.wait_ge(S("ones"), 1)
            pool.wait_ge(S("kl"), reached)
            nc.gpsimd.memset(gL[:, :], 1.0).then_inc(S("l_up"), 1)
            ready_k(pool, ns, u, i)
            if ns == 2:
                pool.wait_ge(S("decay"), count("decay", 2))
            for lev in range(1, NLEV + 1):
                h = 1 << (lev - 1)
                R = T if h <= 4 else TP
                pool.wait_ge(S("l_up"), count("l_up", G("l_up", lev)))
                if lev > 1:
                    if lev > 3:
                        pool.wait_ge(S("scores"), count("scores", G("scores", (lev - 1) * ns)))
                    elif lev == 2:
                        pool.wait_ge(S("turned_out"), count("turned_out", G("turned_out", 0)))
                    nc.gpsimd.tensor_tensor(kl[:, lev % 2, 0:R], gk[:, 0:R], gL[:, 0:R], ALU.mult).then_inc(S("kl"), 1)
                    pool.wait_ge(S("kl"), count("kl", G("kl", lev - 1)))
                    pool.wait_ge(S("u_up"), count("u_up", G("u_up", lev - 1)))
                lv = gL[:, 0:R].rearrange("p (b a h) -> p b a h", a=2, h=h)
                uv = U[:, 0:R].rearrange("p (b a h) -> p b a h", a=2, h=h)
                nc.gpsimd.tensor_tensor(lv[:, :, 0, :], lv[:, :, 0, :],
                                        uv[:, :, 1, h - 1:h].broadcast_to([P, R // (2 * h), h]), ALU.mult)\
                    .then_inc(S("l_up"), 1)
                if lev == 4:
                    for s in range(ns):
                        pool.wait_ge(S("turned_out"), count("turned_out", G("turned_out", 2 * s + 2)))
                        nc.gpsimd.tensor_tensor(
                            vm[0:TS, s, :, :], vt[0:TS, s, CH, :].unsqueeze(1).broadcast_to([TS, NBAT, P]),
                            batch_of[0:TS, :].unsqueeze(2).broadcast_to([TS, NBAT, P]), ALU.mult)\
                            .then_inc(S("vm"), 1)
            pool.wait_ge(S("l_up"), count("l_up", G("l_up", 8)))
            pool.wait_ge(S("scores"), count("scores", G("scores", 7 * ns)))
            nc.gpsimd.tensor_tensor(kl[:, 0, :], gk[:, :], gL[:, :], ALU.mult).then_inc(S("kl"), 1)
            reached = early(pool, count("turned_out", G("turned_out", 2 * ns + 3)))
            pool.wait_ge(S("ones"), 1)
            pool.wait_ge(S("turned_out"), reached)
            dst = out["hgrn_p"][i] if ns == 1 else out["gla_p"][pair]
            pool.dma_start(dst, St[:, CH - 1, :]).then_inc(S("S_out"), 16)
            reached = early(pool, count("turned_out", G("turned_out", 2 * ns + 4)))
            pool.wait_ge(S("ones"), 1)
            pool.wait_ge(S("turned_out"), reached)
            dst = out["hgrn_s"][i] if ns == 1 else out["gla_s"][pair]
            pool.dma_start(dst, Sn[:, :, :]).then_inc(S("S_out"), 16)
            for s in range(ns):
                pool.wait_ge(S("omixh"), count("omixh", G("omixh", s + 1)))
                if ns == 1:
                    hi, lo = hid[0][:, i, :], hid[1][:, i, :]
                else:
                    hi, lo = hid[0][:, 4 + 2 * pair + s, :], hid[1][:, 4 + 2 * pair + s, :]
                nc.gpsimd.tensor_tensor(lo, z1[:, :], hi, ALU.subtract).then_inc(S("omixl"), 1)
            pool.wait_ge(S("S_out"), count("S_out", G("S_out", 32)))

        def retention_head(u, i):
            R = lambda k, per: Lin(k, per, i)
            reached = early(pool, count("rnew", R(0, 16)))
            pool.wait_ge(S("ones"), 1)
            pool.wait_ge(S("rnew"), reached)
            pool.wait_ge(S("ratt"), count("ratt", R(0, 5)))
            pool.dma_start(ctab[:, :], d["ctab"][i]).then_inc(S("ctab_in"), 16)

            def rotate(dst, k, a, done):
                for c in (k - 1, k):
                    pool.wait_ge(S(f"taken{(u + c).mod(2)}"), count(f"taken{(u + c).mod(2)}", (u + c).div(2) + 1))
                nc.gpsimd.tensor_tensor(dst[:, 1, :], rz[:, 1, :], cosT[:, :], ALU.mult)
                nc.gpsimd.tensor_tensor(rtp[:, :], rz[:, 0, :], sinT[:, :], ALU.mult).then_inc(S("rot_b"), 1)
                pool.wait_ge(S("rot_b"), count("rot_b", R(a, 2)))
                nc.gpsimd.tensor_tensor(dst[:, 1, :], dst[:, 1, :], rtp[:, :], ALU.add).then_inc(S(done), 1)

            rotate(rq, 1, 1, "rot_q1")
            rotate(rk, 3, 2, "rot_k1")
            pool.wait_ge(S("ctab_in"), count("ctab_in", R(16, 16)))
            pool.wait_ge(S("rot_q0"), count("rot_q0", R(1, 1)))
            pool.wait_ge(S("rot_q1"), count("rot_q1", R(1, 1)))
            nc.gpsimd.tensor_tensor(qd[:, :, :], rq[:, :, TP:T], qdec.unsqueeze(1).broadcast_to([P, 2, TS]), ALU.mult)\
                .then_inc(S("qd"), 1)
            pool.wait_ge(S("rturned_out"), count("rturned_out", R(6, 6)))
            pool.wait_ge(S("rot_k0"), count("rot_k0", R(1, 1)))
            pool.wait_ge(S("rot_k1"), count("rot_k1", R(1, 1)))
            nc.gpsimd.tensor_tensor(kdm[0:TS, :, :], kd[0:TS, CH, :].unsqueeze(1).broadcast_to([TS, NBAT, 2 * P]),
                                    batch_of[0:TS, :].unsqueeze(2).broadcast_to([TS, NBAT, 2 * P]), ALU.mult)\
                .then_inc(S("kdm"), 1)
            reached = early(pool, count("rstate_out", R(2, 2)))
            pool.wait_ge(S("ones"), 1)
            pool.wait_ge(S("rstate_out"), reached)
            pool.dma_start(out["ret_p"][i], rSt[:, :, :]).then_inc(S("rSt_stored"), 16)

            def reload(b):
                reached = early(pool, count(f"rS_out{b % 4}", Lin(16 * (b // 4 + 1), 32, i)))
                pool.wait_ge(S("ones"), 1)
                pool.wait_ge(S(f"rS_out{b % 4}"), reached)
                pool.dma_start(rS0[:, b % 4, :, :], d["s_ret"][(Lin(b + 4, NBAT, i)).value()])\
                    .then_inc(S(f"rS0_in{b % 4}"), 16)

            for b in range(NBAT):
                reached = early(pool, count("rnew", R(2 * b + 2, 16)))
                pool.wait_ge(S("ones"), 1)
                pool.wait_ge(S("rnew"), reached)
                pool.dma_start(out["ret_s"][Lin(b, NBAT, i).value()], rS0[:, b % 4, :, :])\
                    .then_inc(S(f"rS_out{b % 4}"), 16)
                if b:
                    reload(b - 1)
            reload(NBAT - 1)
            for vb in range(4):
                pool.wait_ge(S("rmixh"), count("rmixh", R(vb + 1, 4)))
                nc.gpsimd.tensor_tensor(hid[1][:, vb, :], ro[:, vb, :], hid[0][:, vb, :], ALU.subtract)\
                    .then_inc(S("rmixl"), 1)
            pool.wait_ge(S("rSt_stored"), count("rSt_stored", R(16, 16)))

        nc.gpsimd.memset(ones[:, :], 1.0).then_inc(S("ones"), 1)
        norm_total(0)
        for ph_ in phases:
            norm = ph_["norm"]
            if ph_["kind"] == "ffn":
                j0 = ph_["j"]
                for J in FF_PARTS:
                    with pool.Fori(0, J // 2) as i:
                        for k in range(2):
                            pool.wait_ge(S("hid_high"), count("hid_high", Lin(j0 + k + 1, 2, i)))
                            nc.gpsimd.tensor_tensor(hid[1][:, i * 2 + k, :], ff[:, k, :], hid[0][:, i * 2 + k, :], ALU.subtract)\
                                .then_inc(S("hid_low"), 1)
                    j0 += J
            elif ph_["kind"] == "ab":
                pool.wait_ge(S("hid_low"), count("hid_low", ph_["j"]))
                pool.wait_ge(S("norm_sum"), count("norm_sum", norm + 1))
                pool.dma_start(masks[:, :, :], d["masks"]).then_inc(S("masks_in"), 16)
                pool.dma_start(gk2, d["gk2"]).then_inc(S("gk2_in"), 16)
                pool.wait_ge(S("const_in"), count("const_in", 48))
                u0 = ph_["u"]
                with pool.Fori(0, H) as i:
                    gated_group(1, Lin(u0, 4, i), i, None)
                for p in range(2):
                    gated_group(2, Lin(u0 + 4 * H + 1 + N_GLA * p), None, p)
            elif ph_["kind"] == "ret":
                pool.wait_ge(S("hid_low"), count("hid_low", ph_["j"]))
                pool.dma_start(cosT[:, :], d["cosT"]).then_inc(S("rope_in"), 16)
                pool.dma_start(sinT[:, :], d["sinT"]).then_inc(S("rope_in"), 16)
                for b in range(4):
                    pool.dma_start(rS0[:, b, :, :], d["s_ret"][b]).then_inc(S(f"rS0_in{b}"), 16)
                pool.wait_ge(S("rope_in"), count("rope_in", 32))
                with pool.Fori(0, H) as i:
                    retention_head(Lin(ph_["u"], 12 + NB, i), i)
                for b in range(4):
                    pool.wait_ge(S(f"rS0_in{b}"), count(f"rS0_in{b}", 16 * (2 * H + 1)))
                    pool.wait_ge(S(f"rS_out{b}"), count(f"rS_out{b}", 32 * H))
            else:
                pool.wait_ge(S("hid_low"), count("hid_low", ph_["j"]))
                pool.dma_start(praw[:, :, :], d["pT"][ph_["layer"]]).then_inc(S("praw_in"), 16)
            norm_total(norm + 1)

    block_cm.__exit__(None, None, None)


def _tiles(w, k0, k1, c0):
    return w[k0 * P:k1 * P, c0:c0 + P].reshape(k1 - k0, P, P).transpose(1, 0, 2).reshape(P, -1)


def _weight_stream(a):
    w = np.zeros((N_PIECES, P, D), np.float32)
    n = 0

    def put(*parts):
        nonlocal n
        c = 0
        for t in parts:
            w[n, :, c:c + t.shape[1]] = t
            c += t.shape[1]
        n += 1

    def ffn(w_in, w_out):
        k = 0
        for J in FF_PARTS:
            for j in range(k, k + J):
                put(_tiles(w_in, 0, NB, j * P))
                put(_tiles(w_in, 0, NB, DFF + j * P))
            for m in range(NB):
                put(_tiles(w_out, k, k + J, m * P))
            k += J

    for layer in range(2):
        ffn(a["ffn1_w_in"][layer], a["ffn1_w_out"][layer])
        if layer == 0:
            w_in, w_out = a["ab_w_in"][0], a["ab_w_out"][0]
            for h in range(H):
                for c in (512, 0, 1024, 1536):
                    put(_tiles(w_in, 0, NB, c + h * P))
            put(_tiles(w_in, 0, NB, 3072))
            for p in range(2):
                for c in (2304 + p * P, 2048 + p * P, 2560 + 2 * p * P, 2688 + 2 * p * P,
                          3088 + 2 * p * P, 3216 + 2 * p * P):
                    put(_tiles(w_in, 0, NB, c))
            for m in range(NB):
                put(_tiles(w_out, 0, NB, m * P))
        else:
            w_in, w_out = a["ret_w_in"][0], a["ret_w_out"][0]
            for h in range(H):
                for base, per in ((0, 2), (1024, 2), (2048, 4), (4096, 4)):
                    for k in range(per):
                        put(_tiles(w_in, 0, NB, base + (h * per + k) * P))
                for m in range(0, NB, 2):
                    put(_tiles(w_out, 4 * h, 4 * h + 4, m * P), _tiles(w_out, 4 * h, 4 * h + 4, (m + 1) * P))
        ffn(a["ffn2_w_in"][layer], a["ffn2_w_out"][layer])
        for m in range(NB):
            put(_tiles(a["ple_w_gate"][layer], 0, NB, m * P))
        for m in range(0, NB, 4):
            put(*(_tiles(a["ple_w_proj"][layer], 0, 2, (m + k) * P) for k in range(4)))
    assert n == N_PIECES
    return w


def _columns(v):
    return v.reshape(-1, P).T


def _feature_major(prompt, sample, width):
    both = np.concatenate([prompt.reshape(TP, width), sample.reshape(TS, width)], 0)
    return np.ascontiguousarray(both.T).reshape(width // P, P, T)


def _constants():
    s, t = np.arange(P)[:, None], np.arange(P)[None, :]
    masks = np.zeros((P, NLEV, P), np.int32)
    for lev in range(NLEV):
        h = 1 << lev
        masks[:, lev] = (s // (2 * h) == t // (2 * h)) & (s // h % 2 == 0) & (t // h % 2 == 1)
    half = P
    inv = np.float32(10000.0) ** (-np.arange(half, dtype=np.float32) / np.float32(half))
    pos = np.concatenate([np.arange(TP), PAST + np.tile(np.arange(LS), NBAT)]).astype(np.float32)
    ang = (inv[:, None] * pos[None, :]).astype(np.float32).astype(np.float64)
    ctab = np.zeros((H, P, CT), np.float32)
    for h in range(H):
        lg = np.log1p(-np.exp2(-5.0 - h))
        r = np.arange(TP)[None, :] - np.arange(P)[:, None]
        ctab[h, :, 0:TP] = np.where(r >= 0, np.exp(lg * np.maximum(r, 0)) / 16, 0)
        s, t = np.arange(TS)[:, None], np.arange(TS)[None, :]
        ctab[h, 0:TS, TP:TP + TS] = np.where((s // LS == t // LS) & (t >= s), np.exp(lg * (t - s)) / 16, 0)
        ctab[h, :, TP + TS:TP + 2 * TS] = np.exp(lg * (np.arange(TS) % LS + 1))[None, :]
        o = TP + 2 * TS
        for c in range(CH):
            ctab[h, :, o + c] = np.exp(lg * (TP - 1 - (c * P + np.arange(P)))) / 16
        ctab[h, 0:TS, o + CH] = np.exp(lg * (LS - 1 - np.arange(TS) % LS)) / 16
        ctab[h, :, o + CH + 1] = np.exp(lg * LS)
    return {"masks": masks, "cosT": np.cos(ang).astype(np.float32), "sinT": np.sin(ang).astype(np.float32),
            "ctab": ctab, "ident": np.eye(P, dtype=np.float32)}


def kernel(**inputs):
    from concourse import bacc
    from concourse.bass_utils import run_bass_kernel_spmd

    a = {k: np.asarray(v) for k, v in inputs.items()}
    gains = np.zeros((P, 9, NB), np.float32)
    for layer in range(2):
        for k, name in enumerate(NORMS):
            gains[:, 4 * layer + k] = _columns(a[name][layer])
    gains[:, 8] = _columns(a["norm_final"])
    small = np.zeros((P, 24), np.float32)
    small[:, 0:1] = _columns(a["ab_gn_hgrn"][0])
    small[:, 1:2] = _columns(a["ab_gn_gla"][0])
    small[:, 2:6] = _columns(a["ret_gn"][0])
    small[:, 6:8] = _columns(a["ab_b_gk"][0])
    small[:, 8:12] = _columns(a["hgrn_lb_logits"][0])
    small[:, 12:16] = _columns(a["hgrn_lb_logits"][1])
    small[0:TS, 16:24] = np.arange(TS)[:, None] // LS == np.arange(NBAT)[None, :]
    s_ret = np.zeros((H * NBAT + 4, P, 2, 4 * P), np.float32)
    s_ret[:H * NBAT] = a["state_ret"][0].transpose(1, 0, 2, 3).reshape(H * NBAT, 2, P, 4 * P).transpose(0, 2, 1, 3)
    s_gla = a["state_gla"][0].reshape(NBAT, 2, 2, 64, P).transpose(1, 2, 3, 0, 4).reshape(2, P, NBAT, P)
    arrays = {
        "w": _weight_stream(a),
        "xT": _feature_major(a["x_prompt"], a["x_sample"], D),
        "pT": np.stack([_feature_major(a["p_prompt"][k], a["p_sample"][k], 2 * P).transpose(1, 0, 2) for k in range(2)]),
        "s_hgrn": a["state_hgrn"][0].transpose(1, 2, 0, 3), "s_gla": s_gla, "s_ret": s_ret,
        "gains": gains, "small": small, "gk2": a["ab_w_gk2"][0], **_constants(),
    }
    arrays = {k: np.ascontiguousarray(v) for k, v in arrays.items()}
    nc = bacc.Bacc("TRN2", target_bir_lowering=False, num_devices=1)
    d = {k: nc.dram_tensor(f"in_{k}", v.shape, mybir.dt.from_np(v.dtype), kind="ExternalInput").ap()
         for k, v in arrays.items()}
    shapes = {"yT": (NB, P, T), "hgrn_p": (H, P, P), "gla_p": (2, P, P), "ret_p": (H, P, 2, 4 * P),
              "hgrn_s": (H, P, NBAT, P), "gla_s": (2, P, NBAT, P), "ret_s": (H * NBAT, P, 2, 4 * P)}
    out = {k: nc.dram_tensor(f"out_{k}", v, F32, kind="ExternalOutput").ap() for k, v in shapes.items()}
    build(nc, d, out)
    r = run_bass_kernel_spmd(nc, [{f"in_{k}": v for k, v in arrays.items()}], core_ids=[0]).results[0]
    r = {k: np.asarray(r[f"out_{k}"]) for k in shapes}
    y = r["yT"].reshape(D, T).T
    c = np.ascontiguousarray
    return (c(y[:TP]).reshape(1, TP, D), c(y[TP:]).reshape(NBAT, LS, D),
            r["hgrn_p"].reshape(1, 1, H, P, P), r["gla_p"].reshape(1, 1, H, 64, P),
            c(r["ret_p"].transpose(0, 2, 1, 3)).reshape(1, 1, H, 2 * P, 4 * P),
            c(r["hgrn_s"].transpose(2, 0, 1, 3)).reshape(1, NBAT, H, P, P),
            c(r["gla_s"].reshape(2, 2, 64, NBAT, P).transpose(3, 0, 1, 2, 4)).reshape(1, NBAT, H, 64, P),
            c(r["ret_s"].reshape(H, NBAT, P, 2, 4 * P).transpose(1, 0, 3, 2, 4)).reshape(1, NBAT, H, 2 * P, 4 * P))
```

```python
import numpy as np
import concourse.bass as bass
import concourse.mybir as mybir

F32 = mybir.dt.float32
F32R = mybir.dt.float32r
I32 = mybir.dt.int32
ALU = mybir.AluOpType
ACT = mybir.ActivationFunctionType

P = 128
D = 1024
NB = D // P
TP, TS = 512, 64
T = TP + TS
TH = T // 2
NBAT, LS = 8, 8
DFF = 2816
FF_PARTS = (8, 8, 6)
H = 4
CH = TP // P
NRAW = 4
NLEV = 7
EPS = 1e-6
PAST = 4096
CT = TP + TS + TS + CH + 1 + 1
NORMS = ("norm_ffn1", "norm_mix", "norm_ffn2", "norm_ple")

N_FFN = sum(2 * j + NB for j in FF_PARTS)
N_HGRN, N_GLA, N_RET = 4, 6, 16
N_PIECES = 4 * N_FFN + H * N_HGRN + 1 + 2 * N_GLA + NB + H * N_RET + 2 * (NB + 2)


def early(eng, n):
    return n if isinstance(n, int) else eng.to_reg(n)


class Lin:

    def __init__(self, c, k=0, i=None):
        if i is None or isinstance(i, int):
            c, k = c + k * (i or 0), 0
        self.c, self.k, self.i = c, k, i

    def __add__(self, n):
        return Lin(self.c + n, self.k, self.i)

    def div(self, d):
        assert self.k % d == 0
        return Lin(self.c // d, self.k // d, self.i)

    def mod(self, d):
        assert self.k % d == 0
        return self.c % d

    def value(self):
        return self.c if not self.k else self.i * self.k + self.c


FROM_ONE = ("taken0", "taken1", "o_done", "oss", "orms", "ot", "omixl", "kl", "turned_out", "gated", "silu",
            "hid_low", "rkv", "rmix", "rnew", "ratt", "rturned_out")


def count(name, n):
    n = n if isinstance(n, Lin) else Lin(n)
    assert n.c >= 0 and (not n.k or n.c > 0 or name in FROM_ONE), name
    return (n + 1 if name in FROM_ONE else n).value()


def two(ap):
    return ap.rearrange("p (a b) -> p a b", a=2)


def build(nc, d, out):
    at = [16512]

    def sb(name, cols, dt=F32, where=None):
        n = int(np.prod(cols)) * 4
        if where is None:
            where = at[0]
            at[0] = (where + n + 31) // 32 * 32
        return nc.alloc_sbuf_tensor_at(name, [P] + list(cols), dt, offset=where)

    x = sb("x", [NB, T])
    xh = sb("xh", [NB, T], F32R)
    xl = sb("xl", [NB, T], F32R)
    raw = sb("raw", [NRAW, D])
    wh = sb("wh", [2, D], F32R)
    wl = sb("wl", [2, D], F32R)
    rinv = sb("rinv", [T])
    rms = sb("rms", [T])
    sq = sb("sq", [2, T])
    sqsum = sb("sqsum", [T])
    gains = sb("gains", [9, NB])
    ident = sb("ident", [P])
    ones = sb("ones", [P])
    small = sb("small", [64])
    gnormA = small[:, 0:1]
    gnormB = small[:, 1:2]
    gnormR = small[:, 2:6]
    bgk = small[:, 6:8]
    logits = small[:, 8:16]
    batch_of = small[:, 16:24]
    lbmax, lbe, lbs = small[:, 24:28], small[:, 28:36], small[:, 36:40]
    bounds = sb("bounds", [2, H, 1])
    lb, one_lb = bounds[:, 0, :, 0], bounds[:, 1, :, 0]
    eps = small[:, 48:49]
    spare = at[0] + 4 * T * 4
    hid = [sb("hid_high", [8, T], F32R), sb("hid_low", [8, T], F32R)]
    free = at[0]

    fa = sb("ff_a", [2, T])
    fs = sb("ff_silu", [2, T])
    fb = sb("ff_b", [2, T])
    ff = sb("ff_gated", [2, T])
    at[0] = free
    praw = sb("praw", [2, T])
    ph = sb("ph", [2, T], F32R)
    pl = sb("pl", [2, T], F32R)
    pz = sb("pz", [2, T])
    pg = sb("pgate", [NB, T])
    pt = sb("ptmp", [2, T])
    at[0] = free
    z1 = sb("z1", [T])
    s1 = sb("s1", [T])
    s2 = sb("s2", [T])
    gk = sb("gk", [T])
    gU = sb("gU", [T])
    gL = sb("gL", [T])
    gq = sb("gq", [T])
    qu = sb("qu", [2, T])
    kl = sb("kl", [2, T])
    gate = sb("gate", [2, T])
    vf = sb("vf", [T])
    go = sb("go", [T])
    decay = sb("decay", [2, T])
    vt = sb("vt", [2, CH + 1, P])
    att = sb("att", [2, T])
    klt = sb("klt", [CH + 1, P])
    St = sb("St", [CH, P])
    S0 = sb("S0", [NBAT, P])
    Sn = sb("Sn", [NBAT, P])
    vm = sb("vm", [2, NBAT, P])
    masks = sb("masks", [NLEV, P], I32)
    lr = go
    gk2 = sq[0:16, 0, 0:2 * P]
    at[0] = free
    rz = sb("rz", [2, T])
    rtd = sb("rtd", [T])
    rtp = sb("rtp", [T])
    kdm = sb("kdm", [NBAT, 2 * P], where=free)
    rq = sb("rq", [2, T])
    rk = sb("rk", [2, T])
    rv = sb("rv", [2, T])
    rvt = sb("rvt", [CH + 1, 4 * P])
    kd = sb("kd", [CH + 1, 2 * P])
    ratt = sb("ratt", [1280])
    ratts = sb("ratts", [TS])
    qd = sb("qd", [2, TS])
    rS0 = sb("rS0", [4, 2, 4 * P])
    rSt = sb("rSt", [2, 4 * P])
    ctab = sb("ctab", [CT])
    cosT = sb("cosT", [T])
    sinT = sb("sinT", [T])
    ro = sb("ro", [4, T], where=spare)
    rg = sb("rg", [4, T], where=spare + 8 * T * 4)
    Dm = ctab[:, 0:TP]
    Ds = ctab[0:TS, TP:TP + TS]
    qdec = ctab[:, TP + TS:TP + 2 * TS]
    kdec = ctab[:, TP + 2 * TS:TP + 2 * TS + CH]
    kdecs = ctab[0:TS, TP + 2 * TS + CH:TP + 2 * TS + CH + 1]
    gam = ctab[:, TP + 2 * TS + CH + 1:CT]
    rr = rms[:, :]
    rsum = sqsum[:, :]
    RAT = [0, 512, 896, 1152]

    ps = nc.alloc_psum_tensor("ps", [P, 8, 512], F32)

    sems = {}

    def S(name):
        if name not in sems:
            sems[name] = nc.alloc_semaphore(name)
        return sems[name]

    for name in FROM_ONE:
        nc.sync.sem_inc(S(name), 1)
    block_cm = nc.Block()
    block = block_cm.__enter__()

    phases, n, u, g, norm, ffj, ffu = [], 0, 0, 0, 0, 0, 0
    for layer in range(2):
        for kind in ("ffn", "ab" if layer == 0 else "ret", "ffn", "ple"):
            phases.append(dict(kind=kind, layer=layer, n=n, u=u, norm=norm, j=ffj))
            if kind == "ffn":
                n, u, ffj = n + N_FFN, u + N_FFN, ffj + sum(FF_PARTS)
            elif kind == "ab":
                m = H * N_HGRN + 1 + 2 * N_GLA + NB
                n, u = n + m, u + m
            elif kind == "ret":
                n, u = n + H * N_RET, u + H * (12 + NB)
            else:
                n, u = n + NB + 2, u + 2 * NB
            norm += 1
    assert n == N_PIECES

    def per_group(name, ns):
        return {"sig": 4 if ns == 1 else 2, "scores": 8 * ns, "picked": 8 * ns, "qu": 8, "kl": 7, "u_up": 7,
                "l_up": 8, "turned": 2 * ns + 4, "turned_out": 2 * ns + 4, "s_step": 3, "S0_in": 16, "S_out": 32,
                "s_new": 1}.get(name, ns)

    def ready_k(eng, ns, u, i):
        if ns == 1:
            eng.wait_ge(S("k_ready"), count("k_ready", Lin(1, 1, i)))
        else:
            eng.wait_ge(S(f"taken{u.mod(2)}"), count(f"taken{u.mod(2)}", u.div(2) + 1))

    def ready_q(eng, ns, u, i):
        if ns == 1:
            eng.wait_ge(S("q_ready"), count("q_ready", Lin(1, 1, i)))
        else:
            eng.wait_ge(S(f"taken{(u + 1).mod(2)}"), count(f"taken{(u + 1).mod(2)}", (u + 1).div(2) + 1))

    def group_count(name, ns, i, pair, k):
        if ns == 1:
            return Lin(k, per_group(name, 1), i)
        assert name not in ("k_ready", "q_ready")
        return Lin(H * per_group(name, 1) + pair * per_group(name, 2) + k)

    @block.sync
    def _(sp):
        for m in range(NB):
            sp.dma_start(x[:, m, :], d["xT"][m]).then_inc(S(f"x_in{m}"), 16)
            if m == 0:
                sp.dma_start(gains[:, :, :], d["gains"]).then_inc(S("small_in"), 16)
                sp.dma_start(small[:, 0:24], d["small"][:, 0:24]).then_inc(S("small_in"), 16)
            if m < 2:
                sp.dma_start(raw[:, m, :], d["w"][m]).then_inc(S(f"landed{m}"), 16)
        for m in (2, 3):
            sp.dma_start(raw[:, m, :], d["w"][m]).then_inc(S(f"landed{m}"), 16)
        sp.dma_start(ident[:, :], d["ident"]).then_inc(S("ident_in"), 16)

        def piece(k, i):
            n = Lin(NRAW + k, NRAW, i)
            sp.wait_ge(S("lo_made"), count("lo_made", n + (1 - NRAW)))
            sp.dma_start(raw[:, k % NRAW, :], d["w"][n.value()]).then_inc(S(f"landed{k % NRAW}"), 16)

        rounds = (N_PIECES - NRAW) // NRAW
        with sp.Fori(0, rounds) as i:
            for k in range(NRAW):
                piece(k, i)
        for k in range(rounds * NRAW, N_PIECES - NRAW):
            piece(k, None)
        for m in range(NB):
            sp.wait_ge(S("y_ready"), count("y_ready", m + 1))
            sp.dma_start(out["yT"][m], x[:, m, :]).then_inc(S("y_out"), 16)
        sp.wait_ge(S("y_out"), count("y_out", 16 * NB))

    @block.tensor
    def _(pe):
        def product(bank_pair, w0, rhs, K, first_piece_col=0):
            last = None
            for k in range(K):
                w = slice((w0 + k) * P, (w0 + k + 1) * P)
                for j, (wt, r) in enumerate(((wh, 0), (wh, 1), (wl, 0))):
                    for a in range(2):
                        last = nc.tensor.matmul(
                            ps[:, 2 * bank_pair + a, 0:TH], lhsT=wt[:, first_piece_col, w],
                            rhs=rhs(r, k)[:, a * TH:(a + 1) * TH],
                            start=(k == 0 and j == 0), stop=(k == K - 1 and j == 2))
            return last

        def unit(n, u, rhs, K, w0=0, before=None, between=None):
            pe.wait_ge(S("lo_made"), count("lo_made", n + 1))
            s = u.mod(2)
            pe.wait_ge(S(f"taken{s}"), count(f"taken{s}", u.div(2)))
            slot = n.mod(2)
            if before is None and between is None:
                product(s, w0, rhs, K, slot).then_inc(S("unit"), 1)
                return
            for k in range(K):
                if before is not None:
                    before(k)
                w = slice((w0 + k) * P, (w0 + k + 1) * P)
                for j, (wt, r) in enumerate(((wh, 0), (wh, 1), (wl, 0))):
                    for a in range(2):
                        last = nc.tensor.matmul(
                            ps[:, 2 * s + a, 0:TH], lhsT=wt[:, slot, w],
                            rhs=rhs(r, k)[:, a * TH:(a + 1) * TH],
                            start=(k == 0 and j == 0), stop=(k == K - 1 and j == 2))
                if k == K - 1:
                    last.then_inc(S("unit"), 1)
                if between is not None and k % 2 == 1:
                    between(k // 2)

        def xin(r, k):
            return (xh, xl)[r][:, k, :]

        def hin(r, k):
            return hid[r][:, k, :]

        def norm_sum(norm):
            pe.wait_ge(S("sqsum"), count("sqsum", 7 * (norm + 1)))
            for a in range(2):
                last = nc.tensor.matmul(ps[:, 4 + a, 0:TH], lhsT=ones[:, :], rhs=sqsum[:, a * TH:(a + 1) * TH],
                                        start=True, stop=True)
            last.then_inc(S("norm_sum"), 1)

        def gated_group(ns, n, u, i, pair, first=None):
            G = lambda name, k: group_count(name, ns, i, pair, k)
            rows = [slice(0, P)] if ns == 1 else [slice(0, 64), slice(64, P)]

            def scores(lev):
                if lev == 0:
                    ready_k(pe, ns, u, i)
                    ready_q(pe, ns, u, i)
                    ka, qa = gk[:, :], gq[:, :]
                else:
                    pe.wait_ge(S("qu"), count("qu", G("qu", lev)))
                    ka, qa = gk[:, :], qu[:, lev % 2, :]
                    if lev > 1:
                        pe.wait_ge(S("kl"), count("kl", G("kl", lev - 1)))
                        ka = kl[:, lev % 2, :]
                for s in range(ns):
                    j = lev * ns + s
                    bank = 4 + j % 2
                    if j >= 2:
                        pe.wait_ge(S("picked"), count("picked", G("picked", j - 1)))
                    else:
                        pe.wait_ge(S("orms"), count("orms", G("orms", 0)))
                    for c in range(CH):
                        t = slice(c * P, (c + 1) * P)
                        last = nc.tensor.matmul(ps[:, bank, t], lhsT=ka[rows[s], t], rhs=qa[rows[s], t],
                                                start=True, stop=True)
                    if lev <= 3:
                        t = slice(TP, T)
                        o = 256 * s + 64 * lev
                        if j:
                            pe.wait_ge(S("picked"), count("picked", G("picked", j)))
                        last = nc.tensor.matmul(ps[0:TS, 6, o:o + TS], lhsT=ka[rows[s], t], rhs=qa[rows[s], t],
                                                start=True, stop=True)
                    last.then_inc(S("scores"), 1)

            turn = [0]

            def free_turn():
                reached = early(pe, count("turned_out", G("turned_out", turn[0])))
                pe.wait_ge(S("ones"), 1)
                pe.wait_ge(S("turned_out"), reached)
                turn[0] += 1

            def turn_tiles(src, prompt):
                free_turn()
                if prompt:
                    for c in range(CH):
                        last = nc.tensor.transpose(ps[:, 7, c * P:(c + 1) * P], src[:, c * P:(c + 1) * P], ident[:, :])
                else:
                    last = nc.tensor.transpose(ps[0:TS, 7, 0:P], src[:, TP:T], ident[:, :])
                last.then_inc(S("turned"), 1)

            def turn_v(s, uv):
                pe.wait_ge(S(f"taken{uv.mod(2)}"), count(f"taken{uv.mod(2)}", uv.div(2) + 1))
                turn_tiles(vf, True)
                turn_tiles(vf, False)

            npc = 0

            def proj(k, before=None):
                unit(n + k, u + k, xin, NB, before=before)

            if first:
                first()
            else:
                proj(0)
            proj(1)
            proj(2)
            scores(0)
            turn_v(0, u + 2)
            scores(1)
            if ns == 2:
                proj(3)
                turn_v(1, u + 3)
                proj(4)
                proj(5)
            else:
                proj(3)
            for lev in range(2, NLEV + 1):
                scores(lev)
            pe.wait_ge(S("kl"), count("kl", G("kl", 7)))
            turn_tiles(kl[:, 0, :], True)
            turn_tiles(kl[:, 0, :], False)
            free_turn()
            for s in range(ns):
                for c in range(CH):
                    last = nc.tensor.matmul(ps[rows[s], 7, c * P:(c + 1) * P], lhsT=klt[:, c, rows[s]],
                                            rhs=vt[:, s, c, :], start=True, stop=True)
            last.then_inc(S("turned"), 1)
            free_turn()
            pe.wait_ge(S("picked"), count("picked", G("picked", 8 * ns)))
            for s in range(ns):
                pe.wait_ge(S("vm"), count("vm", G("vm", s + 1)))
                for a in range(2):
                    last = nc.tensor.matmul(ps[rows[s], 6 + a, :], lhsT=klt[0:TS, CH, rows[s]],
                                            rhs=vm[0:TS, s, 4 * a:4 * a + 4, :], start=True, stop=True)
            last.then_inc(S("turned"), 1)
            pe.wait_ge(S("qu"), count("qu", G("qu", 8)))
            pe.wait_ge(S("S0_in"), count("S0_in", G("S0_in", 16)))
            for s in range(ns):
                if s:
                    pe.wait_ge(S("orms"), count("orms", G("orms", s)))
                for c in range(CH):
                    t = slice(c * P, (c + 1) * P)
                    last = nc.tensor.matmul(ps[:, 4, t], lhsT=vt[:, s, c, :], rhs=att[:, s, t],
                                            start=True, stop=(c == 0))
                    if c:
                        last = nc.tensor.matmul(ps[:, 4, t], lhsT=St[rows[s], c - 1, :], rhs=qu[rows[s], 0, t],
                                                start=False, stop=True)
                last = nc.tensor.matmul(ps[:, 5, 0:TS], lhsT=vt[0:TS, s, CH, :], rhs=att[0:TS, s, TP:T],
                                        start=True, stop=True, skip_group_check=True)
                if s:
                    last.then_inc(S("own_tokens"), 1)
                    pe.wait_ge(S("own_tokens"), count("own_tokens", pair + 1))
                for b in range(NBAT):
                    t = slice(LS * b, LS * b + LS)
                    last = nc.tensor.matmul(ps[:, 5, t], lhsT=S0[rows[s], b, :],
                                            rhs=qu[rows[s], 0, TP + LS * b:TP + LS * b + LS],
                                            start=False, stop=True, skip_group_check=True)
                last.then_inc(S("o_done"), 1)
                pe.wait_ge(S("osq"), count("osq", G("osq", s + 1)))
                for a in range(2):
                    last = nc.tensor.matmul(ps[:, 4 + a, 0:TH], lhsT=ones[:, :],
                                            rhs=s1[:, a * TH:(a + 1) * TH], start=True, stop=True)
                last.then_inc(S("oss"), 1)

        def retention_head(n, u, i, last_head):
            R = lambda k, per: Lin(k, per, i)

            def turn_k(kk):
                pe.wait_ge(S("rturned_out"), count("rturned_out", R(kk, 6)))
                if kk == 0:
                    pe.wait_ge(S("rot_k0"), count("rot_k0", R(1, 1)))
                    pe.wait_ge(S("rot_k1"), count("rot_k1", R(1, 1)))
                for c in range(CH):
                    nc.tensor.transpose(ps[:, 7, c * P:(c + 1) * P], rk[:, kk, c * P:(c + 1) * P], ident[:, :])
                nc.tensor.transpose(ps[0:TS, 6, 0:P], rk[:, kk, TP:T], ident[:, :]).then_inc(S("rturned"), 1)

            def turn_v(vb):
                pe.wait_ge(S(f"taken{(u + vb).mod(2)}"), count(f"taken{(u + vb).mod(2)}", (u + vb).div(2) + 1))
                pe.wait_ge(S("rturned_out"), count("rturned_out", R(2 + vb, 6)))
                for c in range(CH):
                    nc.tensor.transpose(ps[:, 7, c * P:(c + 1) * P], rv[:, vb % 2, c * P:(c + 1) * P], ident[:, :])
                nc.tensor.transpose(ps[0:TS, 6, 0:P], rv[:, vb % 2, TP:T], ident[:, :]).then_inc(S("rturned"), 1)

            def scores(j):
                if j >= 2 and j < 4:
                    pe.wait_ge(S("ratt"), count("ratt", R(j - 1, 5)))
                if j == 4:
                    pe.wait_ge(S("rturned_out"), count("rturned_out", R(6, 6)))
                for kk in range(2):
                    if j < 4:
                        last = nc.tensor.matmul(ps[:, 4 + j % 2, 0:TP - P * j], lhsT=rk[:, kk, P * j:P * j + P],
                                                rhs=rq[:, kk, P * j:TP], start=(kk == 0), stop=(kk == 1))
                    else:
                        last = nc.tensor.matmul(ps[0:TS, 6, 0:TS], lhsT=rk[:, kk, TP:T], rhs=rq[:, kk, TP:T],
                                                start=(kk == 0), stop=(kk == 1))
                last.then_inc(S("rscores"), 1)

            def outputs(vb):
                if vb >= 2:
                    pe.wait_ge(S("ro_out"), count("ro_out", R(vb - 1, 5)))
                else:
                    pe.wait_ge(S("rturned_out"), count("rturned_out", R(3 + vb, 6)))
                    pe.wait_ge(S("ratt"), count("ratt", R(4, 5)))
                for j in range(CH):
                    last = nc.tensor.matmul(ps[:, 4 + vb % 2, P * j:TP], lhsT=rvt[:, j, vb * P:(vb + 1) * P],
                                            rhs=ratt[:, RAT[j]:RAT[j] + TP - P * j],
                                            start=(j == 0), stop=True, skip_group_check=True)
                last.then_inc(S("ro_done"), 1)

            def prompt_state(kk):
                pe.wait_ge(S("ro_out"), count("ro_out", R(3 + kk, 5)))
                for j in range(CH):
                    last = nc.tensor.matmul(ps[:, 4 + kk, :], lhsT=kd[:, j, kk * P:(kk + 1) * P], rhs=rvt[:, j, :],
                                            start=(j == 0), stop=(j == CH - 1))
                last.then_inc(S("rstate"), 1)

            def own_tokens():
                pe.wait_ge(S("ratt"), count("ratt", R(5, 5)))
                for vb in range(4):
                    nc.tensor.matmul(ps[:, 6, vb * TS:(vb + 1) * TS], lhsT=rvt[0:TS, CH, vb * P:(vb + 1) * P],
                                     rhs=ratts[0:TS, :], start=(vb == 0), stop=True, skip_group_check=True)
                pe.wait_ge(S("kdm"), count("kdm", R(1, 1)))
                pe.wait_ge(S("qd"), count("qd", R(1, 1)))

            def sequence(b, kk):
                if kk == 0:
                    pe.wait_ge(S(f"rS0_in{b % 4}"), count(f"rS0_in{b % 4}", Lin(16 * (b // 4 + 1), 32, i)))
                    for k in range(2):
                        for vb in range(4):
                            o = vb * TS + LS * b
                            last = nc.tensor.matmul(ps[:, 6, o:o + LS], lhsT=rS0[:, b % 4, k, vb * P:(vb + 1) * P],
                                                    rhs=qd[:, k, LS * b:LS * b + LS], start=False,
                                                    stop=(k == 1), skip_group_check=True)
                    if b == NBAT - 1:
                        last.then_inc(S("ro_done"), 1)
                j = 2 * b + kk
                if j == 8:
                    pe.wait_ge(S("rstate_out"), count("rstate_out", R(2, 2)))
                elif j:
                    pe.wait_ge(S("rnew"), count("rnew", R(j if j < 8 else j - 1, 16)))
                bank = 5 if b >= 4 and kk == 0 else 7
                nc.tensor.matmul(ps[:, bank, :], lhsT=kdm[0:TS, b, kk * P:(kk + 1) * P],
                                 rhs=rvt[0:TS, CH, :], start=True, stop=True).then_inc(S("rkv"), 1)

            def mean():
                pe.wait_ge(S("rsummed"), count("rsummed", R(3, 3)))
                pe.wait_ge(S("rnew"), count("rnew", R(16, 16)))
                for a in range(2):
                    last = nc.tensor.matmul(ps[:, 4 + a, 0:TH], lhsT=ones[:, :], rhs=sqsum[:, a * TH:(a + 1) * TH],
                                            start=True, stop=True)
                last.then_inc(S("rmean"), 1)

            def variance():
                pe.wait_ge(S("rcent"), count("rcent", R(4, 4)))
                pe.wait_ge(S("rsqsum"), count("rsqsum", R(3, 3)))
                for a in range(2):
                    last = nc.tensor.matmul(ps[:, 4 + a, 0:TH], lhsT=ones[:, :], rhs=sqsum[:, a * TH:(a + 1) * TH],
                                            start=True, stop=True)
                last.then_inc(S("rvar"), 1)

            between = {
                (0, 0): [lambda: turn_k(0)], (0, 1): [lambda: scores(0)], (0, 2): [lambda: turn_k(1)],
                (1, 0): [lambda: scores(1)], (1, 1): [lambda: turn_v(0)],
                (2, 0): [lambda: scores(2)], (2, 1): [lambda: turn_v(1)],
                (3, 0): [lambda: scores(3)], (3, 1): [lambda: turn_v(2)],
                (4, 0): [lambda: outputs(0)], (4, 1): [lambda: turn_v(3)], (4, 2): [lambda: outputs(1)],
                (4, 3): [lambda: scores(4)],
                (5, 0): [own_tokens, lambda: sequence(0, 0)], (5, 1): [lambda: sequence(0, 1), lambda: outputs(2)],
                (5, 2): [lambda: sequence(1, 0)], (5, 3): [lambda: sequence(1, 1), lambda: outputs(3)],
                (6, 0): [lambda: sequence(2, 0), lambda: prompt_state(0)], (6, 1): [lambda: sequence(2, 1)],
                (6, 2): [lambda: sequence(3, 0), lambda: prompt_state(1)], (6, 3): [lambda: sequence(3, 1)],
                (7, 0): [lambda: sequence(4, 0), lambda: sequence(4, 1)],
                (7, 1): [lambda: sequence(5, 0), lambda: sequence(5, 1)],
                (7, 2): [lambda: sequence(6, 0), lambda: sequence(6, 1)],
                (7, 3): [lambda: sequence(7, 0), lambda: sequence(7, 1)],
                (8, 3): [mean], (10, 0): [variance],
            }

            def put_in(k):
                def run(q):
                    for step in between.get((k, q), ()):
                        step()
                return run

            for k in range(8 if last_head else 12):
                unit(n + k, u + k, xin, NB, between=put_in(k))
            if last_head:
                mean()
                variance()
            o = 8 if last_head else 12
            for m in range(NB):
                ready = lambda k: pe.wait_ge(S("rmixl"), count("rmixl", R(k + 1, 4)))
                unit(n + (o + m // 2), u + (o + m), hin, 4, w0=4 * (m % 2), before=ready if m == 0 else None)

        def first_unit(norm, n, u):
            unit(n, u, xin, NB, before=lambda k: pe.wait_ge(S("xl_made"), count("xl_made", NB * norm + k + 1)))
            norm_sum(norm)

        pe.wait_ge(S("ones"), count("ones", 1))
        for ph_ in phases:
            n, u, norm = Lin(ph_["n"]), Lin(ph_["u"]), ph_["norm"]
            if ph_["kind"] == "ffn":
                j0 = ph_["j"]
                first_unit(norm, n, u)
                for k in range(1, 4):
                    unit(n + k, u + k, xin, NB)
                for part, J in enumerate(FF_PARTS):
                    with pe.Fori(0 if part else 1, J // 2) as i:
                        for k in range(4):
                            unit(Lin(n.c + k, 4, i), Lin(u.c + k, 4, i), xin, NB)
                    n, u = n + 2 * J, u + 2 * J
                    for m in range(NB):
                        unit(n + m, u + m, hin, J,
                             before=(lambda k: pe.wait_ge(S("hid_low"), count("hid_low", j0 + k + 1))) if m == 0 else None)
                    n, u, j0 = n + NB, u + NB, j0 + J
            elif ph_["kind"] == "ab":
                pe.wait_ge(S("ident_in"), count("ident_in", 16))
                gated_group(1, n, u, 0, None, first=lambda: first_unit(norm, n, u))
                with pe.Fori(1, H) as i:
                    gated_group(1, Lin(n.c, 4, i), Lin(u.c, 4, i), i, None)
                n, u = n + 4 * H, u + 4 * H
                unit(n, u, xin, NB)
                pe.wait_ge(S(f"taken{u.mod(2)}"), count(f"taken{u.mod(2)}", u.div(2) + 1))
                pe.wait_ge(S("gk2_in"), count("gk2_in", 16))
                pe.wait_ge(S("orms"), count("orms", H))
                pe.wait_ge(S("turned_out"), count("turned_out", 6 * H))
                for p in range(2):
                    for a in range(2):
                        last = nc.tensor.matmul(ps[:, 4 + 2 * p + a, 0:TH], lhsT=gk2[:, p * P:(p + 1) * P],
                                                rhs=lr[0:16, a * TH:(a + 1) * TH], start=True, stop=True)
                last.then_inc(S("gkz"), 1)
                pe.wait_ge(S("gkz_out"), count("gkz_out", 2))
                n, u = n + 1, u + 1
                for p in range(2):
                    gated_group(2, n, u, None, p)
                    n, u = n + N_GLA, u + N_GLA
                for m in range(NB):
                    unit(n + m, u + m, hin, NB,
                         before=(lambda k: pe.wait_ge(S("omixl"), count("omixl", k + 1))) if m == 0 else None)
            elif ph_["kind"] == "ret":
                first_unit(norm, n, u)
                for k in range(1, 4):
                    unit(n + k, u + k, xin, NB)
                with pe.Fori(0, H - 1) as i:
                    retention_head(Lin(n.c + 4, N_RET, i), Lin(u.c + 4, 12 + NB, i), i, False)
                retention_head(n + (4 + (H - 1) * N_RET), u + (4 + (H - 1) * (12 + NB)), H - 1, True)
            else:
                first_unit(norm, n, u)
                for m in range(1, NB):
                    unit(n + m, u + m, xin, NB)
                pe.wait_ge(S("p_low"), count("p_low", 2 * (ph_["layer"] + 1)))
                n, u = n + NB, u + NB
                for m in range(NB):
                    unit(n + m // 4, u + m, lambda r, k: (ph, pl)[r][:, k, :], 2, w0=2 * (m % 4))
        norm_sum(8)

    @block.scalar
    def _(act):
        def split(n, used):
            if n.c >= N_PIECES:
                return
            r = n.mod(NRAW)
            act.wait_ge(S(f"landed{r}"), count(f"landed{r}", Lin(16 * (n.c // NRAW + 1), 16 * n.k // NRAW, n.i)))
            act.wait_ge(S("unit"), count("unit", used))
            nc.scalar.activation(wh[:, n.mod(2), :], raw[:, r, :], ACT.Copy).then_inc(S("hi_made"), 1)

        def norm_prep(norm, m, ready):
            ready()
            if norm < 8:
                nc.scalar.activation(xh[:, m, :], x[:, m, :], ACT.Copy, scale=gains[:, norm, m:m + 1])\
                    .then_inc(S("xh_made"), 1)
            if m >= 2:
                act.wait_ge(S("sqsum"), count("sqsum", 7 * norm + m - 1))
            elif norm:
                act.wait_ge(S("norm_sum"), count("norm_sum", norm))
            nc.scalar.activation(sq[:, m % 2, :], x[:, m, :], ACT.Square).then_inc(S("sq"), 1)

        def norm_root(norm):
            act.wait_ge(S("norm_sum"), count("norm_sum", norm + 1))
            if norm:
                act.wait_ge(S("rinv"), count("rinv", norm))
            nc.scalar.activation(two(rms[:, :]), ps[:, 4:6, 0:TH], ACT.Sqrt, bias=eps, scale=1.0 / D)\
                .then_inc(S("rms"), 1)

        def gated_group(ns, n, u, i, pair):
            G = lambda name, k: group_count(name, ns, i, pair, k)
            rounds = [0]

            def turn_out(dst, prompt):
                rounds[0] += 1
                act.wait_ge(S("turned"), count("turned", G("turned", rounds[0])))
                if prompt:
                    src = ps[:, 7, :].rearrange("p (c k) -> p c k", c=CH)
                    nc.scalar.activation(dst[:, 0:CH, :], src, ACT.Copy).then_inc(S("turned_out"), 1)
                else:
                    nc.scalar.activation(dst[0:TS, CH, :], ps[0:TS, 7, 0:P], ACT.Copy).then_inc(S("turned_out"), 1)

            def step(k):
                split(n + (k + 2), u + (k + 1))

            def taken(k):
                act.wait_ge(S(f"taken{(u + k).mod(2)}"), count(f"taken{(u + k).mod(2)}", (u + k).div(2) + 1))

            step(0)
            if ns == 1:
                taken(0)
                nc.scalar.activation(s1[:, :], z1[:, :], ACT.Sigmoid).then_inc(S("sig"), 1)
                nc.scalar.activation(s2[:, :], z1[:, :], ACT.Sigmoid, scale=-1.0).then_inc(S("sig"), 1)
            step(1)
            if ns == 1:
                taken(1)
                act.wait_ge(S("k_ready"), count("k_ready", G("k_ready", 1)))
                nc.scalar.activation(s1[:, :], gate[:, 0, :], ACT.Sigmoid).then_inc(S("sig"), 1)
            step(2)
            turn_out(vt[:, 0], True)
            turn_out(vt[:, 0], False)
            step(3)
            if ns == 2:
                turn_out(vt[:, 1], True)
                turn_out(vt[:, 1], False)
                step(4)
                for s in range(2):
                    if s:
                        step(5)
                    taken(4 + s)
                    if s:
                        act.wait_ge(S("gate"), count("gate", G("gate", 1)))
                    nc.scalar.activation(s1[:, :], gate[:, s, :], ACT.Sigmoid).then_inc(S("sig"), 1)
            else:
                taken(3)
                act.wait_ge(S("q_ready"), count("q_ready", G("q_ready", 1)))
                nc.scalar.activation(s1[:, :], gate[:, 0, :], ACT.Sigmoid).then_inc(S("sig"), 1)
            turn_out(klt, True)
            turn_out(klt, False)
            for s in range(ns):
                act.wait_ge(S("o_done"), count("o_done", G("o_done", s + 1)))
                act.wait_ge(S("ot"), count("ot", G("ot", s)))
                act.wait_ge(S("gate"), count("gate", G("gate", ns)))
                nc.scalar.activation(go[:, 0:TP], ps[:, 4, :], ACT.Copy)
                nc.scalar.activation(go[:, TP:T], ps[:, 5, 0:TS], ACT.Copy).then_inc(S("o_out"), 1)
                act.wait_ge(S("o_out"), count("o_out", G("o_out", s + 1)))
                nc.scalar.activation(s1[:, :], go[:, :], ACT.Square).then_inc(S("osq"), 1)
                act.wait_ge(S("oss"), count("oss", G("oss", s + 1)))
                nc.scalar.activation(two(s2[:, :]), ps[:, 4:6, 0:TH], ACT.Sqrt, bias=eps, scale=1.0 / P)\
                    .then_inc(S("orms"), 1)
                act.wait_ge(S("omix"), count("omix", G("omix", s + 1)))
                dst = hid[0][:, i, :] if ns == 1 else hid[0][:, 4 + 2 * pair + s, :]
                nc.scalar.activation(dst, z1[:, :], ACT.Copy).then_inc(S("omixh"), 1)

        def retention_head(n, u, i, last_head):
            R = lambda k, per: Lin(k, per, i)
            o = 8 if last_head else 12

            def step(k):
                split(n + (k + 2), u + (k + 1 if k < o else o + 2 * (k - o + 1)))

            def turned_v(vb):
                act.wait_ge(S("rturned"), count("rturned", R(3 + vb, 6)))
                nc.scalar.activation(rvt[:, 0:CH, vb * P:(vb + 1) * P],
                                     ps[:, 7, :].rearrange("p (c k) -> p c k", c=CH), ACT.Copy)
                nc.scalar.activation(rvt[0:TS, CH, vb * P:(vb + 1) * P], ps[0:TS, 6, 0:P], ACT.Copy)\
                    .then_inc(S("rturned_out"), 1)

            def silu(gb):
                act.wait_ge(S(f"taken{(u + 4 + gb).mod(2)}"),
                            count(f"taken{(u + 4 + gb).mod(2)}", (u + 4 + gb).div(2) + 1))
                nc.scalar.activation(rg[:, gb, :], rv[:, gb % 2, :], ACT.Silu).then_inc(S("rgate"), 1)

            def output(vb):
                act.wait_ge(S("ro_done"), count("ro_done", R(vb + 1, 5)))
                nc.scalar.activation(ro[:, vb, 0:TP], ps[:, 4 + vb % 2, :], ACT.Copy).then_inc(S("ro_out"), 1)

            act.wait_ge(S("ctab_in"), count("ctab_in", R(16, 16)))
            for kk in range(2):
                act.wait_ge(S("rturned"), count("rturned", R(1 + kk, 6)))
                for c in range(CH):
                    nc.scalar.activation(kd[:, c, kk * P:(kk + 1) * P], ps[:, 7, c * P:(c + 1) * P], ACT.Copy,
                                         scale=kdec[:, c:c + 1])
                nc.scalar.activation(kd[0:TS, CH, kk * P:(kk + 1) * P], ps[0:TS, 6, 0:P], ACT.Copy, scale=kdecs)\
                    .then_inc(S("rturned_out"), 1)
            step(0)
            for k in range(1, 4):
                turned_v(k - 1)
                step(k)
            output(0)
            turned_v(3)
            output(1)
            step(4)
            silu(0)
            output(2)
            output(3)
            step(5)
            silu(1)
            for kk in range(2):
                act.wait_ge(S("rstate"), count("rstate", R(kk + 1, 2)))
                nc.scalar.activation(rSt[:, kk, :], ps[:, 4 + kk, :], ACT.Copy).then_inc(S("rstate_out"), 1)
            step(6)
            silu(2)
            step(7)
            silu(3)
            act.wait_ge(S("ro_done"), count("ro_done", R(5, 5)))
            nc.scalar.activation(ro[:, :, TP:T], ps[:, 6, 0:4 * TS].rearrange("p (v t) -> p v t", v=4), ACT.Copy)\
                .then_inc(S("ro_out"), 1)
            if not last_head:
                step(8)
            for vb in range(4):
                act.wait_ge(S("rcent"), count("rcent", R(vb + 1, 4)))
                if vb >= 2:
                    act.wait_ge(S("rsqsum"), count("rsqsum", R(vb - 1, 3)))
                nc.scalar.activation(sq[:, vb % 2, :], ro[:, vb, :], ACT.Square).then_inc(S("rsq"), 1)
            if not last_head:
                step(9)
            act.wait_ge(S("rvar"), count("rvar", R(1, 1)))
            nc.scalar.activation(two(rr), ps[:, 4:6, 0:TH], ACT.Sqrt, bias=eps, scale=1.0 / 512).then_inc(S("rrms"), 1)
            for vb in range(4):
                act.wait_ge(S("rmix"), count("rmix", R(vb + 1, 4)))
                nc.scalar.activation(hid[0][:, vb, :], ro[:, vb, :], ACT.Copy).then_inc(S("rmixh"), 1)
            if not last_head:
                step(10)
                step(11)
                for k in range(12, 16):
                    step(k)

        act.wait_ge(S("small_in"), count("small_in", 32))
        act.wait_ge(S("lb_shift"), count("lb_shift", 1))
        nc.scalar.activation(lbe, lbe, ACT.Exp).then_inc(S("lb_exp"), 1)
        act.wait_ge(S("eps"), count("eps", 1))
        split(Lin(0), 0)
        split(Lin(1), 0)
        for m in range(NB):
            norm_prep(0, m, lambda: act.wait_ge(S(f"x_in{m}"), count(f"x_in{m}", 16)))
        for ph_ in phases:
            n, u, norm = Lin(ph_["n"]), Lin(ph_["u"]), ph_["norm"]
            norm_root(norm)

            def x_new(k):
                act.wait_ge(S(f"taken{(u + k).mod(2)}"), count(f"taken{(u + k).mod(2)}", (u + k).div(2) + 1))

            if ph_["kind"] == "ffn":
                j0 = ph_["j"]
                for part, J in enumerate(FF_PARTS):
                    with act.Fori(0, J // 2) as i:
                        for k in range(2):
                            nn, uu = Lin(n.c + 2 * k, 4, i), Lin(u.c + 2 * k, 4, i)
                            j = Lin(j0 + k, 2, i)
                            split(nn + 2, uu + 1)
                            act.wait_ge(S(f"taken{uu.mod(2)}"), count(f"taken{uu.mod(2)}", uu.div(2) + 1))
                            act.wait_ge(S("gated"), count("gated", j))
                            nc.scalar.activation(fs[:, k, :], fa[:, k, :], ACT.Silu).then_inc(S("silu"), 1)
                            split(nn + 3, uu + 2)
                            act.wait_ge(S("gated"), count("gated", j + 1))
                            dst = hid[0][:, i * 2 + k, :]
                            nc.scalar.activation(dst, ff[:, k, :], ACT.Copy).then_inc(S("hid_high"), 1)
                    n, u, j0 = n + 2 * J, u + 2 * J, j0 + J
                    for m in range(NB):
                        split(n + (m + 2), u + (m + 1))
                        if part == 2:
                            norm_prep(norm + 1, m, lambda: x_new(m))
                    n, u = n + NB, u + NB
            elif ph_["kind"] == "ab":
                with act.Fori(0, H) as i:
                    gated_group(1, Lin(n.c, 4, i), Lin(u.c, 4, i), i, None)
                n, u = n + 4 * H, u + 4 * H
                split(n + 2, u + 1)
                for p in range(2):
                    act.wait_ge(S("gkz_out"), count("gkz_out", p + 1))
                    if p:
                        act.wait_ge(S("gk_min"), count("gk_min", 1))
                    nc.scalar.activation(s1[:, :], z1[:, :], ACT.Abs).then_inc(S("gk_ln"), 1)
                    act.wait_ge(S("gk_ln"), count("gk_ln", 3 * p + 1))
                    nc.scalar.activation(s2[:, :], s1[:, :], ACT.Exp, scale=-1.0).then_inc(S("gk_ln"), 1)
                    act.wait_ge(S("gk_ln"), count("gk_ln", 3 * p + 2))
                    nc.scalar.activation(s1[:, :], s2[:, :], ACT.Ln, bias=1.0).then_inc(S("gk_ln"), 1)
                    act.wait_ge(S("gk_min"), count("gk_min", p + 1))
                    nc.scalar.activation(decay[:, p, :], z1[:, :], ACT.Exp, scale=1.0 / 16).then_inc(S("decay"), 1)
                n, u = n + 1, u + 1
                for p in range(2):
                    gated_group(2, n, u, None, p)
                    n, u = n + N_GLA, u + N_GLA
                for m in range(NB):
                    split(n + (m + 2), u + (m + 1))
                    norm_prep(norm + 1, m, lambda: x_new(m))
            elif ph_["kind"] == "ret":
                for k in range(4):
                    split(n + (k + 2), u + (k + 1))
                with act.Fori(0, H - 1) as i:
                    retention_head(Lin(n.c + 4, N_RET, i), Lin(u.c + 4, 12 + NB, i), i, False)
                n, u = n + (4 + (H - 1) * N_RET), u + (4 + (H - 1) * (12 + NB))
                retention_head(n, u, H - 1, True)
                u = u + (8 + NB)
                for m in range(NB):
                    if m % 2 == 1:
                        split(n + (10 + m // 2), u + (-NB + m + 1))
                    norm_prep(norm + 1, m, lambda: act.wait_ge(S(f"taken{(u + (-NB + m)).mod(2)}"), count(f"taken{(u + (-NB + m)).mod(2)}", (u + (-NB + m)).div(2) + 1)))
            else:
                lay = ph_["layer"]
                act.wait_ge(S("praw_in"), count("praw_in", 16 * (lay + 1)))
                for k in range(2):
                    nc.scalar.activation(ph[:, k, :], praw[:, k, :], ACT.Copy).then_inc(S("p_high"), 1)
                for m in range(NB):
                    split(n + (m + 2), u + (m + 1))
                    act.wait_ge(S(f"taken{(u + m).mod(2)}"), count(f"taken{(u + m).mod(2)}", (u + m).div(2) + 1))
                    nc.scalar.activation(pg[:, m, :], pz[:, m % 2, :], ACT.Sigmoid).then_inc(S("pgate"), 1)
                n, u = n + NB, u + NB
                for m in range(NB):
                    if m % 4 == 3:
                        split(n + (m // 4 + 2), u + (m + 1))
                    norm_prep(norm + 1, m, lambda: act.wait_ge(S("p_added"), count("p_added", NB * lay + m + 1)))
        norm_root(8)

    @block.vector
    def _(dve):
        def split(n):
            if n.c >= N_PIECES:
                return
            dve.wait_ge(S("hi_made"), count("hi_made", n + 1))
            nc.vector.tensor_tensor(wl[:, n.mod(2), :], raw[:, n.mod(NRAW), :], wh[:, n.mod(2), :], ALU.subtract)\
                .then_inc(S("lo_made"), 1)

        def pair_of(u):
            s = u.mod(2)
            return ps[:, 2 * s:2 * s + 2, 0:TH]

        def scaled(dst, u):
            dve.wait_ge(S("unit"), count("unit", u + 1))
            nc.vector.tensor_tensor(two(dst), pair_of(u), two(rinv[:, :]), ALU.mult).then_inc(S(f"taken{u.mod(2)}"), 1)

        def add_to_x(m, u, scale):
            dve.wait_ge(S("unit"), count("unit", u + 1))
            nc.vector.scalar_tensor_tensor(out=two(x[:, m, :]), in0=pair_of(u), scalar=scale, in1=two(x[:, m, :]),
                                           op0=ALU.mult, op1=ALU.add).then_inc(S(f"taken{u.mod(2)}"), 1)

        def norm_low(norm, m):
            if norm == 8:
                return
            dve.wait_ge(S("xh_made"), count("xh_made", NB * norm + m + 1))
            nc.vector.scalar_tensor_tensor(out=xl[:, m, :], in0=x[:, m, :], scalar=gains[:, norm, m:m + 1],
                                           in1=xh[:, m, :], op0=ALU.mult, op1=ALU.subtract).then_inc(S("xl_made"), 1)

        def norm_inverse(norm):
            dve.wait_ge(S("rms"), count("rms", norm + 1))
            nc.vector.reciprocal(rinv[:, :], rms[:, :]).then_inc(S("rinv"), 1)
            dve.wait_ge(S("rinv"), count("rinv", norm + 1))

        def gated_group(ns, n, u, i, pair):
            G = lambda name, k: group_count(name, ns, i, pair, k)
            U = gU[:, :] if ns == 1 else decay[:, pair, :]

            def picked(lev):
                for s in range(ns):
                    j = lev * ns + s
                    reached = early(dve, count("scores", G("scores", j + 1)))
                    dve.wait_ge(S("masks_in"), 16)
                    dve.wait_ge(S("scores"), reached)
                    src = ps[:, 4 + j % 2, :].rearrange("p (c t) -> p c t", c=CH)
                    dst = att[:, s, 0:TP].rearrange("p (c t) -> p c t", c=CH)
                    if lev <= 3:
                        smp = ps[0:TS, 6, 256 * s + 64 * lev:256 * s + 64 * lev + TS]
                    if lev == 0:
                        dve.wait_ge(S("o_done"), count("o_done", G("o_done", 0)))
                        m = ident[:, :].unsqueeze(1).broadcast_to([P, CH, P])
                        nc.vector.tensor_tensor(dst, src, m, ALU.mult)
                        nc.vector.tensor_tensor(att[0:TS, s, TP:T], smp, ident[0:TS, 0:TS], ALU.mult)\
                            .then_inc(S("picked"), 1)
                        continue
                    dve.wait_ge(S("picked"), count("picked", G("picked", j)))
                    m = masks[:, lev - 1, :].unsqueeze(1).broadcast_to([P, CH, P])
                    last = nc.vector.copy_predicated(dst, m, src)
                    if lev <= 3:
                        last = nc.vector.copy_predicated(att[0:TS, s, TP:T], masks[0:TS, lev - 1, 0:TS], smp)
                    last.then_inc(S("picked"), 1)

            def level(lev):
                h = 1 << (lev - 1)
                R = T if h <= 4 else TP
                if lev > 2:
                    dve.wait_ge(S("scores"), count("scores", G("scores", (lev - 1) * ns)))
                else:
                    dve.wait_ge(S("oss"), count("oss", G("oss", 0)))
                ready_q(dve, ns, u, i)
                if lev > 1:
                    dve.wait_ge(S("u_up"), count("u_up", G("u_up", lev - 1)))
                nc.vector.tensor_tensor(qu[:, lev % 2, 0:R], gq[:, 0:R], U[:, 0:R], ALU.mult).then_inc(S("qu"), 1)
                dve.wait_ge(S("l_up"), count("l_up", G("l_up", lev + 1)))
                dve.wait_ge(S("qu"), count("qu", G("qu", lev)))
                v = U[:, 0:R].rearrange("p (b a h) -> p b a h", a=2, h=h)
                nc.vector.tensor_tensor(v[:, :, 1, :], v[:, :, 1, :],
                                        v[:, :, 0, h - 1:h].broadcast_to([P, R // (2 * h), h]), ALU.mult)\
                    .then_inc(S("u_up"), 1)

            def taken(k):
                dve.wait_ge(S(f"taken{(u + k).mod(2)}"), count(f"taken{(u + k).mod(2)}", (u + k).div(2) + 1))

            split(n + 2)
            if ns == 1:
                dve.wait_ge(S("omixl"), count("omixl", G("omixl", 0)))
                dve.wait_ge(S("kl"), count("kl", G("kl", 0)))
                scaled(z1[:, :], u)
                dve.wait_ge(S("sig"), count("sig", G("sig", 2)))
                nc.vector.tensor_scalar(gU[:, :], s1[:, :], one_lb_at(i), lb_at(i), ALU.mult, ALU.add)
                nc.vector.tensor_scalar(gk[:, :], s2[:, :], one_lb_at(i), None, ALU.mult).then_inc(S("k_ready"), 1)
            else:
                dve.wait_ge(S("unit"), count("unit", u + 1))
                dve.wait_ge(S("kl"), count("kl", G("kl", 0)))
                nc.vector.tensor_tensor(two(gk[:, :]), pair_of(u), two(rinv[:, :]), ALU.mult)\
                    .then_inc(S(f"taken{u.mod(2)}"), 1)
            split(n + 3)
            if ns == 1:
                scaled(gate[:, 0, :], u + 1)
                dve.wait_ge(S("sig"), count("sig", G("sig", 3)))
                nc.vector.tensor_tensor(gq[:, :], gate[:, 0, :], s1[:, :], ALU.mult).then_inc(S("q_ready"), 1)
            else:
                dve.wait_ge(S("unit"), count("unit", u + 2))
                nc.vector.scalar_tensor_tensor(out=two(gq[:, :]), in0=pair_of(u + 1), scalar=0.125,
                                               in1=two(rinv[:, :]), op0=ALU.mult, op1=ALU.mult)\
                    .then_inc(S(f"taken{(u + 1).mod(2)}"), 1)
                dve.wait_ge(S("decay"), count("decay", 2))
            level(1)
            level(2)
            split(n + 4)
            scaled(vf[:, :], u + 2)
            picked(0)
            picked(1)
            level(3)
            split(n + 5)
            if ns == 1:
                scaled(gate[:, 0, :], u + 3)
                dve.wait_ge(S("sig"), count("sig", G("sig", 4)))
                nc.vector.tensor_tensor(gate[:, 0, :], gate[:, 0, :], s1[:, :], ALU.mult).then_inc(S("gate"), 1)
            else:
                dve.wait_ge(S("turned"), count("turned", G("turned", 2)))
                scaled(vf[:, :], u + 3)
                for s in range(2):
                    split(n + (6 + s))
                    scaled(gate[:, s, :], u + (4 + s))
                    dve.wait_ge(S("sig"), count("sig", G("sig", s + 1)))
                    nc.vector.tensor_tensor(gate[:, s, :], gate[:, s, :], s1[:, :], ALU.mult).then_inc(S("gate"), 1)
            for lev in range(2, NLEV + 1):
                picked(lev)
                if lev + 2 <= NLEV:
                    level(lev + 2)
                if lev == NLEV - 1:
                    dve.wait_ge(S("scores"), count("scores", G("scores", 7 * ns)))
                    dve.wait_ge(S("u_up"), count("u_up", G("u_up", 7)))
                    nc.vector.tensor_tensor(qu[:, 0, :], gq[:, :], U, ALU.mult).then_inc(S("qu"), 1)
            k = 2 * ns + 3
            dve.wait_ge(S("turned"), count("turned", G("turned", k)))
            for c in range(CH):
                src = ps[:, 7, c * P:(c + 1) * P]
                if c == 0:
                    nc.vector.tensor_copy(St[:, 0, :], src).then_inc(S("s_step"), 1)
                    continue
                dve.wait_ge(S("s_step"), count("s_step", G("s_step", c)))
                last = nc.vector.scalar_tensor_tensor(out=St[:, c, :], in0=St[:, c - 1, :],
                                                      scalar=U[:, c * P + P - 1:c * P + P], in1=src,
                                                      op0=ALU.mult, op1=ALU.add)
                last.then_inc(S("turned_out" if c == CH - 1 else "s_step"), 1)
            dve.wait_ge(S("S0_in"), count("S0_in", G("S0_in", 16)))
            Tb = U[:, TP:T].rearrange("p (b t) -> p b t", t=LS)[:, :, LS - 1:LS].broadcast_to([P, NBAT, P])
            nc.vector.tensor_tensor(Sn[:, :, :], S0[:, :, :], Tb, ALU.mult).then_inc(S("s_new"), 1)
            dve.wait_ge(S("s_new"), count("s_new", G("s_new", 1)))
            dve.wait_ge(S("turned"), count("turned", G("turned", k + 1)))
            nc.vector.tensor_tensor(Sn[:, :, :].rearrange("p (a b) k -> p a (b k)", a=2),
                                    Sn[:, :, :].rearrange("p (a b) k -> p a (b k)", a=2), ps[:, 6:8, :], ALU.add)\
                .then_inc(S("turned_out"), 1)
            for s in range(ns):
                dve.wait_ge(S("orms"), count("orms", G("orms", s + 1)))
                nc.vector.reciprocal(s2[:, :], s2[:, :]).then_inc(S("orr"), 1)
                dve.wait_ge(S("orr"), count("orr", G("orr", s + 1)))
                dve.wait_ge(S("omixl"), count("omixl", G("omixl", s)))
                nc.vector.scalar_tensor_tensor(out=z1[:, :], in0=go[:, :], scalar=gnormA if ns == 1 else gnormB,
                                               in1=s2[:, :], op0=ALU.mult, op1=ALU.mult).then_inc(S("ot"), 1)
                dve.wait_ge(S("ot"), count("ot", G("ot", s + 1)))
                nc.vector.tensor_tensor(z1[:, :], z1[:, :], gate[:, s, :], ALU.mult).then_inc(S("omix"), 1)

        def one_lb_at(i):
            return bounds[:, 1, i, :]

        def lb_at(i):
            return bounds[:, 0, i, :]

        def queries_keys(n, u, R, norm_steps=None):
            tail = norm_steps or [lambda: None] * 3

            def rotate(dst, second, first, k):
                dve.wait_ge(S(f"taken{(u + k).mod(2)}"), count(f"taken{(u + k).mod(2)}", (u + k).div(2) + 1))
                nc.vector.tensor_tensor(dst[:, 0, :], rz[:, 0, :], cosT[:, :], ALU.mult)
                nc.vector.tensor_tensor(rtd[:, :], rz[:, 1, :], sinT[:, :], ALU.mult).then_inc(S("rot_a"), 1)
                dve.wait_ge(S("rot_a"), count("rot_a", R(first, 2)))
                nc.vector.tensor_tensor(dst[:, 0, :], dst[:, 0, :], rtd[:, :], ALU.subtract).then_inc(S(second), 1)

            tail[0]()
            split(n + 2)
            scaled(rz[:, 0, :], u)
            tail[1]()
            split(n + 3)
            scaled(rz[:, 1, :], u + 1)
            rotate(rq, "rot_q0", 1, 1)
            tail[2]()
            split(n + 4)
            dve.wait_ge(S("rot_q0"), count("rot_q0", R(1, 1)))
            dve.wait_ge(S("rot_q1"), count("rot_q1", R(1, 1)))
            scaled(rz[:, 0, :], u + 2)
            split(n + 5)
            scaled(rz[:, 1, :], u + 3)
            rotate(rk, "rot_k0", 2, 3)

        def retention_head(n, u, i, last_head):
            R = lambda k, per: Lin(k, per, i)

            def picked(j):
                dve.wait_ge(S("rscores"), count("rscores", R(j + 1, 5)))
                if j == 0:
                    dve.wait_ge(S("ctab_in"), count("ctab_in", R(16, 16)))
                if j < 4:
                    nc.vector.tensor_tensor(ratt[:, RAT[j]:RAT[j] + TP - P * j], ps[:, 4 + j % 2, 0:TP - P * j],
                                            Dm[:, 0:TP - P * j], ALU.mult).then_inc(S("ratt"), 1)
                else:
                    nc.vector.tensor_tensor(ratts[0:TS, :], ps[0:TS, 6, 0:TS], Ds, ALU.mult).then_inc(S("ratt"), 1)

            def sequence(b):
                for kk in range(2):
                    bank = 5 if b >= 4 and kk == 0 else 7
                    dve.wait_ge(S("rkv"), count("rkv", R(2 * b + kk + 1, 16)))
                    nc.vector.scalar_tensor_tensor(out=rS0[:, b % 4, kk, :], in0=rS0[:, b % 4, kk, :], scalar=gam,
                                                   in1=ps[:, bank, :], op0=ALU.mult, op1=ALU.add)\
                        .then_inc(S("rnew"), 1)

            for k in range(4):
                split(n + (k + 2))
                picked(k)
                if k >= 2:
                    dve.wait_ge(S("rturned"), count("rturned", R(k + 1, 6)))
                scaled(rv[:, k % 2, :], u + k)
            for gb in range(4):
                for b in ((), (0, 1), (2, 3), (4, 5, 6, 7))[gb]:
                    sequence(b)
                split(n + (6 + gb))
                if gb == 0:
                    picked(4)
                if gb >= 2:
                    dve.wait_ge(S("rgate"), count("rgate", R(gb - 1, 4)))
                else:
                    dve.wait_ge(S("rturned"), count("rturned", R(5 + gb, 6)))
                scaled(rv[:, gb % 2, :], u + (4 + gb))

            def summed():
                dve.wait_ge(S("ro_out"), count("ro_out", R(5, 5)))
                nc.vector.tensor_tensor(rsum, ro[:, 0, :], ro[:, 1, :], ALU.add).then_inc(S("rsummed"), 1)
                for vb in (2, 3):
                    dve.wait_ge(S("rsummed"), count("rsummed", R(vb - 1, 3)))
                    nc.vector.tensor_tensor(rsum, rsum, ro[:, vb, :], ALU.add).then_inc(S("rsummed"), 1)

            def centred():
                dve.wait_ge(S("rmean"), count("rmean", R(1, 1)))
                for vb in range(4):
                    nc.vector.scalar_tensor_tensor(out=two(ro[:, vb, :]), in0=ps[:, 4:6, 0:TH], scalar=-1.0 / 512,
                                                   in1=two(ro[:, vb, :]), op0=ALU.mult, op1=ALU.add)\
                        .then_inc(S("rcent"), 1)

            def gated():
                dve.wait_ge(S("rgate"), count("rgate", R(4, 4)))
                for vb in range(4):
                    dve.wait_ge(S("rsq"), count("rsq", R(vb + 1, 4)))
                    nc.vector.scalar_tensor_tensor(out=ro[:, vb, :], in0=ro[:, vb, :], scalar=gnormR[:, vb:vb + 1],
                                                   in1=rg[:, vb, :], op0=ALU.mult, op1=ALU.mult)\
                        .then_inc(S("rnorm"), 1)
                dve.wait_ge(S("rrms"), count("rrms", R(1, 1)))
                nc.vector.reciprocal(rr, rr).then_inc(S("rrr"), 1)
                dve.wait_ge(S("rrr"), count("rrr", R(1, 1)))
                for vb in range(4):
                    dve.wait_ge(S("rnorm"), count("rnorm", R(vb + 1, 4)))
                    nc.vector.tensor_tensor(ro[:, vb, :], ro[:, vb, :], rr, ALU.mult).then_inc(S("rmix"), 1)

            if last_head:
                summed()
                centred()
                gated()
                return
            queries_keys(n + 8, u + 8, lambda k, per: R(k + per, per), [summed, centred, gated])
            for m in range(NB):
                if m % 2 == 1:
                    split(n + (14 + m // 2))
                add_to_x(m, u + (12 + m), 1.0)

        dve.wait_ge(S("small_in"), count("small_in", 32))
        nc.vector.memset(eps, EPS).then_inc(S("eps"), 1)
        nc.vector.tensor_tensor(lbmax, logits[:, 0:4], logits[:, 4:8], ALU.max).then_inc(S("lb"), 1)
        dve.wait_ge(S("lb"), count("lb", 1))
        nc.vector.tensor_tensor(lbe[:, 0:4], logits[:, 0:4], lbmax, ALU.subtract)
        nc.vector.tensor_tensor(lbe[:, 4:8], logits[:, 4:8], lbmax, ALU.subtract).then_inc(S("lb_shift"), 1)
        dve.wait_ge(S("lb_exp"), count("lb_exp", 1))
        nc.vector.tensor_tensor(lbs, lbe[:, 0:4], lbe[:, 4:8], ALU.add).then_inc(S("lb"), 1)
        dve.wait_ge(S("lb"), count("lb", 2))
        nc.vector.reciprocal(lbs, lbs).then_inc(S("lb"), 1)
        dve.wait_ge(S("lb"), count("lb", 3))
        nc.vector.tensor_tensor(lb, lbe[:, 0:4], lbs, ALU.mult).then_inc(S("lb"), 1)
        dve.wait_ge(S("lb"), count("lb", 4))
        nc.vector.tensor_scalar(one_lb, lb, -1.0, 1.0, ALU.mult, ALU.add).then_inc(S("lb"), 1)
        dve.wait_ge(S("lb"), count("lb", 5))
        split(Lin(0))
        split(Lin(1))
        for m in range(NB):
            dve.wait_ge(S(f"x_in{m}"), count(f"x_in{m}", 16))
            norm_low(0, m)
            dve.wait_ge(S("sq"), count("sq", m + 1))
            if m == 1:
                nc.vector.tensor_tensor(sqsum[:, :], sq[:, 0, :], sq[:, 1, :], ALU.add).then_inc(S("sqsum"), 1)
            elif m:
                dve.wait_ge(S("sqsum"), count("sqsum", m - 1))
                nc.vector.tensor_tensor(sqsum[:, :], sqsum[:, :], sq[:, m % 2, :], ALU.add)\
                    .then_inc(S("sqsum"), 1)
        for ph_ in phases:
            n, u, norm = Lin(ph_["n"]), Lin(ph_["u"]), ph_["norm"]
            norm_inverse(norm)
            if ph_["kind"] == "ffn":
                j0 = ph_["j"]
                for part, J in enumerate(FF_PARTS):
                    with dve.Fori(0, J // 2) as i:
                        for k in range(2):
                            nn, uu = Lin(n.c + 2 * k, 4, i), Lin(u.c + 2 * k, 4, i)
                            j = Lin(j0 + k, 2, i)
                            split(nn + 2)
                            dve.wait_ge(S("silu"), count("silu", j))
                            scaled(fa[:, k, :], uu)
                            split(nn + 3)
                            scaled(fb[:, k, :], uu + 1)
                            dve.wait_ge(S("silu"), count("silu", j + 1))
                            dve.wait_ge(S(f"taken{(uu + 1).mod(2)}"), count(f"taken{(uu + 1).mod(2)}", (uu + 1).div(2) + 1))
                            dve.wait_ge(S("hid_low"), count("hid_low", j))
                            nc.vector.tensor_tensor(ff[:, k, :], fs[:, k, :], fb[:, k, :], ALU.mult)\
                                .then_inc(S("gated"), 1)
                    n, u, j0 = n + 2 * J, u + 2 * J, j0 + J
                    for m in range(NB):
                        split(n + (m + 2))
                        add_to_x(m, u + m, 0.5)
                        if part == 2 and m:
                            norm_low(norm + 1, m - 1)
                    n, u = n + NB, u + NB
                norm_low(norm + 1, NB - 1)
            elif ph_["kind"] == "ab":
                dve.wait_ge(S("masks_in"), count("masks_in", 16))
                dve.wait_ge(S("ident_in"), count("ident_in", 16))
                with dve.Fori(0, H) as i:
                    gated_group(1, Lin(n.c, 4, i), Lin(u.c, 4, i), i, None)
                n, u = n + 4 * H, u + 4 * H
                split(n + 2)
                dve.wait_ge(S("unit"), count("unit", u + 1))
                dve.wait_ge(S("omixl"), count("omixl", H))
                nc.vector.tensor_tensor(two(lr[0:16, :]), ps[0:16, 2 * u.mod(2):2 * u.mod(2) + 2, 0:TH],
                                        two(rinv[0:16, :]), ALU.mult).then_inc(S(f"taken{u.mod(2)}"), 1)
                dve.wait_ge(S("gkz"), count("gkz", 1))
                for p in range(2):
                    if p:
                        dve.wait_ge(S("decay"), count("decay", 1))
                    nc.vector.tensor_scalar(two(z1[:, :]), ps[:, 4 + 2 * p:6 + 2 * p, 0:TH], bgk[:, p:p + 1], None,
                                            ALU.add).then_inc(S("gkz_out"), 1)
                    dve.wait_ge(S("gk_ln"), count("gk_ln", 3 * p + 3))
                    nc.vector.scalar_tensor_tensor(out=z1[:, :], in0=z1[:, :], scalar=0.0, in1=s1[:, :],
                                                   op0=ALU.min, op1=ALU.subtract).then_inc(S("gk_min"), 1)
                n, u = n + 1, u + 1
                for p in range(2):
                    gated_group(2, n, u, None, p)
                    n, u = n + N_GLA, u + N_GLA
                for m in range(NB):
                    split(n + (m + 2))
                    add_to_x(m, u + m, 1.0)
                    if m:
                        norm_low(norm + 1, m - 1)
                norm_low(norm + 1, NB - 1)
            elif ph_["kind"] == "ret":
                dve.wait_ge(S("rope_in"), count("rope_in", 32))
                queries_keys(n, u, lambda k, per: Lin(k))
                with dve.Fori(0, H - 1) as i:
                    retention_head(Lin(n.c + 4, N_RET, i), Lin(u.c + 4, 12 + NB, i), i, False)
                n, u = n + (4 + (H - 1) * N_RET), u + (4 + (H - 1) * (12 + NB))
                retention_head(n, u, H - 1, True)
                for m in range(NB):
                    if m % 2 == 1:
                        split(n + (10 + m // 2))
                    add_to_x(m, u + (8 + m), 1.0)
                    if m:
                        norm_low(norm + 1, m - 1)
                norm_low(norm + 1, NB - 1)
            else:
                lay = ph_["layer"]
                for k in range(2):
                    dve.wait_ge(S("p_high"), count("p_high", 2 * lay + k + 1))
                    nc.vector.tensor_tensor(pl[:, k, :], praw[:, k, :], ph[:, k, :], ALU.subtract)\
                        .then_inc(S("p_low"), 1)
                for m in range(NB):
                    split(n + (m + 2))
                    if m >= 2:
                        dve.wait_ge(S("pgate"), count("pgate", NB * lay + m - 1))
                    scaled(pz[:, m % 2, :], u + m)
                n, u = n + NB, u + NB
                dve.wait_ge(S("pgate"), count("pgate", NB * (lay + 1)))
                for m in range(NB):
                    if m % 4 == 3:
                        split(n + (m // 4 + 2))
                    dve.wait_ge(S("unit"), count("unit", u + (m + 1)))
                    if m >= 2:
                        dve.wait_ge(S("p_added"), count("p_added", NB * lay + m - 1))
                    nc.vector.tensor_tensor(two(pt[:, m % 2, :]), pair_of(u + m), two(pg[:, m, :]), ALU.mult)\
                        .then_inc(S(f"taken{(u + m).mod(2)}"), 1)
                    dve.wait_ge(S(f"taken{(u + m).mod(2)}"), count(f"taken{(u + m).mod(2)}", (u + m).div(2) + 1))
                    nc.vector.tensor_tensor(x[:, m, :], x[:, m, :], pt[:, m % 2, :], ALU.add).then_inc(S("p_added"), 1)
                    if m:
                        norm_low(norm + 1, m - 1)
                norm_low(norm + 1, NB - 1)
        norm_inverse(8)
        for m in range(NB):
            dve.wait_ge(S("sq"), count("sq", NB * 8 + m + 1))
            nc.vector.scalar_tensor_tensor(out=x[:, m, :], in0=x[:, m, :], scalar=gains[:, 8, m:m + 1],
                                           in1=rinv[:, :], op0=ALU.mult, op1=ALU.mult).then_inc(S("y_ready"), 1)

    @block.gpsimd
    def _(pool):
        def norm_total(norm):
            for m in range(1, NB):
                pool.wait_ge(S("sq"), count("sq", NB * norm + m + 1))
                if m == 1:
                    if norm:
                        pool.wait_ge(S("norm_sum"), count("norm_sum", norm))
                    nc.gpsimd.tensor_tensor(sqsum[:, :], sq[:, 0, :], sq[:, 1, :], ALU.add).then_inc(S("sqsum"), 1)
                else:
                    pool.wait_ge(S("sqsum"), count("sqsum", 7 * norm + m - 1))
                    nc.gpsimd.tensor_tensor(sqsum[:, :], sqsum[:, :], sq[:, m % 2, :], ALU.add)\
                        .then_inc(S("sqsum"), 1)

        def gated_group(ns, u, i, pair):
            G = lambda name, k: group_count(name, ns, i, pair, k)
            U = gU[:, :] if ns == 1 else decay[:, pair, :]
            reached = early(pool, count("turned_out", G("turned_out", 0)))
            pool.wait_ge(S("ones"), 1)
            pool.wait_ge(S("turned_out"), reached)
            pool.wait_ge(S("o_done"), count("o_done", G("o_done", 0)))
            if ns == 1:
                pool.dma_start(S0[:, :, :], d["s_hgrn"][i]).then_inc(S("S0_in"), 16)
            else:
                pool.dma_start(S0[:, :, :], d["s_gla"][pair]).then_inc(S("S0_in"), 16)
            reached = early(pool, count("kl", G("kl", 0)))
            pool.wait_ge(S("ones"), 1)
            pool.wait_ge(S("kl"), reached)
            nc.gpsimd.memset(gL[:, :], 1.0).then_inc(S("l_up"), 1)
            ready_k(pool, ns, u, i)
            if ns == 2:
                pool.wait_ge(S("decay"), count("decay", 2))
            for lev in range(1, NLEV + 1):
                h = 1 << (lev - 1)
                R = T if h <= 4 else TP
                pool.wait_ge(S("l_up"), count("l_up", G("l_up", lev)))
                if lev > 1:
                    if lev > 3:
                        pool.wait_ge(S("scores"), count("scores", G("scores", (lev - 1) * ns)))
                    elif lev == 2:
                        pool.wait_ge(S("turned_out"), count("turned_out", G("turned_out", 0)))
                    nc.gpsimd.tensor_tensor(kl[:, lev % 2, 0:R], gk[:, 0:R], gL[:, 0:R], ALU.mult).then_inc(S("kl"), 1)
                    pool.wait_ge(S("kl"), count("kl", G("kl", lev - 1)))
                    pool.wait_ge(S("u_up"), count("u_up", G("u_up", lev - 1)))
                lv = gL[:, 0:R].rearrange("p (b a h) -> p b a h", a=2, h=h)
                uv = U[:, 0:R].rearrange("p (b a h) -> p b a h", a=2, h=h)
                nc.gpsimd.tensor_tensor(lv[:, :, 0, :], lv[:, :, 0, :],
                                        uv[:, :, 1, h - 1:h].broadcast_to([P, R // (2 * h), h]), ALU.mult)\
                    .then_inc(S("l_up"), 1)
                if lev == 4:
                    for s in range(ns):
                        pool.wait_ge(S("turned_out"), count("turned_out", G("turned_out", 2 * s + 2)))
                        nc.gpsimd.tensor_tensor(
                            vm[0:TS, s, :, :], vt[0:TS, s, CH, :].unsqueeze(1).broadcast_to([TS, NBAT, P]),
                            batch_of[0:TS, :].unsqueeze(2).broadcast_to([TS, NBAT, P]), ALU.mult)\
                            .then_inc(S("vm"), 1)
            pool.wait_ge(S("l_up"), count("l_up", G("l_up", 8)))
            pool.wait_ge(S("scores"), count("scores", G("scores", 7 * ns)))
            nc.gpsimd.tensor_tensor(kl[:, 0, :], gk[:, :], gL[:, :], ALU.mult).then_inc(S("kl"), 1)
            reached = early(pool, count("turned_out", G("turned_out", 2 * ns + 3)))
            pool.wait_ge(S("ones"), 1)
            pool.wait_ge(S("turned_out"), reached)
            dst = out["hgrn_p"][i] if ns == 1 else out["gla_p"][pair]
            pool.dma_start(dst, St[:, CH - 1, :]).then_inc(S("S_out"), 16)
            reached = early(pool, count("turned_out", G("turned_out", 2 * ns + 4)))
            pool.wait_ge(S("ones"), 1)
            pool.wait_ge(S("turned_out"), reached)
            dst = out["hgrn_s"][i] if ns == 1 else out["gla_s"][pair]
            pool.dma_start(dst, Sn[:, :, :]).then_inc(S("S_out"), 16)
            for s in range(ns):
                pool.wait_ge(S("omixh"), count("omixh", G("omixh", s + 1)))
                if ns == 1:
                    hi, lo = hid[0][:, i, :], hid[1][:, i, :]
                else:
                    hi, lo = hid[0][:, 4 + 2 * pair + s, :], hid[1][:, 4 + 2 * pair + s, :]
                nc.gpsimd.tensor_tensor(lo, z1[:, :], hi, ALU.subtract).then_inc(S("omixl"), 1)
            pool.wait_ge(S("S_out"), count("S_out", G("S_out", 32)))

        def load_tables(h):
            pool.dma_start(ctab[:, :], d["ctab"][h]).then_inc(S("ctab_in"), 16)

        def rotate(u, R, dst, k, a, done):
            for c in (k - 1, k):
                pool.wait_ge(S(f"taken{(u + c).mod(2)}"), count(f"taken{(u + c).mod(2)}", (u + c).div(2) + 1))
            nc.gpsimd.tensor_tensor(dst[:, 1, :], rz[:, 1, :], cosT[:, :], ALU.mult)
            nc.gpsimd.tensor_tensor(rtp[:, :], rz[:, 0, :], sinT[:, :], ALU.mult).then_inc(S("rot_b"), 1)
            pool.wait_ge(S("rot_b"), count("rot_b", R(a, 2)))
            nc.gpsimd.tensor_tensor(dst[:, 1, :], dst[:, 1, :], rtp[:, :], ALU.add).then_inc(S(done), 1)

        def retention_head(u, i, last_head):
            R = lambda k, per: Lin(k, per, i)
            pool.wait_ge(S("ctab_in"), count("ctab_in", R(16, 16)))
            pool.wait_ge(S("rot_q0"), count("rot_q0", R(1, 1)))
            pool.wait_ge(S("rot_q1"), count("rot_q1", R(1, 1)))
            nc.gpsimd.tensor_tensor(qd[:, :, :], rq[:, :, TP:T], qdec.unsqueeze(1).broadcast_to([P, 2, TS]), ALU.mult)\
                .then_inc(S("qd"), 1)
            pool.wait_ge(S("rturned_out"), count("rturned_out", R(2, 6)))
            pool.wait_ge(S("rot_k0"), count("rot_k0", R(1, 1)))
            pool.wait_ge(S("rot_k1"), count("rot_k1", R(1, 1)))
            nc.gpsimd.tensor_tensor(kdm[0:TS, :, :], kd[0:TS, CH, :].unsqueeze(1).broadcast_to([TS, NBAT, 2 * P]),
                                    batch_of[0:TS, :].unsqueeze(2).broadcast_to([TS, NBAT, 2 * P]), ALU.mult)\
                .then_inc(S("kdm"), 1)

            def reload(b):
                reached = early(pool, count(f"rS_out{b % 4}", Lin(16 * (b // 4 + 1), 32, i)))
                pool.wait_ge(S("ones"), 1)
                pool.wait_ge(S(f"rS_out{b % 4}"), reached)
                pool.dma_start(rS0[:, b % 4, :, :], d["s_ret"][(Lin(b + 4, NBAT, i)).value()])\
                    .then_inc(S(f"rS0_in{b % 4}"), 16)

            def store_prompt():
                reached = early(pool, count("rstate_out", R(2, 2)))
                pool.wait_ge(S("ones"), 1)
                pool.wait_ge(S("rstate_out"), reached)
                pool.dma_start(out["ret_p"][i], rSt[:, :, :]).then_inc(S("rSt_stored"), 16)

            for b in range(NBAT):
                reached = early(pool, count("rnew", R(2 * b + 2, 16)))
                pool.wait_ge(S("ones"), 1)
                pool.wait_ge(S("rnew"), reached)
                pool.dma_start(out["ret_s"][Lin(b, NBAT, i).value()], rS0[:, b % 4, :, :])\
                    .then_inc(S(f"rS_out{b % 4}"), 16)
                if b:
                    reload(b - 1)
                if b == 3:
                    store_prompt()
            if not last_head:
                load_tables(i + 1)
            reload(NBAT - 1)
            for vb in range(1, 4):
                pool.wait_ge(S("rsq"), count("rsq", R(vb + 1, 4)))
                if vb == 1:
                    nc.gpsimd.tensor_tensor(rsum, sq[:, 0, :], sq[:, 1, :], ALU.add).then_inc(S("rsqsum"), 1)
                else:
                    pool.wait_ge(S("rsqsum"), count("rsqsum", R(vb - 1, 3)))
                    nc.gpsimd.tensor_tensor(rsum, rsum, sq[:, vb % 2, :], ALU.add).then_inc(S("rsqsum"), 1)
            if not last_head:
                rotate(u + 8, lambda k, per: R(k + per, per), rq, 1, 1, "rot_q1")
            for vb in range(4):
                pool.wait_ge(S("rmixh"), count("rmixh", R(vb + 1, 4)))
                nc.gpsimd.tensor_tensor(hid[1][:, vb, :], ro[:, vb, :], hid[0][:, vb, :], ALU.subtract)\
                    .then_inc(S("rmixl"), 1)
            if not last_head:
                rotate(u + 8, lambda k, per: R(k + per, per), rk, 3, 2, "rot_k1")
            pool.wait_ge(S("rSt_stored"), count("rSt_stored", R(16, 16)))

        nc.gpsimd.memset(ones[:, :], 1.0).then_inc(S("ones"), 1)
        for ph_ in phases:
            norm = ph_["norm"]
            if ph_["kind"] == "ffn":
                j0 = ph_["j"]
                for J in FF_PARTS:
                    with pool.Fori(0, J // 2) as i:
                        for k in range(2):
                            pool.wait_ge(S("hid_high"), count("hid_high", Lin(j0 + k + 1, 2, i)))
                            nc.gpsimd.tensor_tensor(hid[1][:, i * 2 + k, :], ff[:, k, :], hid[0][:, i * 2 + k, :], ALU.subtract)\
                                .then_inc(S("hid_low"), 1)
                    j0 += J
            elif ph_["kind"] == "ab":
                pool.wait_ge(S("hid_low"), count("hid_low", ph_["j"]))
                pool.wait_ge(S("norm_sum"), count("norm_sum", norm + 1))
                pool.dma_start(masks[:, :, :], d["masks"]).then_inc(S("masks_in"), 16)
                pool.dma_start(gk2, d["gk2"]).then_inc(S("gk2_in"), 16)
                pool.wait_ge(S("small_in"), count("small_in", 32))
                u0 = ph_["u"]
                with pool.Fori(0, H) as i:
                    gated_group(1, Lin(u0, 4, i), i, None)
                for p in range(2):
                    gated_group(2, Lin(u0 + 4 * H + 1 + N_GLA * p), None, p)
            elif ph_["kind"] == "ret":
                pool.wait_ge(S("hid_low"), count("hid_low", ph_["j"]))
                pool.dma_start(cosT[:, :], d["cosT"]).then_inc(S("rope_in"), 16)
                pool.dma_start(sinT[:, :], d["sinT"]).then_inc(S("rope_in"), 16)
                for b in range(4):
                    pool.dma_start(rS0[:, b, :, :], d["s_ret"][b]).then_inc(S(f"rS0_in{b}"), 16)
                pool.wait_ge(S("rope_in"), count("rope_in", 32))
                load_tables(0)
                u0 = Lin(ph_["u"])
                rotate(u0, lambda k, per: Lin(k), rq, 1, 1, "rot_q1")
                rotate(u0, lambda k, per: Lin(k), rk, 3, 2, "rot_k1")
                with pool.Fori(0, H - 1) as i:
                    retention_head(Lin(ph_["u"] + 4, 12 + NB, i), i, False)
                retention_head(u0 + (4 + (H - 1) * (12 + NB)), H - 1, True)
                for b in range(4):
                    pool.wait_ge(S(f"rS0_in{b}"), count(f"rS0_in{b}", 16 * (2 * H + 1)))
                    pool.wait_ge(S(f"rS_out{b}"), count(f"rS_out{b}", 32 * H))
            else:
                pool.wait_ge(S("hid_low"), count("hid_low", ph_["j"]))
                pool.dma_start(praw[:, :, :], d["pT"][ph_["layer"]]).then_inc(S("praw_in"), 16)
            norm_total(norm + 1)

    block_cm.__exit__(None, None, None)


def _tiles(w, k0, k1, c0):
    return w[k0 * P:k1 * P, c0:c0 + P].reshape(k1 - k0, P, P).transpose(1, 0, 2).reshape(P, -1)


def _weight_stream(a):
    w = np.zeros((N_PIECES, P, D), np.float32)
    n = 0

    def put(*parts):
        nonlocal n
        c = 0
        for t in parts:
            w[n, :, c:c + t.shape[1]] = t
            c += t.shape[1]
        n += 1

    def ffn(w_in, w_out):
        k = 0
        for J in FF_PARTS:
            for j in range(k, k + J):
                put(_tiles(w_in, 0, NB, j * P))
                put(_tiles(w_in, 0, NB, DFF + j * P))
            for m in range(NB):
                put(_tiles(w_out, k, k + J, m * P))
            k += J

    for layer in range(2):
        ffn(a["ffn1_w_in"][layer], a["ffn1_w_out"][layer])
        if layer == 0:
            w_in, w_out = a["ab_w_in"][0], a["ab_w_out"][0]
            for h in range(H):
                for c in (512, 0, 1024, 1536):
                    put(_tiles(w_in, 0, NB, c + h * P))
            put(_tiles(w_in, 0, NB, 3072))
            for p in range(2):
                for c in (2304 + p * P, 2048 + p * P, 2560 + 2 * p * P, 2688 + 2 * p * P,
                          3088 + 2 * p * P, 3216 + 2 * p * P):
                    put(_tiles(w_in, 0, NB, c))
            for m in range(NB):
                put(_tiles(w_out, 0, NB, m * P))
        else:
            w_in, w_out = a["ret_w_in"][0], a["ret_w_out"][0]
            def project(h, *parts):
                for base, per in parts:
                    for k in range(per):
                        put(_tiles(w_in, 0, NB, base + (h * per + k) * P))

            project(0, (0, 2), (1024, 2))
            for h in range(H):
                project(h, (2048, 4), (4096, 4))
                if h < H - 1:
                    project(h + 1, (0, 2), (1024, 2))
                for m in range(0, NB, 2):
                    put(_tiles(w_out, 4 * h, 4 * h + 4, m * P), _tiles(w_out, 4 * h, 4 * h + 4, (m + 1) * P))
        ffn(a["ffn2_w_in"][layer], a["ffn2_w_out"][layer])
        for m in range(NB):
            put(_tiles(a["ple_w_gate"][layer], 0, NB, m * P))
        for m in range(0, NB, 4):
            put(*(_tiles(a["ple_w_proj"][layer], 0, 2, (m + k) * P) for k in range(4)))
    assert n == N_PIECES
    return w


def _columns(v):
    return v.reshape(-1, P).T


def _feature_major(prompt, sample, width):
    both = np.concatenate([prompt.reshape(TP, width), sample.reshape(TS, width)], 0)
    return np.ascontiguousarray(both.T).reshape(width // P, P, T)


def _constants():
    s, t = np.arange(P)[:, None], np.arange(P)[None, :]
    masks = np.zeros((P, NLEV, P), np.int32)
    for lev in range(NLEV):
        h = 1 << lev
        masks[:, lev] = (s // (2 * h) == t // (2 * h)) & (s // h % 2 == 0) & (t // h % 2 == 1)
    half = P
    inv = np.float32(10000.0) ** (-np.arange(half, dtype=np.float32) / np.float32(half))
    pos = np.concatenate([np.arange(TP), PAST + np.tile(np.arange(LS), NBAT)]).astype(np.float32)
    ang = (inv[:, None] * pos[None, :]).astype(np.float32).astype(np.float64)
    ctab = np.zeros((H, P, CT), np.float32)
    for h in range(H):
        lg = np.log1p(-np.exp2(-5.0 - h))
        r = np.arange(TP)[None, :] - np.arange(P)[:, None]
        ctab[h, :, 0:TP] = np.where(r >= 0, np.exp(lg * np.maximum(r, 0)) / 16, 0)
        s, t = np.arange(TS)[:, None], np.arange(TS)[None, :]
        ctab[h, 0:TS, TP:TP + TS] = np.where((s // LS == t // LS) & (t >= s), np.exp(lg * (t - s)) / 16, 0)
        ctab[h, :, TP + TS:TP + 2 * TS] = np.exp(lg * (np.arange(TS) % LS + 1))[None, :]
        o = TP + 2 * TS
        for c in range(CH):
            ctab[h, :, o + c] = np.exp(lg * (TP - 1 - (c * P + np.arange(P)))) / 16
        ctab[h, 0:TS, o + CH] = np.exp(lg * (LS - 1 - np.arange(TS) % LS)) / 16
        ctab[h, :, o + CH + 1] = np.exp(lg * LS)
    return {"masks": masks, "cosT": np.cos(ang).astype(np.float32), "sinT": np.sin(ang).astype(np.float32),
            "ctab": ctab, "ident": np.eye(P, dtype=np.float32)}


def kernel(**inputs):
    from concourse import bacc
    from concourse.bass_utils import run_bass_kernel_spmd

    a = {k: np.asarray(v) for k, v in inputs.items()}
    gains = np.zeros((P, 9, NB), np.float32)
    for layer in range(2):
        for k, name in enumerate(NORMS):
            gains[:, 4 * layer + k] = _columns(a[name][layer])
    gains[:, 8] = _columns(a["norm_final"])
    small = np.zeros((P, 24), np.float32)
    small[:, 0:1] = _columns(a["ab_gn_hgrn"][0])
    small[:, 1:2] = _columns(a["ab_gn_gla"][0])
    small[:, 2:6] = _columns(a["ret_gn"][0])
    small[:, 6:8] = _columns(a["ab_b_gk"][0])
    small[:, 8:12] = _columns(a["hgrn_lb_logits"][0])
    small[:, 12:16] = _columns(a["hgrn_lb_logits"][1])
    small[0:TS, 16:24] = np.arange(TS)[:, None] // LS == np.arange(NBAT)[None, :]
    s_ret = np.zeros((H * NBAT + 4, P, 2, 4 * P), np.float32)
    s_ret[:H * NBAT] = a["state_ret"][0].transpose(1, 0, 2, 3).reshape(H * NBAT, 2, P, 4 * P).transpose(0, 2, 1, 3)
    s_gla = a["state_gla"][0].reshape(NBAT, 2, 2, 64, P).transpose(1, 2, 3, 0, 4).reshape(2, P, NBAT, P)
    arrays = {
        "w": _weight_stream(a),
        "xT": _feature_major(a["x_prompt"], a["x_sample"], D),
        "pT": np.stack([_feature_major(a["p_prompt"][k], a["p_sample"][k], 2 * P).transpose(1, 0, 2) for k in range(2)]),
        "s_hgrn": a["state_hgrn"][0].transpose(1, 2, 0, 3), "s_gla": s_gla, "s_ret": s_ret,
        "gains": gains, "small": small, "gk2": a["ab_w_gk2"][0], **_constants(),
    }
    arrays = {k: np.ascontiguousarray(v) for k, v in arrays.items()}
    nc = bacc.Bacc("TRN2", target_bir_lowering=False, num_devices=1)
    d = {k: nc.dram_tensor(f"in_{k}", v.shape, mybir.dt.from_np(v.dtype), kind="ExternalInput").ap()
         for k, v in arrays.items()}
    shapes = {"yT": (NB, P, T), "hgrn_p": (H, P, P), "gla_p": (2, P, P), "ret_p": (H, P, 2, 4 * P),
              "hgrn_s": (H, P, NBAT, P), "gla_s": (2, P, NBAT, P), "ret_s": (H * NBAT, P, 2, 4 * P)}
    out = {k: nc.dram_tensor(f"out_{k}", v, F32, kind="ExternalOutput").ap() for k, v in shapes.items()}
    build(nc, d, out)
    r = run_bass_kernel_spmd(nc, [{f"in_{k}": v for k, v in arrays.items()}], core_ids=[0]).results[0]
    r = {k: np.asarray(r[f"out_{k}"]) for k in shapes}
    y = r["yT"].reshape(D, T).T
    c = np.ascontiguousarray
    return (c(y[:TP]).reshape(1, TP, D), c(y[TP:]).reshape(NBAT, LS, D),
            r["hgrn_p"].reshape(1, 1, H, P, P), r["gla_p"].reshape(1, 1, H, 64, P),
            c(r["ret_p"].transpose(0, 2, 1, 3)).reshape(1, 1, H, 2 * P, 4 * P),
            c(r["hgrn_s"].transpose(2, 0, 1, 3)).reshape(1, NBAT, H, P, P),
            c(r["gla_s"].reshape(2, 2, 64, NBAT, P).transpose(3, 0, 1, 2, 4)).reshape(1, NBAT, H, 64, P),
            c(r["ret_s"].reshape(H, NBAT, P, 2, 4 * P).transpose(1, 0, 3, 2, 4)).reshape(1, NBAT, H, 2 * P, 4 * P))
```

```python
import numpy as np
import concourse.bass as bass
import concourse.mybir as mybir

F32 = mybir.dt.float32
F32R = mybir.dt.float32r
I32 = mybir.dt.int32
ALU = mybir.AluOpType
ACT = mybir.ActivationFunctionType

P = 128
D = 1024
NB = D // P
TP, TS = 512, 64
T = TP + TS
TH = T // 2
NBAT, LS = 8, 8
DFF = 2816
FF_PARTS = (8, 8, 6)
H = 4
CH = TP // P
NRAW = 4
NLEV = 7
EPS = 1e-6
PAST = 4096
CT = TP + TS + TS + CH + 1 + 1
NORMS = ("norm_ffn1", "norm_mix", "norm_ffn2", "norm_ple")

N_FFN = sum(2 * j + NB for j in FF_PARTS)
N_HGRN, N_GLA, N_RET = 4, 6, 16
N_PIECES = 4 * N_FFN + H * N_HGRN + 1 + 2 * N_GLA + NB + H * N_RET + 2 * (NB + 2)


def early(eng, n):
    return n if isinstance(n, int) else eng.to_reg(n)


class Lin:

    def __init__(self, c, k=0, i=None, start=0):
        if i is None or isinstance(i, int):
            c, k = c + k * (i or 0), 0
        self.c, self.k, self.i, self.start = c, k, i, start

    def __add__(self, n):
        return Lin(self.c + n, self.k, self.i, self.start)

    def div(self, d):
        assert self.k % d == 0
        return Lin(self.c // d, self.k // d, self.i, self.start)

    def mod(self, d):
        assert self.k % d == 0
        return self.c % d

    def lowest(self):
        return self.c + self.k * self.start

    def value(self):
        return self.c if not self.k else self.i * self.k + self.c


FROM_ONE = ("taken0", "taken1", "o_done", "oss", "orms", "ot", "omixl", "kl", "turned_out", "gated", "silu",
            "hid_low", "rkv", "rmix", "rnew", "ratt", "rturned_out")


def count(name, n):
    n = n if isinstance(n, Lin) else Lin(n)
    assert n.lowest() >= 0 and (not n.k or n.lowest() > 0 or name in FROM_ONE), name
    return (n + 1 if name in FROM_ONE else n).value()


def two(ap):
    return ap.rearrange("p (a b) -> p a b", a=2)


def build(nc, d, out):
    at = [16512]

    def sb(name, cols, dt=F32, where=None):
        n = int(np.prod(cols)) * 4
        if where is None:
            where = at[0]
            at[0] = (where + n + 31) // 32 * 32
        return nc.alloc_sbuf_tensor_at(name, [P] + list(cols), dt, offset=where)

    x = sb("x", [NB, T])
    xh = sb("xh", [NB, T], F32R)
    xl = sb("xl", [NB, T], F32R)
    raw = sb("raw", [NRAW, D])
    wh = sb("wh", [2, D], F32R)
    wl = sb("wl", [2, D], F32R)
    rinv = sb("rinv", [T])
    rms = sb("rms", [T])
    sq = sb("sq", [2, T])
    sqsum = sb("sqsum", [T])
    gains = sb("gains", [9, NB])
    ident = sb("ident", [P])
    ones = sb("ones", [P])
    small = sb("small", [64])
    gnormA = small[:, 0:1]
    gnormB = small[:, 1:2]
    gnormR = small[:, 2:6]
    bgk = small[:, 6:8]
    logits = small[:, 8:16]
    batch_of = small[:, 16:24]
    lbmax, lbe, lbs = small[:, 24:28], small[:, 28:36], small[:, 36:40]
    bounds = sb("bounds", [2, H, 1])
    lb, one_lb = bounds[:, 0, :, 0], bounds[:, 1, :, 0]
    eps = small[:, 48:49]
    spare = at[0] + 4 * T * 4
    hid = [sb("hid_high", [8, T], F32R), sb("hid_low", [8, T], F32R)]
    free = at[0]

    fa = sb("ff_a", [2, T])
    fs = sb("ff_silu", [2, T])
    fb = sb("ff_b", [2, T])
    ff = sb("ff_gated", [2, T])
    at[0] = free
    praw = sb("praw", [2, T])
    ph = sb("ph", [2, T], F32R)
    pl = sb("pl", [2, T], F32R)
    pz = sb("pz", [2, T])
    pg = sb("pgate", [NB, T])
    pt = sb("ptmp", [2, T])
    at[0] = free
    z1 = sb("z1", [T])
    s1 = sb("s1", [T])
    s2 = sb("s2", [T])
    gk = sb("gk", [T])
    gU = sb("gU", [T])
    gL = sb("gL", [T])
    gq = sb("gq", [T])
    qu = sb("qu", [2, T])
    kl = sb("kl", [2, T])
    gate = sb("gate", [2, T])
    vf = sb("vf", [T])
    go = sb("go", [T])
    decay = sb("decay", [2, T])
    vt = sb("vt", [2, CH + 1, P])
    att = sb("att", [2, T])
    klt = sb("klt", [CH + 1, P])
    St = sb("St", [CH, P])
    S0 = sb("S0", [NBAT, P])
    Sn = sb("Sn", [NBAT, P])
    vm = sb("vm", [2, NBAT, P])
    masks = sb("masks", [NLEV, P], I32)
    lr = go
    gkz = [z1[:, :], go[:, :]]
    kz, qz = rms, sqsum
    hout = [go[:, :], qz[:, :]]
    hsq = [sq[:, 1, :], kz[:, :]]
    gk2 = sq[0:16, 0, 0:2 * P]
    at[0] = free
    rz = sb("rz", [2, T])
    rtd = sb("rtd", [T])
    rtp = sb("rtp", [T])
    kdm = sb("kdm", [NBAT, 2 * P], where=free)
    rq = sb("rq", [2, T])
    rk = sb("rk", [2, T])
    rv = sb("rv", [2, T])
    rvt = sb("rvt", [CH + 1, 4 * P])
    kd = sb("kd", [CH + 1, 2 * P])
    ratt = sb("ratt", [1280])
    ratts = sb("ratts", [TS])
    qd = sb("qd", [2, TS])
    rS0 = sb("rS0", [4, 2, 4 * P])
    rSt = sb("rSt", [2, 4 * P])
    ctab = sb("ctab", [CT])
    cosT = sb("cosT", [T])
    sinT = sb("sinT", [T])
    ro = sb("ro", [4, T], where=spare)
    rg = sb("rg", [4, T], where=spare + 8 * T * 4)
    Dm = ctab[:, 0:TP]
    Ds = ctab[0:TS, TP:TP + TS]
    qdec = ctab[:, TP + TS:TP + 2 * TS]
    kdec = ctab[:, TP + 2 * TS:TP + 2 * TS + CH]
    kdecs = ctab[0:TS, TP + 2 * TS + CH:TP + 2 * TS + CH + 1]
    gam = ctab[:, TP + 2 * TS + CH + 1:CT]
    rr = rms[:, :]
    rsum = sqsum[:, :]
    RAT = [0, 512, 896, 1152]

    ps = nc.alloc_psum_tensor("ps", [P, 8, 512], F32)

    sems = {}

    def S(name):
        if name not in sems:
            sems[name] = nc.alloc_semaphore(name)
        return sems[name]

    for name in FROM_ONE:
        nc.sync.sem_inc(S(name), 1)
    block_cm = nc.Block()
    block = block_cm.__enter__()

    phases, n, u, g, norm, ffj, ffu = [], 0, 0, 0, 0, 0, 0
    for layer in range(2):
        for kind in ("ffn", "ab" if layer == 0 else "ret", "ffn", "ple"):
            phases.append(dict(kind=kind, layer=layer, n=n, u=u, norm=norm, j=ffj))
            if kind == "ffn":
                n, u, ffj = n + N_FFN, u + N_FFN, ffj + sum(FF_PARTS)
            elif kind == "ab":
                m = H * N_HGRN + 1 + 2 * N_GLA + NB
                n, u = n + m, u + m
            elif kind == "ret":
                n, u = n + H * N_RET, u + H * (12 + NB)
            else:
                n, u = n + NB + 2, u + 2 * NB
            norm += 1
    assert n == N_PIECES

    def per_group(name, ns):
        return {"sig": 4 if ns == 1 else 2, "scores": 8 * ns, "picked": 8 * ns, "qu": 8, "kl": 7, "u_up": 7,
                "l_up": 8, "turned": 2 * ns + 4, "turned_out": 2 * ns + 4, "s_step": 3, "S0_in": 16, "S_out": 32,
                "s_new": 1, "orr": 4}.get(name, ns)

    def ready_k(eng, ns, u, i):
        u = u + -2
        if ns == 1:
            eng.wait_ge(S("k_ready"), count("k_ready", Lin(1, 1, i, 1)))
        else:
            eng.wait_ge(S(f"taken{u.mod(2)}"), count(f"taken{u.mod(2)}", u.div(2) + 1))

    def ready_q(eng, ns, u, i):
        u = u + -2
        if ns == 1:
            eng.wait_ge(S("q_ready"), count("q_ready", Lin(1, 1, i, 1)))
        else:
            eng.wait_ge(S(f"taken{(u + 1).mod(2)}"), count(f"taken{(u + 1).mod(2)}", (u + 1).div(2) + 1))

    def group_count(name, ns, i, pair, k):
        if ns == 1:
            return Lin(k, per_group(name, 1), i, 1)
        assert name not in ("k_ready", "q_ready")
        return Lin(H * per_group(name, 1) + pair * per_group(name, 2) + k)

    @block.sync
    def _(sp):
        for m in range(NB):
            sp.dma_start(x[:, m, :], d["xT"][m]).then_inc(S(f"x_in{m}"), 16)
            if m == 0:
                sp.dma_start(gains[:, :, :], d["gains"]).then_inc(S("small_in"), 16)
                sp.dma_start(small[:, 0:24], d["small"][:, 0:24]).then_inc(S("small_in"), 16)
            if m < 2:
                sp.dma_start(raw[:, m, :], d["w"][m]).then_inc(S(f"landed{m}"), 16)
        for m in (2, 3):
            sp.dma_start(raw[:, m, :], d["w"][m]).then_inc(S(f"landed{m}"), 16)
        sp.dma_start(ident[:, :], d["ident"]).then_inc(S("ident_in"), 16)

        def piece(k, i):
            n = Lin(NRAW + k, NRAW, i)
            sp.wait_ge(S("lo_made"), count("lo_made", n + (1 - NRAW)))
            sp.dma_start(raw[:, k % NRAW, :], d["w"][n.value()]).then_inc(S(f"landed{k % NRAW}"), 16)

        rounds = (N_PIECES - NRAW) // NRAW
        with sp.Fori(0, rounds) as i:
            for k in range(NRAW):
                piece(k, i)
        for k in range(rounds * NRAW, N_PIECES - NRAW):
            piece(k, None)
        for m in range(NB):
            sp.wait_ge(S("y_ready"), count("y_ready", m + 1))
            sp.dma_start(out["yT"][m], x[:, m, :]).then_inc(S("y_out"), 16)
        sp.wait_ge(S("y_out"), count("y_out", 16 * NB))

    @block.tensor
    def _(pe):
        def product(bank_pair, w0, rhs, K, first_piece_col=0):
            last = None
            for k in range(K):
                w = slice((w0 + k) * P, (w0 + k + 1) * P)
                for j, (wt, r) in enumerate(((wh, 0), (wh, 1), (wl, 0))):
                    for a in range(2):
                        last = nc.tensor.matmul(
                            ps[:, 2 * bank_pair + a, 0:TH], lhsT=wt[:, first_piece_col, w],
                            rhs=rhs(r, k)[:, a * TH:(a + 1) * TH],
                            start=(k == 0 and j == 0), stop=(k == K - 1 and j == 2))
            return last

        def unit(n, u, rhs, K, w0=0, before=None, between=None, ks=None):
            pe.wait_ge(S("lo_made"), count("lo_made", n + 1))
            s = u.mod(2)
            pe.wait_ge(S(f"taken{s}"), count(f"taken{s}", u.div(2)))
            slot = n.mod(2)
            if before is None and between is None:
                product(s, w0, rhs, K, slot).then_inc(S("unit"), 1)
                return
            for k in ks or range(K):
                if before is not None:
                    before(k)
                w = slice((w0 + k) * P, (w0 + k + 1) * P)
                for j, (wt, r) in enumerate(((wh, 0), (wh, 1), (wl, 0))):
                    for a in range(2):
                        last = nc.tensor.matmul(
                            ps[:, 2 * s + a, 0:TH], lhsT=wt[:, slot, w],
                            rhs=rhs(r, k)[:, a * TH:(a + 1) * TH],
                            start=(k == 0 and j == 0), stop=(k == K - 1 and j == 2))
                if k == K - 1:
                    last.then_inc(S("unit"), 1)
                if between is not None and k % 2 == 1:
                    between(k // 2)

        def xin(r, k):
            return (xh, xl)[r][:, k, :]

        def hin(r, k):
            return hid[r][:, k, :]

        def norm_sum(norm):
            pe.wait_ge(S("sqsum"), count("sqsum", 7 * (norm + 1)))
            for a in range(2):
                last = nc.tensor.matmul(ps[:, 4 + a, 0:TH], lhsT=ones[:, :], rhs=sqsum[:, a * TH:(a + 1) * TH],
                                        start=True, stop=True)
            last.then_inc(S("norm_sum"), 1)

        def gated_group(ns, n, u, i, pair, previous_norm, following=True):
            G = lambda name, k: group_count(name, ns, i, pair, k)
            rows = [slice(0, P)] if ns == 1 else [slice(0, 64), slice(64, P)]

            def scores(lev):
                if lev == 0:
                    ready_k(pe, ns, u, i)
                    ready_q(pe, ns, u, i)
                    ka, qa = gk[:, :], gq[:, :]
                else:
                    pe.wait_ge(S("qu"), count("qu", G("qu", lev)))
                    ka, qa = gk[:, :], qu[:, lev % 2, :]
                    if lev > 1:
                        pe.wait_ge(S("kl"), count("kl", G("kl", lev - 1)))
                        ka = kl[:, lev % 2, :]
                def sample(s):
                    o = 256 * s + 64 * lev
                    return nc.tensor.matmul(ps[0:TS, 6, o:o + TS], lhsT=ka[rows[s], TP:T], rhs=qa[rows[s], TP:T],
                                            start=True, stop=True)

                if ns == 2 and lev <= 3:
                    if lev:
                        pe.wait_ge(S("picked"), count("picked", G("picked", 2 * lev)))
                    else:
                        pe.wait_ge(S("turned_out"), count("turned_out", G("turned_out", 0)))
                    sample(0).then_inc(S("first_sample"), 1)
                    pe.wait_ge(S("first_sample"), count("first_sample", 4 * pair + lev + 1))
                    sample(1)
                for s in range(ns):
                    j = lev * ns + s
                    bank = 4 + j % 2
                    if j >= 2:
                        pe.wait_ge(S("picked"), count("picked", G("picked", j - 1)))
                    else:
                        pe.wait_ge(S("orms"), count("orms", G("orms", 0)))
                    for c in range(CH):
                        t = slice(c * P, (c + 1) * P)
                        last = nc.tensor.matmul(ps[:, bank, t], lhsT=ka[rows[s], t], rhs=qa[rows[s], t],
                                                start=True, stop=True)
                    if ns == 1 and lev <= 3:
                        if j:
                            pe.wait_ge(S("picked"), count("picked", G("picked", j)))
                        last = sample(s)
                    last.then_inc(S("scores"), 1)

            turn = [0]

            def free_turn():
                reached = early(pe, count("turned_out", G("turned_out", turn[0])))
                pe.wait_ge(S("ones"), 1)
                pe.wait_ge(S("turned_out"), reached)
                turn[0] += 1

            def turn_tiles(src, prompt):
                free_turn()
                if prompt:
                    for c in range(CH):
                        last = nc.tensor.transpose(ps[:, 7, c * P:(c + 1) * P], src[:, c * P:(c + 1) * P], ident[:, :])
                else:
                    last = nc.tensor.transpose(ps[0:TS, 7, 0:P], src[:, TP:T], ident[:, :])
                last.then_inc(S("turned"), 1)

            def turn_v(s, uv, prompt):
                if prompt:
                    pe.wait_ge(S(f"taken{uv.mod(2)}"), count(f"taken{uv.mod(2)}", uv.div(2) + 1))
                turn_tiles(vf, prompt)

            def turn_kl(prompt):
                if prompt:
                    pe.wait_ge(S("kl"), count("kl", G("kl", 7)))
                turn_tiles(kl[:, 0, :], prompt)

            def state_prompt():
                free_turn()
                for s in range(ns):
                    for c in range(CH):
                        last = nc.tensor.matmul(ps[rows[s], 7, c * P:(c + 1) * P], lhsT=klt[:, c, rows[s]],
                                                rhs=vt[:, s, c, :], start=True, stop=True)
                last.then_inc(S("turned"), 1)

            def state_sample():
                free_turn()
                pe.wait_ge(S("picked"), count("picked", G("picked", 8 * ns)))
                for s in range(ns):
                    pe.wait_ge(S("vm"), count("vm", G("vm", s + 1)))
                    for a in range(2):
                        last = nc.tensor.matmul(ps[rows[s], 6 + a, :], lhsT=klt[0:TS, CH, rows[s]],
                                                rhs=vm[0:TS, s, 4 * a:4 * a + 4, :], start=True, stop=True)
                last.then_inc(S("turned"), 1)

            def outputs(s):
                if s:
                    pe.wait_ge(S("orms"), count("orms", G("orms", s)))
                else:
                    pe.wait_ge(S("qu"), count("qu", G("qu", 8)))
                    pe.wait_ge(S("S0_in"), count("S0_in", G("S0_in", 16)))
                for c in range(CH):
                    t = slice(c * P, (c + 1) * P)
                    last = nc.tensor.matmul(ps[:, 4, t], lhsT=vt[:, s, c, :], rhs=att[:, s, t],
                                            start=True, stop=(c == 0))
                    if c:
                        last = nc.tensor.matmul(ps[:, 4, t], lhsT=St[rows[s], c - 1, :], rhs=qu[rows[s], 0, t],
                                                start=False, stop=True)
                last = nc.tensor.matmul(ps[:, 5, 0:TS], lhsT=vt[0:TS, s, CH, :], rhs=att[0:TS, s, TP:T],
                                        start=True, stop=True, skip_group_check=True)
                if s:
                    last.then_inc(S("own_tokens"), 1)
                    pe.wait_ge(S("own_tokens"), count("own_tokens", pair + 1))
                for b in range(NBAT):
                    t = slice(LS * b, LS * b + LS)
                    last = nc.tensor.matmul(ps[:, 5, t], lhsT=S0[rows[s], b, :],
                                            rhs=qu[rows[s], 0, TP + LS * b:TP + LS * b + LS],
                                            start=False, stop=True, skip_group_check=True)
                last.then_inc(S("o_done"), 1)

            v = lambda s, prompt: (lambda: turn_v(s, u + s, prompt))
            if ns == 1:
                between = {
                    (0, 0): [previous_norm], (0, 2): [lambda: scores(0)], (0, 3): [lambda: scores(1)],
                    (1, 0): [v(0, True), lambda: scores(2)], (1, 1): [v(0, False), lambda: scores(3)],
                    (1, 2): [lambda: scores(4)], (1, 3): [lambda: scores(5)],
                    (2, 0): [lambda: scores(6)], (2, 1): [lambda: scores(7)],
                    (2, 2): [lambda: turn_kl(True)], (2, 3): [lambda: turn_kl(False)],
                    (3, 0): [state_prompt], (3, 1): [state_sample], (3, 2): [lambda: outputs(0)],
                }
            else:
                between = {
                    (0, 0): [previous_norm], (0, 1): [lambda: scores(0)], (0, 3): [lambda: scores(1)],
                    (1, 0): [v(0, True)], (1, 1): [v(0, False)], (1, 2): [lambda: scores(2)],
                    (2, 0): [v(1, True)], (2, 1): [v(1, False)], (2, 2): [lambda: scores(3)],
                    (3, 0): [lambda: scores(4)], (3, 2): [lambda: scores(5)],
                    (4, 0): [lambda: scores(6)], (4, 1): [lambda: scores(7)],
                    (4, 2): [lambda: turn_kl(True)], (4, 3): [lambda: turn_kl(False)],
                    (5, 0): [state_prompt], (5, 1): [state_sample, lambda: outputs(0)],
                    (5, 2): [lambda: head_norm(ns, i, pair, 0)], (5, 3): [lambda: outputs(1)],
                }

            def put_in(k):
                def run(q):
                    for step in between.get((k, q), ()):
                        step()
                return run

            for k in range(2 * ns + (2 if following else 0)):
                unit(n + k, u + k, xin, NB, between=put_in(k))
            if not following:
                for k in range(2 * ns, 2 * ns + 2):
                    unit(n + k, u + k, hin, NB, ks=range(NB - 2), between=put_in(k), before=mixed)
                    put_in(k)(3)
                head_norm(ns, i, pair, 1)
                for block in (NB - 2, NB - 1):
                    for k in range(2 * ns, 2 * ns + 2):
                        unit(n + k, u + k, hin, NB, ks=[block], before=mixed)

        def mixed(k):
            pe.wait_ge(S("omixl"), count("omixl", k + 1))

        def head_norm(ns, i, pair, s):
            pe.wait_ge(S("osq"), count("osq", group_count("osq", ns, i, pair, s + 1)))
            for a in range(2):
                last = nc.tensor.matmul(ps[:, 4 + a, 0:TH], lhsT=ones[:, :],
                                        rhs=hsq[max(s, 0)][:, a * TH:(a + 1) * TH], start=True, stop=True)
            last.then_inc(S("oss"), 1)

        def retention_head(n, u, i, before_last=False, last_head=False):
            R = lambda k, per: Lin(k, per, i)

            def turn_k(kk):
                pe.wait_ge(S("rturned_out"), count("rturned_out", R(kk, 6)))
                if kk == 0:
                    pe.wait_ge(S("rot_k0"), count("rot_k0", R(1, 1)))
                    pe.wait_ge(S("rot_k1"), count("rot_k1", R(1, 1)))
                for c in range(CH):
                    nc.tensor.transpose(ps[:, 7, c * P:(c + 1) * P], rk[:, kk, c * P:(c + 1) * P], ident[:, :])
                nc.tensor.transpose(ps[0:TS, 6, 0:P], rk[:, kk, TP:T], ident[:, :]).then_inc(S("rturned"), 1)

            def turn_v(vb):
                pe.wait_ge(S(f"taken{(u + vb).mod(2)}"), count(f"taken{(u + vb).mod(2)}", (u + vb).div(2) + 1))
                pe.wait_ge(S("rturned_out"), count("rturned_out", R(2 + vb, 6)))
                for c in range(CH):
                    nc.tensor.transpose(ps[:, 7, c * P:(c + 1) * P], rv[:, vb % 2, c * P:(c + 1) * P], ident[:, :])
                nc.tensor.transpose(ps[0:TS, 6, 0:P], rv[:, vb % 2, TP:T], ident[:, :]).then_inc(S("rturned"), 1)

            def scores(j):
                if j >= 2 and j < 4:
                    pe.wait_ge(S("ratt"), count("ratt", R(j - 1, 5)))
                if j == 4:
                    pe.wait_ge(S("rturned_out"), count("rturned_out", R(6, 6)))
                for kk in range(2):
                    if j < 4:
                        last = nc.tensor.matmul(ps[:, 4 + j % 2, 0:TP - P * j], lhsT=rk[:, kk, P * j:P * j + P],
                                                rhs=rq[:, kk, P * j:TP], start=(kk == 0), stop=(kk == 1))
                    else:
                        last = nc.tensor.matmul(ps[0:TS, 6, 0:TS], lhsT=rk[:, kk, TP:T], rhs=rq[:, kk, TP:T],
                                                start=(kk == 0), stop=(kk == 1))
                last.then_inc(S("rscores"), 1)

            def outputs(vb):
                if vb >= 2:
                    pe.wait_ge(S("ro_out"), count("ro_out", R(vb - 1, 5)))
                else:
                    pe.wait_ge(S("rturned_out"), count("rturned_out", R(3 + vb, 6)))
                    pe.wait_ge(S("ratt"), count("ratt", R(4, 5)))
                for j in range(CH):
                    last = nc.tensor.matmul(ps[:, 4 + vb % 2, P * j:TP], lhsT=rvt[:, j, vb * P:(vb + 1) * P],
                                            rhs=ratt[:, RAT[j]:RAT[j] + TP - P * j],
                                            start=(j == 0), stop=True, skip_group_check=True)
                last.then_inc(S("ro_done"), 1)

            def prompt_state(kk):
                pe.wait_ge(S("ro_out"), count("ro_out", R(3 + kk, 5)))
                for j in range(CH):
                    last = nc.tensor.matmul(ps[:, 4 + kk, :], lhsT=kd[:, j, kk * P:(kk + 1) * P], rhs=rvt[:, j, :],
                                            start=(j == 0), stop=(j == CH - 1))
                last.then_inc(S("rstate"), 1)

            def own_tokens():
                pe.wait_ge(S("ratt"), count("ratt", R(5, 5)))
                for vb in range(4):
                    nc.tensor.matmul(ps[:, 6, vb * TS:(vb + 1) * TS], lhsT=rvt[0:TS, CH, vb * P:(vb + 1) * P],
                                     rhs=ratts[0:TS, :], start=(vb == 0), stop=True, skip_group_check=True)
                pe.wait_ge(S("kdm"), count("kdm", R(1, 1)))
                pe.wait_ge(S("qd"), count("qd", R(1, 1)))

            def sequence(b, kk):
                if kk == 0:
                    pe.wait_ge(S(f"rS0_in{b % 4}"), count(f"rS0_in{b % 4}", Lin(16 * (b // 4 + 1), 32, i)))
                    for k in range(2):
                        for vb in range(4):
                            o = vb * TS + LS * b
                            last = nc.tensor.matmul(ps[:, 6, o:o + LS], lhsT=rS0[:, b % 4, k, vb * P:(vb + 1) * P],
                                                    rhs=qd[:, k, LS * b:LS * b + LS], start=False,
                                                    stop=(k == 1), skip_group_check=True)
                    if b == NBAT - 1:
                        last.then_inc(S("ro_done"), 1)
                j = 2 * b + kk
                if j == 8:
                    pe.wait_ge(S("rstate_out"), count("rstate_out", R(2, 2)))
                elif j:
                    pe.wait_ge(S("rnew"), count("rnew", R(j if j < 8 else j - 1, 16)))
                bank = 5 if b >= 4 and kk == 0 else 7
                nc.tensor.matmul(ps[:, bank, :], lhsT=kdm[0:TS, b, kk * P:(kk + 1) * P],
                                 rhs=rvt[0:TS, CH, :], start=True, stop=True).then_inc(S("rkv"), 1)

            def mean():
                pe.wait_ge(S("rsummed"), count("rsummed", R(3, 3)))
                pe.wait_ge(S("rnew"), count("rnew", R(16, 16)))
                for a in range(2):
                    last = nc.tensor.matmul(ps[:, 4 + a, 0:TH], lhsT=ones[:, :], rhs=sqsum[:, a * TH:(a + 1) * TH],
                                            start=True, stop=True)
                last.then_inc(S("rmean"), 1)

            def variance():
                pe.wait_ge(S("rcent"), count("rcent", R(4, 4)))
                pe.wait_ge(S("rsqsum"), count("rsqsum", R(3, 3)))
                for a in range(2):
                    last = nc.tensor.matmul(ps[:, 4 + a, 0:TH], lhsT=ones[:, :], rhs=sqsum[:, a * TH:(a + 1) * TH],
                                            start=True, stop=True)
                last.then_inc(S("rvar"), 1)

            between = {
                (0, 2): [lambda: turn_k(0)], (0, 3): [lambda: scores(0)], (1, 0): [lambda: turn_k(1)],
                (1, 1): [lambda: scores(1)], (1, 3): [lambda: turn_v(0)],
                (2, 0): [lambda: scores(2)], (2, 2): [lambda: turn_v(1)],
                (3, 0): [lambda: scores(3)], (3, 2): [lambda: turn_v(2)],
                (4, 0): [lambda: outputs(0)], (4, 1): [lambda: turn_v(3)], (4, 2): [lambda: outputs(1)],
                (4, 3): [lambda: scores(4)],
                (5, 0): [own_tokens, lambda: sequence(0, 0)], (5, 1): [lambda: sequence(0, 1), lambda: outputs(2)],
                (5, 2): [lambda: sequence(1, 0)], (5, 3): [lambda: sequence(1, 1), lambda: outputs(3)],
                (6, 0): [lambda: sequence(2, 0), lambda: prompt_state(0)], (6, 1): [lambda: sequence(2, 1)],
                (6, 2): [lambda: sequence(3, 0), lambda: prompt_state(1)], (6, 3): [lambda: sequence(3, 1)],
                (7, 0): [lambda: sequence(4, 0), lambda: sequence(4, 1)],
                (7, 1): [lambda: sequence(5, 0), lambda: sequence(5, 1)],
                (7, 2): [lambda: sequence(6, 0), lambda: sequence(6, 1)],
                (7, 3): [lambda: sequence(7, 0), lambda: sequence(7, 1)],
                (9, 0): [mean], (10, 0): [variance],
            }

            def put_in(k):
                def run(q):
                    for step in between.get((k, q), ()):
                        step()
                return run

            for k in range(8 if last_head else 12):
                unit(n + k, u + k, xin, NB, between=put_in(k))
            if last_head:
                projection(n + 8, u + 8, between={0: mean, 3: variance})
                projection(n + 12, u + (8 + NB), ready=lambda k: Lin(4 * (H - 1) + k + 1))
            elif not before_last:
                projection(n + 12, u + 12, ready=lambda k: R(k + 1, 4))

        def projection(n, u, ready=None, between={}):
            for m in range(NB):
                wait = lambda k: pe.wait_ge(S("rmixl"), count("rmixl", ready(k)))
                if m == 0 and ready is None:
                    pe.wait_ge(S("rmixl"), count("rmixl", 4 * (H - 1)))
                unit(n + m // 2, u + m, hin, 4, w0=4 * (m % 2), before=wait if m == 0 and ready else None)
                if m in between:
                    between[m]()

        def first_unit(norm, n, u, quarter=2):
            def between(q):
                if q == quarter:
                    norm_sum(norm)

            unit(n, u, xin, NB, before=lambda k: pe.wait_ge(S("xl_made"), count("xl_made", NB * norm + k + 1)),
                 between=between)

        pe.wait_ge(S("ones"), count("ones", 1))
        for ph_ in phases:
            n, u, norm = Lin(ph_["n"]), Lin(ph_["u"]), ph_["norm"]
            if ph_["kind"] == "ffn":
                j0 = ph_["j"]
                first_unit(norm, n, u, quarter=3 if norm in (0, 4) else 2)
                for k in range(1, 4):
                    unit(n + k, u + k, xin, NB)
                for part, J in enumerate(FF_PARTS):
                    with pe.Fori(0 if part else 1, J // 2) as i:
                        for k in range(4):
                            unit(Lin(n.c + k, 4, i), Lin(u.c + k, 4, i), xin, NB)
                    n, u = n + 2 * J, u + 2 * J
                    for m in range(NB):
                        unit(n + m, u + m, hin, J,
                             before=(lambda k: pe.wait_ge(S("hid_low"), count("hid_low", j0 + k + 1))) if m == 0 else None)
                    n, u, j0 = n + NB, u + NB, j0 + J
            elif ph_["kind"] == "ab":
                pe.wait_ge(S("ident_in"), count("ident_in", 16))
                first_unit(norm, n, u)
                unit(n + 1, u + 1, xin, NB)
                pe.wait_ge(S(f"taken{u.mod(2)}"), count(f"taken{u.mod(2)}", u.div(2) + 1))
                pe.wait_ge(S("gk2_in"), count("gk2_in", 16))
                for p in range(2):
                    for a in range(2):
                        last = nc.tensor.matmul(ps[:, 4 + 2 * p + a, 0:TH], lhsT=gk2[:, p * P:(p + 1) * P],
                                                rhs=lr[0:16, a * TH:(a + 1) * TH], start=True, stop=True)
                last.then_inc(S("gkz"), 1)
                unit(n + 2, u + 2, xin, NB)
                pe.wait_ge(S("gkz_out"), count("gkz_out", 2))
                n, u = n + 3, u + 3
                gated_group(1, n, u, 0, None, lambda: None)
                with pe.Fori(1, H) as i:
                    gated_group(1, Lin(n.c, 4, i, 1), Lin(u.c, 4, i, 1), i, None,
                                lambda: head_norm(1, i, None, -1))
                n, u = n + 4 * H, u + 4 * H
                gated_group(2, n, u, None, 0, lambda: head_norm(1, H - 1, None, 0))
                n, u = n + N_GLA, u + N_GLA
                gated_group(2, n, u, None, 1, lambda: head_norm(2, None, 0, 1), following=False)
                n, u = n + 4, u + 4
                for m in range(2, NB):
                    unit(n + m, u + m, hin, NB)
            elif ph_["kind"] == "ret":
                first_unit(norm, n, u)
                for k in range(1, 4):
                    unit(n + k, u + k, xin, NB)
                with pe.Fori(0, H - 2) as i:
                    retention_head(Lin(n.c + 4, N_RET, i), Lin(u.c + 4, 12 + NB, i), i)
                retention_head(n + (4 + (H - 2) * N_RET), u + (4 + (H - 2) * (12 + NB)), H - 2, before_last=True)
                retention_head(n + (H - 1) * N_RET, u + (4 + (H - 1) * (12 + NB) - NB), H - 1, last_head=True)
            else:
                first_unit(norm, n, u)
                for m in range(1, NB):
                    unit(n + m, u + m, xin, NB)
                pe.wait_ge(S("p_low"), count("p_low", 2 * (ph_["layer"] + 1)))
                n, u = n + NB, u + NB
                for m in range(NB):
                    unit(n + m // 4, u + m, lambda r, k: (ph, pl)[r][:, k, :], 2, w0=2 * (m % 4))
        norm_sum(8)

    @block.scalar
    def _(act):
        def split(n, used):
            if n.c >= N_PIECES:
                return
            r = n.mod(NRAW)
            act.wait_ge(S(f"landed{r}"), count(f"landed{r}", Lin(16 * (n.c // NRAW + 1), 16 * n.k // NRAW, n.i)))
            act.wait_ge(S("unit"), count("unit", used))
            nc.scalar.activation(wh[:, n.mod(2), :], raw[:, r, :], ACT.Copy).then_inc(S("hi_made"), 1)

        def norm_prep(norm, m, ready):
            ready()
            if norm < 8:
                nc.scalar.activation(xh[:, m, :], x[:, m, :], ACT.Copy, scale=gains[:, norm, m:m + 1])\
                    .then_inc(S("xh_made"), 1)
            if m >= 2:
                act.wait_ge(S("sqsum"), count("sqsum", 7 * norm + m - 1))
            elif norm:
                act.wait_ge(S("norm_sum"), count("norm_sum", norm))
            nc.scalar.activation(sq[:, m % 2, :], x[:, m, :], ACT.Square).then_inc(S("sq"), 1)

        def norm_root(norm):
            act.wait_ge(S("norm_sum"), count("norm_sum", norm + 1))
            if norm:
                act.wait_ge(S("rinv"), count("rinv", norm))
            nc.scalar.activation(two(rms[:, :]), ps[:, 4:6, 0:TH], ACT.Sqrt, bias=eps, scale=1.0 / D)\
                .then_inc(S("rms"), 1)

        def gated_group(ns, n, u, i, pair, previous, following):
            G = lambda name, k: group_count(name, ns, i, pair, k)
            rounds = [0]

            def turn_out(dst, prompt):
                rounds[0] += 1
                act.wait_ge(S("turned"), count("turned", G("turned", rounds[0])))
                if prompt:
                    src = ps[:, 7, :].rearrange("p (c k) -> p c k", c=CH)
                    nc.scalar.activation(dst[:, 0:CH, :], src, ACT.Copy).then_inc(S("turned_out"), 1)
                else:
                    nc.scalar.activation(dst[0:TS, CH, :], ps[0:TS, 7, 0:P], ACT.Copy).then_inc(S("turned_out"), 1)

            def step(k):
                split(n + (k + 2), u + (k + 1))

            def taken(k):
                act.wait_ge(S(f"taken{(u + k).mod(2)}"), count(f"taken{(u + k).mod(2)}", (u + k).div(2) + 1))

            def output(s):
                act.wait_ge(S("o_done"), count("o_done", G("o_done", s + 1)))
                act.wait_ge(S("omixl"), count("omixl", G("omixl", 0)))
                nc.scalar.activation(hout[s][:, 0:TP], ps[:, 4, :], ACT.Copy)
                nc.scalar.activation(hout[s][:, TP:T], ps[:, 5, 0:TS], ACT.Copy).then_inc(S("o_out"), 1)
                act.wait_ge(S("o_out"), count("o_out", G("o_out", s + 1)))
                nc.scalar.activation(hsq[s], hout[s], ACT.Square).then_inc(S("osq"), 1)

            def gate_sigmoid(s):
                taken(ns + s)
                if s:
                    act.wait_ge(S("gate"), count("gate", G("gate", s)))
                nc.scalar.activation(s1[:, :], gate[:, s, :], ACT.Sigmoid).then_inc(S("sig"), 1)

            if previous:
                head_root(*previous)
            else:
                decay_log(0)
            step(0)
            if not previous:
                decay_exp(0)
            turn_out(vt[:, 0], True)
            turn_out(vt[:, 0], False)
            if not previous:
                decay_log(1)
                decay_exp(1)
            elif ns == 1:
                heads_high(*previous)
            step(1)
            if ns == 2:
                turn_out(vt[:, 1], True)
                turn_out(vt[:, 1], False)
                heads_high(*previous)
                step(2)
                gate_sigmoid(0)
                step(3)
                gate_sigmoid(1)
            else:
                gate_sigmoid(0)
            turn_out(klt, True)
            if following:
                step(2 * ns)
            turn_out(klt, False)
            if following == "hgrn":
                taken(2 * ns)
                act.wait_ge(S("gate"), count("gate", G("gate", ns)))
                key_sigmoids()
            output(0)
            if ns == 2:
                head_root(ns, i, pair, 0)
                output(1)
            if following:
                step(2 * ns + 1)
            if following == "hgrn":
                taken(2 * ns + 1)
                act.wait_ge(S("qu"), count("qu", G("qu", 8)))
                query_sigmoid()

        def decay_log(p):
            act.wait_ge(S("k_ready"), count("k_ready", 1))
            if p:
                act.wait_ge(S("gk_min"), count("gk_min", 1))
            act.wait_ge(S("gkz_out"), count("gkz_out", p + 1))
            nc.scalar.activation(s1[:, :], gkz[p], ACT.Abs).then_inc(S("gk_ln"), 1)
            act.wait_ge(S("gk_ln"), count("gk_ln", 3 * p + 1))
            nc.scalar.activation(s2[:, :], s1[:, :], ACT.Exp, scale=-1.0).then_inc(S("gk_ln"), 1)
            act.wait_ge(S("gk_ln"), count("gk_ln", 3 * p + 2))
            nc.scalar.activation(s1[:, :], s2[:, :], ACT.Ln, bias=1.0).then_inc(S("gk_ln"), 1)

        def decay_exp(p):
            act.wait_ge(S("gk_min"), count("gk_min", p + 1))
            nc.scalar.activation(decay[:, p, :], gkz[p], ACT.Exp, scale=1.0 / 16).then_inc(S("decay"), 1)

        def key_sigmoids():
            nc.scalar.activation(s1[:, :], kz[:, :], ACT.Sigmoid).then_inc(S("sig"), 1)
            nc.scalar.activation(s2[:, :], kz[:, :], ACT.Sigmoid, scale=-1.0).then_inc(S("sig"), 1)

        def query_sigmoid():
            nc.scalar.activation(gq[:, :], qz[:, :], ACT.Sigmoid).then_inc(S("sig"), 1)

        def head_root(ns, i, pair, s):
            G = lambda name, k: group_count(name, ns, i, pair, k)
            act.wait_ge(S("oss"), count("oss", G("oss", s + 1)))
            nc.scalar.activation(two(hsq[max(s, 0)]), ps[:, 4:6, 0:TH], ACT.Sqrt, bias=eps, scale=1.0 / P)\
                .then_inc(S("orms"), 1)

        def heads_high(ns, i, pair, s, heads=None):
            G = lambda name, k: group_count(name, ns, i, pair, k)
            for r in heads or range(ns):
                q = s - ns + 1 + r
                act.wait_ge(S("omix"), count("omix", G("omix", q + 1)))
                dst = hid[0][:, i + q, :] if ns == 1 else hid[0][:, 4 + 2 * pair + q, :]
                nc.scalar.activation(dst, hout[r], ACT.Copy).then_inc(S("omixh"), 1)

        def retention_head(n, u, i, before_last=False, last_head=False):
            R = lambda k, per: Lin(k, per, i)
            o = 8 if last_head else 12

            def step(k):
                split(n + (k + 2), u + (k + 1 if k < o else o + 2 * (k - o + 1)))

            def turned_v(vb):
                act.wait_ge(S("rturned"), count("rturned", R(3 + vb, 6)))
                nc.scalar.activation(rvt[:, 0:CH, vb * P:(vb + 1) * P],
                                     ps[:, 7, :].rearrange("p (c k) -> p c k", c=CH), ACT.Copy)
                nc.scalar.activation(rvt[0:TS, CH, vb * P:(vb + 1) * P], ps[0:TS, 6, 0:P], ACT.Copy)\
                    .then_inc(S("rturned_out"), 1)

            def silu(gb):
                act.wait_ge(S(f"taken{(u + 4 + gb).mod(2)}"),
                            count(f"taken{(u + 4 + gb).mod(2)}", (u + 4 + gb).div(2) + 1))
                nc.scalar.activation(rg[:, gb, :], rv[:, gb % 2, :], ACT.Silu).then_inc(S("rgate"), 1)

            def output(vb):
                act.wait_ge(S("ro_done"), count("ro_done", R(vb + 1, 5)))
                nc.scalar.activation(ro[:, vb, 0:TP], ps[:, 4 + vb % 2, :], ACT.Copy).then_inc(S("ro_out"), 1)

            act.wait_ge(S("ctab_in"), count("ctab_in", R(16, 16)))
            for kk in range(2):
                if kk:
                    step(0)
                act.wait_ge(S("rturned"), count("rturned", R(1 + kk, 6)))
                for c in range(CH):
                    nc.scalar.activation(kd[:, c, kk * P:(kk + 1) * P], ps[:, 7, c * P:(c + 1) * P], ACT.Copy,
                                         scale=kdec[:, c:c + 1])
                nc.scalar.activation(kd[0:TS, CH, kk * P:(kk + 1) * P], ps[0:TS, 6, 0:P], ACT.Copy, scale=kdecs)\
                    .then_inc(S("rturned_out"), 1)
            step(1)
            turned_v(0)
            for k in range(2, 4):
                turned_v(k - 1)
                step(k)
            output(0)
            turned_v(3)
            output(1)
            step(4)
            silu(0)
            output(2)
            output(3)
            step(5)
            silu(1)
            for kk in range(2):
                act.wait_ge(S("rstate"), count("rstate", R(kk + 1, 2)))
                nc.scalar.activation(rSt[:, kk, :], ps[:, 4 + kk, :], ACT.Copy).then_inc(S("rstate_out"), 1)
            step(6)
            silu(2)
            step(7)
            silu(3)
            act.wait_ge(S("ro_done"), count("ro_done", R(5, 5)))
            nc.scalar.activation(ro[:, :, TP:T], ps[:, 6, 0:4 * TS].rearrange("p (v t) -> p v t", v=4), ACT.Copy)\
                .then_inc(S("ro_out"), 1)
            if not last_head:
                step(8)
            for vb in range(4):
                act.wait_ge(S("rcent"), count("rcent", R(vb + 1, 4)))
                if vb >= 2:
                    act.wait_ge(S("rsqsum"), count("rsqsum", R(vb - 1, 3)))
                nc.scalar.activation(sq[:, vb % 2, :], ro[:, vb, :], ACT.Square).then_inc(S("rsq"), 1)
            if last_head:
                step(8)
            step(9)
            act.wait_ge(S("rvar"), count("rvar", R(1, 1)))
            nc.scalar.activation(two(rr), ps[:, 4:6, 0:TH], ACT.Sqrt, bias=eps, scale=1.0 / 512).then_inc(S("rrms"), 1)
            if last_head:
                step(10)
                step(11)
            for vb in range(4):
                act.wait_ge(S("rmix"), count("rmix", R(vb + 1, 4)))
                nc.scalar.activation(hid[0][:, vb, :], ro[:, vb, :], ACT.Copy).then_inc(S("rmixh"), 1)
            if not last_head:
                step(10)
                step(11)
                for k in range(12, 12 if before_last else 16):
                    step(k)

        act.wait_ge(S("small_in"), count("small_in", 32))
        act.wait_ge(S("lb_shift"), count("lb_shift", 1))
        nc.scalar.activation(lbe, lbe, ACT.Exp).then_inc(S("lb_exp"), 1)
        act.wait_ge(S("eps"), count("eps", 1))
        split(Lin(0), 0)
        split(Lin(1), 0)
        for m in range(NB):
            norm_prep(0, m, lambda: act.wait_ge(S(f"x_in{m}"), count(f"x_in{m}", 16)))
        for ph_ in phases:
            n, u, norm = Lin(ph_["n"]), Lin(ph_["u"]), ph_["norm"]
            norm_root(norm)

            def x_new(k):
                act.wait_ge(S(f"taken{(u + k).mod(2)}"), count(f"taken{(u + k).mod(2)}", (u + k).div(2) + 1))

            if ph_["kind"] == "ffn":
                j0 = ph_["j"]
                for part, J in enumerate(FF_PARTS):
                    with act.Fori(0, J // 2) as i:
                        for k in range(2):
                            nn, uu = Lin(n.c + 2 * k, 4, i), Lin(u.c + 2 * k, 4, i)
                            j = Lin(j0 + k, 2, i)
                            split(nn + 2, uu + 1)
                            act.wait_ge(S(f"taken{uu.mod(2)}"), count(f"taken{uu.mod(2)}", uu.div(2) + 1))
                            act.wait_ge(S("gated"), count("gated", j))
                            nc.scalar.activation(fs[:, k, :], fa[:, k, :], ACT.Silu).then_inc(S("silu"), 1)
                            act.wait_ge(S("gated"), count("gated", j + 1))
                            dst = hid[0][:, i * 2 + k, :]
                            nc.scalar.activation(dst, ff[:, k, :], ACT.Copy).then_inc(S("hid_high"), 1)
                            split(nn + 3, uu + 2)
                    n, u, j0 = n + 2 * J, u + 2 * J, j0 + J
                    for m in range(NB):
                        split(n + (m + 2), u + (m + 1))
                        if part == 2:
                            norm_prep(norm + 1, m, lambda: x_new(m))
                    n, u = n + NB, u + NB
            elif ph_["kind"] == "ab":
                split(n + 2, u + 1)
                split(n + 3, u + 2)
                act.wait_ge(S(f"taken{(u + 1).mod(2)}"), count(f"taken{(u + 1).mod(2)}", (u + 1).div(2) + 1))
                key_sigmoids()
                split(n + 4, u + 3)
                act.wait_ge(S(f"taken{(u + 2).mod(2)}"), count(f"taken{(u + 2).mod(2)}", (u + 2).div(2) + 1))
                query_sigmoid()
                n, u = n + 3, u + 3
                gated_group(1, n, u, 0, None, None, "hgrn")
                with act.Fori(1, H - 1) as i:
                    gated_group(1, Lin(n.c, 4, i, 1), Lin(u.c, 4, i, 1), i, None,
                                (1, i, None, -1), "hgrn")
                gated_group(1, n + 4 * (H - 1), u + 4 * (H - 1), H - 1, None,
                            (1, H - 2, None, 0), "gla")
                n, u = n + 4 * H, u + 4 * H
                gated_group(2, n, u, None, 0, (1, H - 1, None, 0), "gla")
                n, u = n + N_GLA, u + N_GLA
                gated_group(2, n, u, None, 1, (2, None, 0, 1), None)
                heads_high(2, None, 1, 1, heads=[0])
                head_root(2, None, 1, 1)
                heads_high(2, None, 1, 1, heads=[1])
                n, u = n + 4, u + 4
                for m in range(NB):
                    split(n + (m + 2), u + (m + 1))
                    norm_prep(norm + 1, m, lambda: x_new(m))
            elif ph_["kind"] == "ret":
                for k in range(4):
                    split(n + (k + 2), u + (k + 1))
                with act.Fori(0, H - 2) as i:
                    retention_head(Lin(n.c + 4, N_RET, i), Lin(u.c + 4, 12 + NB, i), i)
                retention_head(n + (4 + (H - 2) * N_RET), u + (4 + (H - 2) * (12 + NB)), H - 2, before_last=True)
                n, u = n + (H - 1) * N_RET, u + (4 + (H - 1) * (12 + NB) - NB)
                retention_head(n, u, H - 1, last_head=True)
                u = u + (8 + 2 * NB)
                for m in range(NB):
                    if m % 2 == 1:
                        split(n + (14 + m // 2), u + (-NB + m + 1))
                    norm_prep(norm + 1, m, lambda: act.wait_ge(S(f"taken{(u + (-NB + m)).mod(2)}"), count(f"taken{(u + (-NB + m)).mod(2)}", (u + (-NB + m)).div(2) + 1)))
            else:
                lay = ph_["layer"]
                act.wait_ge(S("praw_in"), count("praw_in", 16 * (lay + 1)))
                for k in range(2):
                    nc.scalar.activation(ph[:, k, :], praw[:, k, :], ACT.Copy).then_inc(S("p_high"), 1)
                for m in range(NB):
                    split(n + (m + 2), u + (m + 1))
                    act.wait_ge(S(f"taken{(u + m).mod(2)}"), count(f"taken{(u + m).mod(2)}", (u + m).div(2) + 1))
                    nc.scalar.activation(pg[:, m, :], pz[:, m % 2, :], ACT.Sigmoid).then_inc(S("pgate"), 1)
                n, u = n + NB, u + NB
                for m in range(NB):
                    if m % 4 == 3:
                        split(n + (m // 4 + 2), u + (m + 1))
                    norm_prep(norm + 1, m, lambda: act.wait_ge(S("p_added"), count("p_added", NB * lay + m + 1)))
        norm_root(8)

    @block.vector
    def _(dve):
        def split(n):
            if n.c >= N_PIECES:
                return
            dve.wait_ge(S("hi_made"), count("hi_made", n + 1))
            nc.vector.tensor_tensor(wl[:, n.mod(2), :], raw[:, n.mod(NRAW), :], wh[:, n.mod(2), :], ALU.subtract)\
                .then_inc(S("lo_made"), 1)

        def pair_of(u):
            s = u.mod(2)
            return ps[:, 2 * s:2 * s + 2, 0:TH]

        def scaled(dst, u):
            dve.wait_ge(S("unit"), count("unit", u + 1))
            nc.vector.tensor_tensor(two(dst), pair_of(u), two(rinv[:, :]), ALU.mult).then_inc(S(f"taken{u.mod(2)}"), 1)

        def add_to_x(m, u, scale):
            dve.wait_ge(S("unit"), count("unit", u + 1))
            nc.vector.scalar_tensor_tensor(out=two(x[:, m, :]), in0=pair_of(u), scalar=scale, in1=two(x[:, m, :]),
                                           op0=ALU.mult, op1=ALU.add).then_inc(S(f"taken{u.mod(2)}"), 1)

        def norm_low(norm, m):
            if norm == 8:
                return
            dve.wait_ge(S("xh_made"), count("xh_made", NB * norm + m + 1))
            nc.vector.scalar_tensor_tensor(out=xl[:, m, :], in0=x[:, m, :], scalar=gains[:, norm, m:m + 1],
                                           in1=xh[:, m, :], op0=ALU.mult, op1=ALU.subtract).then_inc(S("xl_made"), 1)

        def norm_inverse(norm):
            dve.wait_ge(S("rms"), count("rms", norm + 1))
            nc.vector.reciprocal(rinv[:, :], rms[:, :]).then_inc(S("rinv"), 1)
            dve.wait_ge(S("rinv"), count("rinv", norm + 1))

        def gated_group(ns, n, u, i, pair, previous, following):
            G = lambda name, k: group_count(name, ns, i, pair, k)
            U = gU[:, :] if ns == 1 else decay[:, pair, :]

            def picked(lev):
                for s in range(ns):
                    j = lev * ns + s
                    reached = early(dve, count("scores", G("scores", j + 1)))
                    dve.wait_ge(S("masks_in"), 16)
                    dve.wait_ge(S("scores"), reached)
                    src = ps[:, 4 + j % 2, :].rearrange("p (c t) -> p c t", c=CH)
                    dst = att[:, s, 0:TP].rearrange("p (c t) -> p c t", c=CH)
                    if lev <= 3:
                        smp = ps[0:TS, 6, 256 * s + 64 * lev:256 * s + 64 * lev + TS]
                    if lev == 0:
                        dve.wait_ge(S("o_done"), count("o_done", G("o_done", 0)))
                        m = ident[:, :].unsqueeze(1).broadcast_to([P, CH, P])
                        nc.vector.tensor_tensor(dst, src, m, ALU.mult)
                        nc.vector.tensor_tensor(att[0:TS, s, TP:T], smp, ident[0:TS, 0:TS], ALU.mult)\
                            .then_inc(S("picked"), 1)
                        continue
                    dve.wait_ge(S("picked"), count("picked", G("picked", j)))
                    m = masks[:, lev - 1, :].unsqueeze(1).broadcast_to([P, CH, P])
                    last = nc.vector.copy_predicated(dst, m, src)
                    if lev <= 3:
                        last = nc.vector.copy_predicated(att[0:TS, s, TP:T], masks[0:TS, lev - 1, 0:TS], smp)
                    last.then_inc(S("picked"), 1)

            def level(lev):
                h = 1 << (lev - 1)
                R = T if h <= 4 else TP
                if lev > 2:
                    dve.wait_ge(S("scores"), count("scores", G("scores", (lev - 1) * ns)))
                else:
                    dve.wait_ge(S("o_done"), count("o_done", G("o_done", 0)))
                ready_q(dve, ns, u, i)
                if lev > 1:
                    dve.wait_ge(S("u_up"), count("u_up", G("u_up", lev - 1)))
                nc.vector.tensor_tensor(qu[:, lev % 2, 0:R], gq[:, 0:R], U[:, 0:R], ALU.mult).then_inc(S("qu"), 1)
                dve.wait_ge(S("l_up"), count("l_up", G("l_up", lev + 1)))
                dve.wait_ge(S("qu"), count("qu", G("qu", lev)))
                v = U[:, 0:R].rearrange("p (b a h) -> p b a h", a=2, h=h)
                nc.vector.tensor_tensor(v[:, :, 1, :], v[:, :, 1, :],
                                        v[:, :, 0, h - 1:h].broadcast_to([P, R // (2 * h), h]), ALU.mult)\
                    .then_inc(S("u_up"), 1)

            def invert(quarter):
                if previous:
                    root_inverse(*previous, quarter)

            def gate_scaled(s):
                if previous:
                    dve.wait_ge(S("omix"), count("omix", G("omix", 0)))
                scaled(gate[:, s, :], u + (ns + s))

            def gated(s):
                dve.wait_ge(S("sig"), count("sig", G("sig", 4 if ns == 1 else s + 1)))
                nc.vector.tensor_tensor(gate[:, s, :], gate[:, s, :], s1[:, :], ALU.mult).then_inc(S("gate"), 1)

            level(1)
            level(2)
            picked(0)
            scaled(vf[:, :], u)
            split(n + 2)
            invert(0)
            picked(1)
            if previous:
                invert(1)
            else:
                decay_min(0)
            level(3)
            picked(2)
            invert(2)
            level(4)
            if ns == 2:
                dve.wait_ge(S("turned"), count("turned", G("turned", 2)))
                scaled(vf[:, :], u + 1)
                split(n + 3)
                invert(3)
                picked(3)
                level(5)
                heads_output(*previous)
                gate_scaled(0)
                split(n + 4)
                gated(0)
                picked(4)
                level(6)
                gate_scaled(1)
                split(n + 5)
                picked(5)
                level(7)
                gated(1)
            else:
                picked(3)
                invert(3)
                level(5)
                if previous:
                    heads_output(*previous)
                else:
                    decay_min(1)
                picked(4)
                level(6)
                gate_scaled(0)
                split(n + 3)
                picked(5)
                level(7)
                gated(0)
            picked(6)
            dve.wait_ge(S("scores"), count("scores", G("scores", 7 * ns)))
            dve.wait_ge(S("u_up"), count("u_up", G("u_up", 7)))
            nc.vector.tensor_tensor(qu[:, 0, :], gq[:, :], U, ALU.mult).then_inc(S("qu"), 1)
            picked(7)
            if following:
                split(n + (2 * ns + 2))
                if following == "hgrn":
                    scaled(kz[:, :], u + 2 * ns)
                else:
                    dve.wait_ge(S("kl"), count("kl", G("kl", 7)))
                    scaled(gk[:, :], u + 2 * ns)
            k = 2 * ns + 3
            dve.wait_ge(S("turned"), count("turned", G("turned", k)))
            for c in range(CH):
                src = ps[:, 7, c * P:(c + 1) * P]
                if c == 0:
                    nc.vector.tensor_copy(St[:, 0, :], src).then_inc(S("s_step"), 1)
                    continue
                dve.wait_ge(S("s_step"), count("s_step", G("s_step", c)))
                last = nc.vector.scalar_tensor_tensor(out=St[:, c, :], in0=St[:, c - 1, :],
                                                      scalar=U[:, c * P + P - 1:c * P + P], in1=src,
                                                      op0=ALU.mult, op1=ALU.add)
                last.then_inc(S("turned_out" if c == CH - 1 else "s_step"), 1)
            dve.wait_ge(S("S0_in"), count("S0_in", G("S0_in", 16)))
            Tb = U[:, TP:T].rearrange("p (b t) -> p b t", t=LS)[:, :, LS - 1:LS].broadcast_to([P, NBAT, P])
            nc.vector.tensor_tensor(Sn[:, :, :], S0[:, :, :], Tb, ALU.mult).then_inc(S("s_new"), 1)
            dve.wait_ge(S("s_new"), count("s_new", G("s_new", 1)))
            dve.wait_ge(S("turned"), count("turned", G("turned", k + 1)))
            nc.vector.tensor_tensor(Sn[:, :, :].rearrange("p (a b) k -> p a (b k)", a=2),
                                    Sn[:, :, :].rearrange("p (a b) k -> p a (b k)", a=2), ps[:, 6:8, :], ALU.add)\
                .then_inc(S("turned_out"), 1)
            if following == "hgrn":
                keys_ready(i, 1)
            if following:
                split(n + (2 * ns + 3))
                if following == "hgrn":
                    scaled(qz[:, :], u + 2 * ns + 1)
                    queries_ready(i, 1)
                else:
                    dve.wait_ge(S("unit"), count("unit", u + (2 * ns + 2)))
                    nc.vector.scalar_tensor_tensor(out=two(gq[:, :]), in0=pair_of(u + (2 * ns + 1)), scalar=0.125,
                                                   in1=two(rinv[:, :]), op0=ALU.mult, op1=ALU.mult)\
                        .then_inc(S(f"taken{(u + (2 * ns + 1)).mod(2)}"), 1)

        def decay_min(p):
            dve.wait_ge(S("gk_ln"), count("gk_ln", 3 * p + 3))
            nc.vector.scalar_tensor_tensor(out=gkz[p], in0=gkz[p], scalar=0.0, in1=s1[:, :],
                                           op0=ALU.min, op1=ALU.subtract).then_inc(S("gk_min"), 1)

        def keys_ready(i, ahead):
            h = i + ahead
            dve.wait_ge(S("sig"), count("sig", group_count("sig", 1, i, None, 4 * ahead + 2)))
            nc.vector.tensor_scalar(gU[:, :], s1[:, :], one_lb_at(h), lb_at(h), ALU.mult, ALU.add)
            nc.vector.tensor_scalar(gk[:, :], s2[:, :], one_lb_at(h), None, ALU.mult).then_inc(S("k_ready"), 1)

        def queries_ready(i, ahead):
            dve.wait_ge(S("sig"), count("sig", group_count("sig", 1, i, None, 4 * ahead + 3)))
            nc.vector.tensor_tensor(gq[:, :], gq[:, :], qz[:, :], ALU.mult).then_inc(S("q_ready"), 1)

        def root_inverse(ns, i, pair, s, quarter):
            r = quarter * ns // 4
            q = s - ns + 1 + r
            w = ns * T // 4
            o = quarter * w - r * T
            dve.wait_ge(S("orms"), count("orms", group_count("orms", ns, i, pair, q + 1)))
            nc.vector.reciprocal(hsq[r][:, o:o + w], hsq[r][:, o:o + w]).then_inc(S("orr"), 1)

        def heads_output(ns, i, pair, s, heads=None):
            G = lambda name, k: group_count(name, ns, i, pair, k)
            for r in heads or range(ns):
                q = s - ns + 1 + r
                dve.wait_ge(S("orr"), count("orr", G("orr", 4 * (q + 1) // ns)))
                nc.vector.scalar_tensor_tensor(out=hout[r], in0=hout[r], scalar=gnormA if ns == 1 else gnormB,
                                               in1=hsq[r], op0=ALU.mult, op1=ALU.mult).then_inc(S("ot"), 1)
                dve.wait_ge(S("ot"), count("ot", G("ot", q + 1)))
                nc.vector.tensor_tensor(hout[r], hout[r], gate[:, r, :], ALU.mult).then_inc(S("omix"), 1)

        def one_lb_at(i):
            return bounds[:, 1, i, :]

        def lb_at(i):
            return bounds[:, 0, i, :]

        def queries_keys(n, u, R, norm_steps=None):
            tail = norm_steps or [lambda: None] * 3

            def rotate(dst, second, first, k):
                dve.wait_ge(S(f"taken{(u + k).mod(2)}"), count(f"taken{(u + k).mod(2)}", (u + k).div(2) + 1))
                nc.vector.tensor_tensor(dst[:, 0, :], rz[:, 0, :], cosT[:, :], ALU.mult)
                nc.vector.tensor_tensor(rtd[:, :], rz[:, 1, :], sinT[:, :], ALU.mult).then_inc(S("rot_a"), 1)
                dve.wait_ge(S("rot_a"), count("rot_a", R(first, 2)))
                nc.vector.tensor_tensor(dst[:, 0, :], dst[:, 0, :], rtd[:, :], ALU.subtract).then_inc(S(second), 1)

            tail[0]()
            scaled(rz[:, 0, :], u)
            split(n + 2)
            tail[1]()
            scaled(rz[:, 1, :], u + 1)
            split(n + 3)
            tail[2]()
            rotate(rq, "rot_q0", 1, 1)
            split(n + 4)
            dve.wait_ge(S("rot_q0"), count("rot_q0", R(1, 1)))
            dve.wait_ge(S("rot_q1"), count("rot_q1", R(1, 1)))
            scaled(rz[:, 0, :], u + 2)
            split(n + 5)
            scaled(rz[:, 1, :], u + 3)
            rotate(rk, "rot_k0", 2, 3)

        def retention_head(n, u, i, before_last=False, last_head=False):
            R = lambda k, per: Lin(k, per, i)

            def picked(j):
                dve.wait_ge(S("rscores"), count("rscores", R(j + 1, 5)))
                if j == 0:
                    dve.wait_ge(S("ctab_in"), count("ctab_in", R(16, 16)))
                if j < 4:
                    nc.vector.tensor_tensor(ratt[:, RAT[j]:RAT[j] + TP - P * j], ps[:, 4 + j % 2, 0:TP - P * j],
                                            Dm[:, 0:TP - P * j], ALU.mult).then_inc(S("ratt"), 1)
                else:
                    nc.vector.tensor_tensor(ratts[0:TS, :], ps[0:TS, 6, 0:TS], Ds, ALU.mult).then_inc(S("ratt"), 1)

            def sequence(b):
                for kk in range(2):
                    bank = 5 if b >= 4 and kk == 0 else 7
                    dve.wait_ge(S("rkv"), count("rkv", R(2 * b + kk + 1, 16)))
                    nc.vector.scalar_tensor_tensor(out=rS0[:, b % 4, kk, :], in0=rS0[:, b % 4, kk, :], scalar=gam,
                                                   in1=ps[:, bank, :], op0=ALU.mult, op1=ALU.add)\
                        .then_inc(S("rnew"), 1)

            for k in range(4):
                picked(k)
                if k >= 2:
                    dve.wait_ge(S("rturned"), count("rturned", R(k + 1, 6)))
                scaled(rv[:, k % 2, :], u + k)
                split(n + (k + 2))
            for gb in range(4):
                for b in ((), (0, 1), (2, 3), (4, 5, 6, 7))[gb]:
                    sequence(b)
                if gb == 0:
                    picked(4)
                if gb >= 2:
                    dve.wait_ge(S("rgate"), count("rgate", R(gb - 1, 4)))
                else:
                    dve.wait_ge(S("rturned"), count("rturned", R(5 + gb, 6)))
                scaled(rv[:, gb % 2, :], u + (4 + gb))
                split(n + (6 + gb))

            def summed():
                dve.wait_ge(S("ro_out"), count("ro_out", R(5, 5)))
                nc.vector.tensor_tensor(rsum, ro[:, 0, :], ro[:, 1, :], ALU.add).then_inc(S("rsummed"), 1)
                for vb in (2, 3):
                    dve.wait_ge(S("rsummed"), count("rsummed", R(vb - 1, 3)))
                    nc.vector.tensor_tensor(rsum, rsum, ro[:, vb, :], ALU.add).then_inc(S("rsummed"), 1)

            def centred():
                dve.wait_ge(S("rmean"), count("rmean", R(1, 1)))
                for vb in range(4):
                    nc.vector.scalar_tensor_tensor(out=two(ro[:, vb, :]), in0=ps[:, 4:6, 0:TH], scalar=-1.0 / 512,
                                                   in1=two(ro[:, vb, :]), op0=ALU.mult, op1=ALU.add)\
                        .then_inc(S("rcent"), 1)

            def gated():
                dve.wait_ge(S("rgate"), count("rgate", R(4, 4)))
                for vb in range(4):
                    dve.wait_ge(S("rsq"), count("rsq", R(vb + 1, 4)))
                    nc.vector.scalar_tensor_tensor(out=ro[:, vb, :], in0=ro[:, vb, :], scalar=gnormR[:, vb:vb + 1],
                                                   in1=rg[:, vb, :], op0=ALU.mult, op1=ALU.mult)\
                        .then_inc(S("rnorm"), 1)

            def normed():
                dve.wait_ge(S("rrms"), count("rrms", R(1, 1)))
                nc.vector.reciprocal(rr, rr).then_inc(S("rrr"), 1)
                dve.wait_ge(S("rrr"), count("rrr", R(1, 1)))
                for vb in range(4):
                    dve.wait_ge(S("rnorm"), count("rnorm", R(vb + 1, 4)))
                    nc.vector.tensor_tensor(ro[:, vb, :], ro[:, vb, :], rr, ALU.mult).then_inc(S("rmix"), 1)

            if last_head:
                def projected(m):
                    add_to_x(m, u + (8 + m), 1.0)

                summed()
                projected(0)
                centred()
                projected(1)
                gated()
                split(n + 10)
                projected(2)
                projected(3)
                split(n + 11)
                normed()
                for m in range(4, NB):
                    projected(m)
                    if m % 2 == 1:
                        split(n + (10 + m // 2))
                return
            queries_keys(n + 8, u + 8, lambda k, per: R(k + per, per), 
                         [summed, lambda: (centred(), gated()), normed])
            if before_last:
                return
            for m in range(NB):
                if m % 2 == 1:
                    split(n + (14 + m // 2))
                add_to_x(m, u + (12 + m), 1.0)

        dve.wait_ge(S("small_in"), count("small_in", 32))
        nc.vector.memset(eps, EPS).then_inc(S("eps"), 1)
        nc.vector.tensor_tensor(lbmax, logits[:, 0:4], logits[:, 4:8], ALU.max).then_inc(S("lb"), 1)
        dve.wait_ge(S("lb"), count("lb", 1))
        nc.vector.tensor_tensor(lbe[:, 0:4], logits[:, 0:4], lbmax, ALU.subtract)
        nc.vector.tensor_tensor(lbe[:, 4:8], logits[:, 4:8], lbmax, ALU.subtract).then_inc(S("lb_shift"), 1)
        dve.wait_ge(S("lb_exp"), count("lb_exp", 1))
        nc.vector.tensor_tensor(lbs, lbe[:, 0:4], lbe[:, 4:8], ALU.add).then_inc(S("lb"), 1)
        dve.wait_ge(S("lb"), count("lb", 2))
        nc.vector.reciprocal(lbs, lbs).then_inc(S("lb"), 1)
        dve.wait_ge(S("lb"), count("lb", 3))
        nc.vector.tensor_tensor(lb, lbe[:, 0:4], lbs, ALU.mult).then_inc(S("lb"), 1)
        dve.wait_ge(S("lb"), count("lb", 4))
        nc.vector.tensor_scalar(one_lb, lb, -1.0, 1.0, ALU.mult, ALU.add).then_inc(S("lb"), 1)
        dve.wait_ge(S("lb"), count("lb", 5))
        split(Lin(0))
        split(Lin(1))
        for m in range(NB):
            dve.wait_ge(S(f"x_in{m}"), count(f"x_in{m}", 16))
            norm_low(0, m)
            dve.wait_ge(S("sq"), count("sq", m + 1))
            if m == 1:
                nc.vector.tensor_tensor(sqsum[:, :], sq[:, 0, :], sq[:, 1, :], ALU.add).then_inc(S("sqsum"), 1)
            elif m:
                dve.wait_ge(S("sqsum"), count("sqsum", m - 1))
                nc.vector.tensor_tensor(sqsum[:, :], sqsum[:, :], sq[:, m % 2, :], ALU.add)\
                    .then_inc(S("sqsum"), 1)
        for ph_ in phases:
            n, u, norm = Lin(ph_["n"]), Lin(ph_["u"]), ph_["norm"]
            norm_inverse(norm)
            if ph_["kind"] == "ffn":
                j0 = ph_["j"]
                for part, J in enumerate(FF_PARTS):
                    with dve.Fori(0, J // 2) as i:
                        for k in range(2):
                            nn, uu = Lin(n.c + 2 * k, 4, i), Lin(u.c + 2 * k, 4, i)
                            j = Lin(j0 + k, 2, i)
                            dve.wait_ge(S("silu"), count("silu", j))
                            scaled(fa[:, k, :], uu)
                            split(nn + 2)
                            scaled(fb[:, k, :], uu + 1)
                            dve.wait_ge(S("silu"), count("silu", j + 1))
                            dve.wait_ge(S(f"taken{(uu + 1).mod(2)}"), count(f"taken{(uu + 1).mod(2)}", (uu + 1).div(2) + 1))
                            dve.wait_ge(S("hid_low"), count("hid_low", j))
                            nc.vector.tensor_tensor(ff[:, k, :], fs[:, k, :], fb[:, k, :], ALU.mult)\
                                .then_inc(S("gated"), 1)
                            split(nn + 3)
                    n, u, j0 = n + 2 * J, u + 2 * J, j0 + J
                    for m in range(NB):
                        add_to_x(m, u + m, 0.5)
                        split(n + (m + 2))
                        if part == 2 and m:
                            norm_low(norm + 1, m - 1)
                    n, u = n + NB, u + NB
                norm_low(norm + 1, NB - 1)
            elif ph_["kind"] == "ab":
                dve.wait_ge(S("masks_in"), count("masks_in", 16))
                dve.wait_ge(S("ident_in"), count("ident_in", 16))
                split(n + 2)
                dve.wait_ge(S("unit"), count("unit", u + 1))
                nc.vector.tensor_tensor(two(lr[0:16, :]), ps[0:16, 2 * u.mod(2):2 * u.mod(2) + 2, 0:TH],
                                        two(rinv[0:16, :]), ALU.mult).then_inc(S(f"taken{u.mod(2)}"), 1)
                split(n + 3)
                scaled(kz[:, :], u + 1)
                dve.wait_ge(S("gkz"), count("gkz", 1))
                for p in range(2):
                    nc.vector.tensor_scalar(two(gkz[p]), ps[:, 4 + 2 * p:6 + 2 * p, 0:TH], bgk[:, p:p + 1], None,
                                            ALU.add).then_inc(S("gkz_out"), 1)
                keys_ready(0, 0)
                split(n + 4)
                scaled(qz[:, :], u + 2)
                queries_ready(0, 0)
                n, u = n + 3, u + 3
                gated_group(1, n, u, 0, None, None, "hgrn")
                with dve.Fori(1, H - 1) as i:
                    gated_group(1, Lin(n.c, 4, i, 1), Lin(u.c, 4, i, 1), i, None,
                                (1, i, None, -1), "hgrn")
                gated_group(1, n + 4 * (H - 1), u + 4 * (H - 1), H - 1, None,
                            (1, H - 2, None, 0), "gla")
                n, u = n + 4 * H, u + 4 * H
                gated_group(2, n, u, None, 0, (1, H - 1, None, 0), "gla")
                n, u = n + N_GLA, u + N_GLA
                gated_group(2, n, u, None, 1, (2, None, 0, 1), None)
                for r in range(2):
                    root_inverse(2, None, 1, 1, 2 * r)
                    root_inverse(2, None, 1, 1, 2 * r + 1)
                    heads_output(2, None, 1, 1, heads=[r])
                n, u = n + 4, u + 4
                for m in range(NB):
                    add_to_x(m, u + m, 1.0)
                    split(n + (m + 2))
                    if m:
                        norm_low(norm + 1, m - 1)
                norm_low(norm + 1, NB - 1)
            elif ph_["kind"] == "ret":
                dve.wait_ge(S("rope_in"), count("rope_in", 32))
                queries_keys(n, u, lambda k, per: Lin(k))
                with dve.Fori(0, H - 2) as i:
                    retention_head(Lin(n.c + 4, N_RET, i), Lin(u.c + 4, 12 + NB, i), i)
                retention_head(n + (4 + (H - 2) * N_RET), u + (4 + (H - 2) * (12 + NB)), H - 2, before_last=True)
                n, u = n + (H - 1) * N_RET, u + (4 + (H - 1) * (12 + NB) - NB)
                retention_head(n, u, H - 1, last_head=True)
                for m in range(NB):
                    if m % 2 == 1:
                        split(n + (14 + m // 2))
                    add_to_x(m, u + (8 + NB + m), 1.0)
                    if m:
                        norm_low(norm + 1, m - 1)
                norm_low(norm + 1, NB - 1)
            else:
                lay = ph_["layer"]
                for k in range(2):
                    dve.wait_ge(S("p_high"), count("p_high", 2 * lay + k + 1))
                    nc.vector.tensor_tensor(pl[:, k, :], praw[:, k, :], ph[:, k, :], ALU.subtract)\
                        .then_inc(S("p_low"), 1)
                for m in range(NB):
                    if m >= 2:
                        dve.wait_ge(S("pgate"), count("pgate", NB * lay + m - 1))
                    scaled(pz[:, m % 2, :], u + m)
                    split(n + (m + 2))
                n, u = n + NB, u + NB
                dve.wait_ge(S("pgate"), count("pgate", NB * (lay + 1)))
                for m in range(NB):
                    dve.wait_ge(S("unit"), count("unit", u + (m + 1)))
                    if m >= 2:
                        dve.wait_ge(S("p_added"), count("p_added", NB * lay + m - 1))
                    nc.vector.tensor_tensor(two(pt[:, m % 2, :]), pair_of(u + m), two(pg[:, m, :]), ALU.mult)\
                        .then_inc(S(f"taken{(u + m).mod(2)}"), 1)
                    dve.wait_ge(S(f"taken{(u + m).mod(2)}"), count(f"taken{(u + m).mod(2)}", (u + m).div(2) + 1))
                    nc.vector.tensor_tensor(x[:, m, :], x[:, m, :], pt[:, m % 2, :], ALU.add).then_inc(S("p_added"), 1)
                    if m % 4 == 3:
                        split(n + (m // 4 + 2))
                    if m:
                        norm_low(norm + 1, m - 1)
                norm_low(norm + 1, NB - 1)
        norm_inverse(8)
        for m in range(NB):
            dve.wait_ge(S("sq"), count("sq", NB * 8 + m + 1))
            nc.vector.scalar_tensor_tensor(out=x[:, m, :], in0=x[:, m, :], scalar=gains[:, 8, m:m + 1],
                                           in1=rinv[:, :], op0=ALU.mult, op1=ALU.mult).then_inc(S("y_ready"), 1)

    @block.gpsimd
    def _(pool):
        def norm_total(norm):
            for m in range(1, NB):
                pool.wait_ge(S("sq"), count("sq", NB * norm + m + 1))
                if m == 1:
                    if norm:
                        pool.wait_ge(S("norm_sum"), count("norm_sum", norm))
                    nc.gpsimd.tensor_tensor(sqsum[:, :], sq[:, 0, :], sq[:, 1, :], ALU.add).then_inc(S("sqsum"), 1)
                else:
                    pool.wait_ge(S("sqsum"), count("sqsum", 7 * norm + m - 1))
                    nc.gpsimd.tensor_tensor(sqsum[:, :], sqsum[:, :], sq[:, m % 2, :], ALU.add)\
                        .then_inc(S("sqsum"), 1)

        def gated_group(ns, u, i, pair, previous):
            G = lambda name, k: group_count(name, ns, i, pair, k)
            U = gU[:, :] if ns == 1 else decay[:, pair, :]
            reached = early(pool, count("turned_out", G("turned_out", 0)))
            pool.wait_ge(S("ones"), 1)
            pool.wait_ge(S("turned_out"), reached)
            pool.wait_ge(S("o_done"), count("o_done", G("o_done", 0)))
            if ns == 1:
                pool.dma_start(S0[:, :, :], d["s_hgrn"][i]).then_inc(S("S0_in"), 16)
            else:
                pool.dma_start(S0[:, :, :], d["s_gla"][pair]).then_inc(S("S0_in"), 16)
            reached = early(pool, count("kl", G("kl", 0)))
            pool.wait_ge(S("ones"), 1)
            pool.wait_ge(S("kl"), reached)
            nc.gpsimd.memset(gL[:, :], 1.0).then_inc(S("l_up"), 1)
            ready_k(pool, ns, u, i)
            if ns == 2:
                pool.wait_ge(S("decay"), count("decay", 2))
            for lev in range(1, NLEV + 1):
                h = 1 << (lev - 1)
                R = T if h <= 4 else TP
                pool.wait_ge(S("l_up"), count("l_up", G("l_up", lev)))
                if lev > 1:
                    if lev > 3:
                        pool.wait_ge(S("scores"), count("scores", G("scores", (lev - 1) * ns)))
                    elif lev == 2:
                        pool.wait_ge(S("turned_out"), count("turned_out", G("turned_out", 0)))
                    nc.gpsimd.tensor_tensor(kl[:, lev % 2, 0:R], gk[:, 0:R], gL[:, 0:R], ALU.mult).then_inc(S("kl"), 1)
                    pool.wait_ge(S("kl"), count("kl", G("kl", lev - 1)))
                    pool.wait_ge(S("u_up"), count("u_up", G("u_up", lev - 1)))
                lv = gL[:, 0:R].rearrange("p (b a h) -> p b a h", a=2, h=h)
                uv = U[:, 0:R].rearrange("p (b a h) -> p b a h", a=2, h=h)
                nc.gpsimd.tensor_tensor(lv[:, :, 0, :], lv[:, :, 0, :],
                                        uv[:, :, 1, h - 1:h].broadcast_to([P, R // (2 * h), h]), ALU.mult)\
                    .then_inc(S("l_up"), 1)
                if lev == 6 and previous:
                    heads_low(*previous)
                if lev == 4:
                    for s in range(ns):
                        pool.wait_ge(S("turned_out"), count("turned_out", G("turned_out", 2 * s + 2)))
                        nc.gpsimd.tensor_tensor(
                            vm[0:TS, s, :, :], vt[0:TS, s, CH, :].unsqueeze(1).broadcast_to([TS, NBAT, P]),
                            batch_of[0:TS, :].unsqueeze(2).broadcast_to([TS, NBAT, P]), ALU.mult)\
                            .then_inc(S("vm"), 1)
            pool.wait_ge(S("l_up"), count("l_up", G("l_up", 8)))
            pool.wait_ge(S("scores"), count("scores", G("scores", 7 * ns)))
            nc.gpsimd.tensor_tensor(kl[:, 0, :], gk[:, :], gL[:, :], ALU.mult).then_inc(S("kl"), 1)
            reached = early(pool, count("turned_out", G("turned_out", 2 * ns + 3)))
            pool.wait_ge(S("ones"), 1)
            pool.wait_ge(S("turned_out"), reached)
            dst = out["hgrn_p"][i] if ns == 1 else out["gla_p"][pair]
            pool.dma_start(dst, St[:, CH - 1, :]).then_inc(S("S_out"), 16)
            reached = early(pool, count("turned_out", G("turned_out", 2 * ns + 4)))
            pool.wait_ge(S("ones"), 1)
            pool.wait_ge(S("turned_out"), reached)
            dst = out["hgrn_s"][i] if ns == 1 else out["gla_s"][pair]
            pool.dma_start(dst, Sn[:, :, :]).then_inc(S("S_out"), 16)

        def heads_low(ns, i, pair, s):
            G = lambda name, k: group_count(name, ns, i, pair, k)
            for r in range(ns):
                q = s - ns + 1 + r
                pool.wait_ge(S("omixh"), count("omixh", G("omixh", q + 1)))
                if ns == 1:
                    hi, lo = hid[0][:, i + q, :], hid[1][:, i + q, :]
                else:
                    hi, lo = hid[0][:, 4 + 2 * pair + q, :], hid[1][:, 4 + 2 * pair + q, :]
                nc.gpsimd.tensor_tensor(lo, hout[r], hi, ALU.subtract).then_inc(S("omixl"), 1)
            pool.wait_ge(S("S_out"), count("S_out", G("S_out", 32 * (s + 1) // ns)))

        def load_tables(h):
            pool.dma_start(ctab[:, :], d["ctab"][h]).then_inc(S("ctab_in"), 16)

        def rotate(u, R, dst, k, a, done):
            for c in (k - 1, k):
                pool.wait_ge(S(f"taken{(u + c).mod(2)}"), count(f"taken{(u + c).mod(2)}", (u + c).div(2) + 1))
            nc.gpsimd.tensor_tensor(dst[:, 1, :], rz[:, 1, :], cosT[:, :], ALU.mult)
            nc.gpsimd.tensor_tensor(rtp[:, :], rz[:, 0, :], sinT[:, :], ALU.mult).then_inc(S("rot_b"), 1)
            pool.wait_ge(S("rot_b"), count("rot_b", R(a, 2)))
            nc.gpsimd.tensor_tensor(dst[:, 1, :], dst[:, 1, :], rtp[:, :], ALU.add).then_inc(S(done), 1)

        def retention_head(u, i, before_last=False, last_head=False):
            R = lambda k, per: Lin(k, per, i)
            pool.wait_ge(S("ctab_in"), count("ctab_in", R(16, 16)))
            pool.wait_ge(S("rot_q0"), count("rot_q0", R(1, 1)))
            pool.wait_ge(S("rot_q1"), count("rot_q1", R(1, 1)))
            nc.gpsimd.tensor_tensor(qd[:, :, :], rq[:, :, TP:T], qdec.unsqueeze(1).broadcast_to([P, 2, TS]), ALU.mult)\
                .then_inc(S("qd"), 1)
            pool.wait_ge(S("rturned_out"), count("rturned_out", R(2, 6)))
            pool.wait_ge(S("rot_k0"), count("rot_k0", R(1, 1)))
            pool.wait_ge(S("rot_k1"), count("rot_k1", R(1, 1)))
            nc.gpsimd.tensor_tensor(kdm[0:TS, :, :], kd[0:TS, CH, :].unsqueeze(1).broadcast_to([TS, NBAT, 2 * P]),
                                    batch_of[0:TS, :].unsqueeze(2).broadcast_to([TS, NBAT, 2 * P]), ALU.mult)\
                .then_inc(S("kdm"), 1)

            def reload(b):
                reached = early(pool, count(f"rS_out{b % 4}", Lin(16 * (b // 4 + 1), 32, i)))
                pool.wait_ge(S("ones"), 1)
                pool.wait_ge(S(f"rS_out{b % 4}"), reached)
                pool.dma_start(rS0[:, b % 4, :, :], d["s_ret"][(Lin(b + 4, NBAT, i)).value()])\
                    .then_inc(S(f"rS0_in{b % 4}"), 16)

            def store_prompt():
                reached = early(pool, count("rstate_out", R(2, 2)))
                pool.wait_ge(S("ones"), 1)
                pool.wait_ge(S("rstate_out"), reached)
                pool.dma_start(out["ret_p"][i], rSt[:, :, :]).then_inc(S("rSt_stored"), 16)

            for b in range(NBAT):
                reached = early(pool, count("rnew", R(2 * b + 2, 16)))
                pool.wait_ge(S("ones"), 1)
                pool.wait_ge(S("rnew"), reached)
                pool.dma_start(out["ret_s"][Lin(b, NBAT, i).value()], rS0[:, b % 4, :, :])\
                    .then_inc(S(f"rS_out{b % 4}"), 16)
                if b and (b <= 4 or not last_head):
                    reload(b - 1)
                if b == 3:
                    store_prompt()
            if not last_head:
                load_tables(i + 1)
                reload(NBAT - 1)
            for vb in range(1, 4):
                pool.wait_ge(S("rsq"), count("rsq", R(vb + 1, 4)))
                if vb == 1:
                    nc.gpsimd.tensor_tensor(rsum, sq[:, 0, :], sq[:, 1, :], ALU.add).then_inc(S("rsqsum"), 1)
                else:
                    pool.wait_ge(S("rsqsum"), count("rsqsum", R(vb - 1, 3)))
                    nc.gpsimd.tensor_tensor(rsum, rsum, sq[:, vb % 2, :], ALU.add).then_inc(S("rsqsum"), 1)
            if not last_head:
                rotate(u + 8, lambda k, per: R(k + per, per), rq, 1, 1, "rot_q1")
            for vb in range(4):
                pool.wait_ge(S("rmixh"), count("rmixh", R(vb + 1, 4)))
                nc.gpsimd.tensor_tensor(hid[1][:, vb, :], ro[:, vb, :], hid[0][:, vb, :], ALU.subtract)\
                    .then_inc(S("rmixl"), 1)
            if not last_head:
                rotate(u + 8, lambda k, per: R(k + per, per), rk, 3, 2, "rot_k1")
            pool.wait_ge(S("rSt_stored"), count("rSt_stored", R(16, 16)))

        nc.gpsimd.memset(ones[:, :], 1.0).then_inc(S("ones"), 1)
        for ph_ in phases:
            norm = ph_["norm"]
            if ph_["kind"] == "ffn":
                j0 = ph_["j"]
                for J in FF_PARTS:
                    with pool.Fori(0, J // 2) as i:
                        for k in range(2):
                            pool.wait_ge(S("hid_high"), count("hid_high", Lin(j0 + k + 1, 2, i)))
                            nc.gpsimd.tensor_tensor(hid[1][:, i * 2 + k, :], ff[:, k, :], hid[0][:, i * 2 + k, :], ALU.subtract)\
                                .then_inc(S("hid_low"), 1)
                    j0 += J
            elif ph_["kind"] == "ab":
                pool.wait_ge(S("hid_low"), count("hid_low", ph_["j"]))
                pool.wait_ge(S("norm_sum"), count("norm_sum", norm + 1))
                pool.dma_start(masks[:, :, :], d["masks"]).then_inc(S("masks_in"), 16)
                pool.dma_start(gk2, d["gk2"]).then_inc(S("gk2_in"), 16)
                pool.wait_ge(S("small_in"), count("small_in", 32))
                u0 = ph_["u"]
                gated_group(1, Lin(u0 + 3), 0, None, None)
                with pool.Fori(1, H) as i:
                    gated_group(1, Lin(u0 + 3, 4, i, 1), i, None, (1, i, None, -1))
                gated_group(2, Lin(u0 + 3 + 4 * H), None, 0, (1, H - 1, None, 0))
                gated_group(2, Lin(u0 + 3 + 4 * H + N_GLA), None, 1, (2, None, 0, 1))
                heads_low(2, None, 1, 1)
            elif ph_["kind"] == "ret":
                pool.wait_ge(S("hid_low"), count("hid_low", ph_["j"]))
                pool.dma_start(cosT[:, :], d["cosT"]).then_inc(S("rope_in"), 16)
                pool.dma_start(sinT[:, :], d["sinT"]).then_inc(S("rope_in"), 16)
                for b in range(4):
                    pool.dma_start(rS0[:, b, :, :], d["s_ret"][b]).then_inc(S(f"rS0_in{b}"), 16)
                pool.wait_ge(S("rope_in"), count("rope_in", 32))
                load_tables(0)
                u0 = Lin(ph_["u"])
                rotate(u0, lambda k, per: Lin(k), rq, 1, 1, "rot_q1")
                rotate(u0, lambda k, per: Lin(k), rk, 3, 2, "rot_k1")
                with pool.Fori(0, H - 2) as i:
                    retention_head(Lin(ph_["u"] + 4, 12 + NB, i), i)
                retention_head(u0 + (4 + (H - 2) * (12 + NB)), H - 2, before_last=True)
                retention_head(u0 + (4 + (H - 1) * (12 + NB) - NB), H - 1, last_head=True)
                for b in range(4):
                    pool.wait_ge(S(f"rS0_in{b}"), count(f"rS0_in{b}", 16 * 2 * H))
                    pool.wait_ge(S(f"rS_out{b}"), count(f"rS_out{b}", 32 * H))
            else:
                pool.wait_ge(S("hid_low"), count("hid_low", ph_["j"]))
                pool.dma_start(praw[:, :, :], d["pT"][ph_["layer"]]).then_inc(S("praw_in"), 16)
            norm_total(norm + 1)

    block_cm.__exit__(None, None, None)


def _tiles(w, k0, k1, c0):
    return w[k0 * P:k1 * P, c0:c0 + P].reshape(k1 - k0, P, P).transpose(1, 0, 2).reshape(P, -1)


def _weight_stream(a):
    w = np.zeros((N_PIECES, P, D), np.float32)
    n = 0

    def put(*parts):
        nonlocal n
        c = 0
        for t in parts:
            w[n, :, c:c + t.shape[1]] = t
            c += t.shape[1]
        n += 1

    def ffn(w_in, w_out):
        k = 0
        for J in FF_PARTS:
            for j in range(k, k + J):
                put(_tiles(w_in, 0, NB, j * P))
                put(_tiles(w_in, 0, NB, DFF + j * P))
            for m in range(NB):
                put(_tiles(w_out, k, k + J, m * P))
            k += J

    for layer in range(2):
        ffn(a["ffn1_w_in"][layer], a["ffn1_w_out"][layer])
        if layer == 0:
            w_in, w_out = a["ab_w_in"][0], a["ab_w_out"][0]
            put(_tiles(w_in, 0, NB, 3072))
            for h in range(H):
                for c in (512, 0, 1024, 1536):
                    put(_tiles(w_in, 0, NB, c + h * P))
            for p in range(2):
                for c in (2304 + p * P, 2048 + p * P, 2560 + 2 * p * P, 2688 + 2 * p * P,
                          3088 + 2 * p * P, 3216 + 2 * p * P):
                    put(_tiles(w_in, 0, NB, c))
            for m in range(NB):
                put(_tiles(w_out, 0, NB, m * P))
        else:
            w_in, w_out = a["ret_w_in"][0], a["ret_w_out"][0]
            def project(h, *parts):
                for base, per in parts:
                    for k in range(per):
                        put(_tiles(w_in, 0, NB, base + (h * per + k) * P))

            project(0, (0, 2), (1024, 2))
            for h in range(H):
                project(h, (2048, 4), (4096, 4))
                if h < H - 1:
                    project(h + 1, (0, 2), (1024, 2))
                for g, m in () if h == H - 2 else [(g, m) for g in range(H - 2 if h == H - 1 else h, h + 1)
                                                   for m in range(0, NB, 2)]:
                    put(_tiles(w_out, 4 * g, 4 * g + 4, m * P), _tiles(w_out, 4 * g, 4 * g + 4, (m + 1) * P))
        ffn(a["ffn2_w_in"][layer], a["ffn2_w_out"][layer])
        for m in range(NB):
            put(_tiles(a["ple_w_gate"][layer], 0, NB, m * P))
        for m in range(0, NB, 4):
            put(*(_tiles(a["ple_w_proj"][layer], 0, 2, (m + k) * P) for k in range(4)))
    assert n == N_PIECES
    return w


def _columns(v):
    return v.reshape(-1, P).T


def _feature_major(prompt, sample, width):
    both = np.concatenate([prompt.reshape(TP, width), sample.reshape(TS, width)], 0)
    return np.ascontiguousarray(both.T).reshape(width // P, P, T)


def _constants():
    s, t = np.arange(P)[:, None], np.arange(P)[None, :]
    masks = np.zeros((P, NLEV, P), np.int32)
    for lev in range(NLEV):
        h = 1 << lev
        masks[:, lev] = (s // (2 * h) == t // (2 * h)) & (s // h % 2 == 0) & (t // h % 2 == 1)
    half = P
    inv = np.float32(10000.0) ** (-np.arange(half, dtype=np.float32) / np.float32(half))
    pos = np.concatenate([np.arange(TP), PAST + np.tile(np.arange(LS), NBAT)]).astype(np.float32)
    ang = (inv[:, None] * pos[None, :]).astype(np.float32).astype(np.float64)
    ctab = np.zeros((H, P, CT), np.float32)
    for h in range(H):
        lg = np.log1p(-np.exp2(-5.0 - h))
        r = np.arange(TP)[None, :] - np.arange(P)[:, None]
        ctab[h, :, 0:TP] = np.where(r >= 0, np.exp(lg * np.maximum(r, 0)) / 16, 0)
        s, t = np.arange(TS)[:, None], np.arange(TS)[None, :]
        ctab[h, 0:TS, TP:TP + TS] = np.where((s // LS == t // LS) & (t >= s), np.exp(lg * (t - s)) / 16, 0)
        ctab[h, :, TP + TS:TP + 2 * TS] = np.exp(lg * (np.arange(TS) % LS + 1))[None, :]
        o = TP + 2 * TS
        for c in range(CH):
            ctab[h, :, o + c] = np.exp(lg * (TP - 1 - (c * P + np.arange(P)))) / 16
        ctab[h, 0:TS, o + CH] = np.exp(lg * (LS - 1 - np.arange(TS) % LS)) / 16
        ctab[h, :, o + CH + 1] = np.exp(lg * LS)
    return {"masks": masks, "cosT": np.cos(ang).astype(np.float32), "sinT": np.sin(ang).astype(np.float32),
            "ctab": ctab, "ident": np.eye(P, dtype=np.float32)}


def kernel(**inputs):
    from concourse import bacc
    from concourse.bass_utils import run_bass_kernel_spmd

    a = {k: np.asarray(v) for k, v in inputs.items()}
    gains = np.zeros((P, 9, NB), np.float32)
    for layer in range(2):
        for k, name in enumerate(NORMS):
            gains[:, 4 * layer + k] = _columns(a[name][layer])
    gains[:, 8] = _columns(a["norm_final"])
    small = np.zeros((P, 24), np.float32)
    small[:, 0:1] = _columns(a["ab_gn_hgrn"][0])
    small[:, 1:2] = _columns(a["ab_gn_gla"][0])
    small[:, 2:6] = _columns(a["ret_gn"][0])
    small[:, 6:8] = _columns(a["ab_b_gk"][0])
    small[:, 8:12] = _columns(a["hgrn_lb_logits"][0])
    small[:, 12:16] = _columns(a["hgrn_lb_logits"][1])
    small[0:TS, 16:24] = np.arange(TS)[:, None] // LS == np.arange(NBAT)[None, :]
    s_ret = a["state_ret"][0].transpose(1, 0, 2, 3).reshape(H * NBAT, 2, P, 4 * P).transpose(0, 2, 1, 3)
    s_gla = a["state_gla"][0].reshape(NBAT, 2, 2, 64, P).transpose(1, 2, 3, 0, 4).reshape(2, P, NBAT, P)
    arrays = {
        "w": _weight_stream(a),
        "xT": _feature_major(a["x_prompt"], a["x_sample"], D),
        "pT": np.stack([_feature_major(a["p_prompt"][k], a["p_sample"][k], 2 * P).transpose(1, 0, 2) for k in range(2)]),
        "s_hgrn": a["state_hgrn"][0].transpose(1, 2, 0, 3), "s_gla": s_gla, "s_ret": s_ret,
        "gains": gains, "small": small, "gk2": a["ab_w_gk2"][0], **_constants(),
    }
    arrays = {k: np.ascontiguousarray(v) for k, v in arrays.items()}
    nc = bacc.Bacc("TRN2", target_bir_lowering=False, num_devices=1)
    d = {k: nc.dram_tensor(f"in_{k}", v.shape, mybir.dt.from_np(v.dtype), kind="ExternalInput").ap()
         for k, v in arrays.items()}
    shapes = {"yT": (NB, P, T), "hgrn_p": (H, P, P), "gla_p": (2, P, P), "ret_p": (H, P, 2, 4 * P),
              "hgrn_s": (H, P, NBAT, P), "gla_s": (2, P, NBAT, P), "ret_s": (H * NBAT, P, 2, 4 * P)}
    out = {k: nc.dram_tensor(f"out_{k}", v, F32, kind="ExternalOutput").ap() for k, v in shapes.items()}
    build(nc, d, out)
    r = run_bass_kernel_spmd(nc, [{f"in_{k}": v for k, v in arrays.items()}], core_ids=[0]).results[0]
    r = {k: np.asarray(r[f"out_{k}"]) for k in shapes}
    y = r["yT"].reshape(D, T).T
    c = np.ascontiguousarray
    return (c(y[:TP]).reshape(1, TP, D), c(y[TP:]).reshape(NBAT, LS, D),
            r["hgrn_p"].reshape(1, 1, H, P, P), r["gla_p"].reshape(1, 1, H, 64, P),
            c(r["ret_p"].transpose(0, 2, 1, 3)).reshape(1, 1, H, 2 * P, 4 * P),
            c(r["hgrn_s"].transpose(2, 0, 1, 3)).reshape(1, NBAT, H, P, P),
            c(r["gla_s"].reshape(2, 2, 64, NBAT, P).transpose(3, 0, 1, 2, 4)).reshape(1, NBAT, H, 64, P),
            c(r["ret_s"].reshape(H, NBAT, P, 2, 4 * P).transpose(1, 0, 3, 2, 4)).reshape(1, NBAT, H, 2 * P, 4 * P))
```
